# Optimizing a Trainium2 kernel written in Bass

```python
import math
import jax, jax.numpy as jnp
from jax import lax
import numpy as np

D_MODEL = 1024
BATCH = 1
SEQ = 512
DEPTH = 1

CHUNK = 64
D_MIX = D_MODEL
S5_WIDTH = 512
S5_GROUP = 16
S5_GROUPS = S5_WIDTH // S5_GROUP
S5_STATE = 64
S5_DT_MIN = 1e-3
S5_DT_MAX = 1e-1
MLA_WIDTH = D_MIX - S5_WIDTH
MLA_HEADS = 8
MLA_NOPE = 64
MLA_ROPE = 32
MLA_V = MLA_WIDTH // MLA_HEADS
Q_LORA = 384
KV_LORA = 256
ROPE_THETA = 10000.0
Q_BLOCK = 128
D_IN = S5_WIDTH + Q_LORA + KV_LORA + MLA_ROPE
PEER_HEADS = 8
PEER_NKEYS = 128
PEER_EXPERTS = PEER_NKEYS * PEER_NKEYS
PEER_QDIM = 256
PEER_HALF = PEER_QDIM // 2
PEER_TOPK = 16
PEER_BLOCK = 128
DEEPNORM_ALPHA = (2.0 * DEPTH) ** 0.25
DEEPNORM_BETA = (8.0 * DEPTH) ** -0.25
NORM_EPS = 1e-6
MASK_VALUE = -1e30

kernel_name = "hybrid_s5_mla_peer_block"

def _layernorm(x, g, b):
    xf = x.astype(jnp.float32)
    mu = jnp.mean(xf, axis=-1, keepdims=True)
    var = jnp.mean(jnp.square(xf - mu), axis=-1, keepdims=True)
    y = (xf - mu) * lax.rsqrt(var + NORM_EPS) * g.astype(jnp.float32) + b.astype(jnp.float32)
    return y.astype(x.dtype)

def _rmsnorm(x, g):
    xf = x.astype(jnp.float32)
    y = xf * lax.rsqrt(jnp.mean(xf * xf, axis=-1, keepdims=True) + NORM_EPS) * g.astype(jnp.float32)
    return y.astype(x.dtype)

def _rope_angles(positions):
    inv_freq = ROPE_THETA ** (-jnp.arange(0, MLA_ROPE, 2, dtype=jnp.float32) / MLA_ROPE)
    ang = positions.astype(jnp.float32)[..., None] * inv_freq
    return jnp.cos(ang), jnp.sin(ang)

def _apply_rope(x, cos, sin):
    x1, x2 = jnp.split(x, 2, axis=-1)
    cos = cos.astype(x.dtype)
    sin = sin.astype(x.dtype)
    return jnp.concatenate([x1 * cos - x2 * sin, x2 * cos + x1 * sin], axis=-1)

def _complex_affine_combine(left, right):
    a1r, a1i, b1r, b1i = left
    a2r, a2i, b2r, b2i = right
    ar = a2r * a1r - a2i * a1i
    ai = a2r * a1i + a2i * a1r
    br = a2r * b1r - a2i * b1i + b2r
    bi = a2r * b1i + a2i * b1r + b2i
    return (ar, ai, br, bi)

def _s5_mixer(u, lam_re, lam_im, log_dt, b_re, b_im, c_re, c_im, d, w_glu, b_glu):
    bsz, L, _ = u.shape
    ug = u.reshape(bsz, L, S5_GROUPS, S5_GROUP)
    dt = jnp.exp(log_dt)[:, None]
    mag = jnp.exp(lam_re * dt)
    ab_re = mag * jnp.cos(lam_im * dt)
    ab_im = mag * jnp.sin(lam_im * dt)
    den = lam_re * lam_re + lam_im * lam_im
    nr = ab_re - 1.0
    coef_re = (nr * lam_re + ab_im * lam_im) / den
    coef_im = (ab_im * lam_re - nr * lam_im) / den
    bb_re = coef_re[..., None] * b_re - coef_im[..., None] * b_im
    bb_im = coef_re[..., None] * b_im + coef_im[..., None] * b_re
    bu_re = jnp.einsum('blgh,gph->blgp', ug, bb_re)
    bu_im = jnp.einsum('blgh,gph->blgp', ug, bb_im)
    a_re = jnp.broadcast_to(ab_re, (1, L) + ab_re.shape)
    a_im = jnp.broadcast_to(ab_im, (1, L) + ab_im.shape)
    _, _, s_re, s_im = lax.associative_scan(_complex_affine_combine, (a_re, a_im, bu_re, bu_im), axis=1)
    y = jnp.einsum('blgp,ghp->blgh', s_re, c_re) - jnp.einsum('blgp,ghp->blgh', s_im, c_im)
    y = y.reshape(bsz, L, S5_WIDTH) + d * u
    y = jax.nn.gelu(y)
    return y * jax.nn.sigmoid(y @ w_glu + b_glu)

def _mla_mixer(cq, ckv, kr, cos, sin, q_norm, w_uq, kv_norm, w_ukv):
    bsz, L, _ = cq.shape
    q = (_rmsnorm(cq, q_norm) @ w_uq).reshape(bsz, L, MLA_HEADS, MLA_NOPE + MLA_ROPE)
    q_nope = q[..., :MLA_NOPE]
    q_pe = _apply_rope(q[..., MLA_NOPE:], cos[:, :, None, :], sin[:, :, None, :])
    kv = (_rmsnorm(ckv, kv_norm) @ w_ukv).reshape(bsz, L, MLA_HEADS, MLA_NOPE + MLA_V)
    k_nope = kv[..., :MLA_NOPE]
    v = kv[..., MLA_NOPE:]
    k_pe = _apply_rope(kr, cos, sin)
    scale = (MLA_NOPE + MLA_ROPE) ** -0.5
    n_blk = L // Q_BLOCK
    k_chunk = jnp.arange(L) // CHUNK

    def q_block(args):
        qn, qp, blk = args
        s = jnp.einsum('bqhd,bkhd->bhqk', qn, k_nope) + jnp.einsum('bqhr,bkr->bhqk', qp, k_pe)
        s = s.astype(jnp.float32) * scale
        q_chunk = (blk * Q_BLOCK + jnp.arange(Q_BLOCK)) // CHUNK
        mask = k_chunk[None, :] <= q_chunk[:, None]
        s = jnp.where(mask[None, None], s, MASK_VALUE)
        p = jax.nn.softmax(s, axis=-1).astype(v.dtype)
        return jnp.einsum('bhqk,bkhd->bqhd', p, v)

    qn_b = q_nope.reshape(bsz, n_blk, Q_BLOCK, MLA_HEADS, MLA_NOPE).transpose(1, 0, 2, 3, 4)
    qp_b = q_pe.reshape(bsz, n_blk, Q_BLOCK, MLA_HEADS, MLA_ROPE).transpose(1, 0, 2, 3, 4)
    out = lax.map(q_block, (qn_b, qp_b, jnp.arange(n_blk)))
    return out.transpose(1, 0, 2, 3, 4).reshape(bsz, L, MLA_WIDTH)

def _peer(h, w_query, keys1, keys2, u_tab, v_tab):
    bsz, L, dm = h.shape
    hb = h.reshape((bsz * L) // PEER_BLOCK, PEER_BLOCK, dm)

    def token_block(ht):
        q = (ht @ w_query).reshape(PEER_BLOCK, PEER_HEADS, PEER_QDIM)
        s1 = jnp.einsum('thd,hkd->thk', q[..., :PEER_HALF], keys1)
        s2 = jnp.einsum('thd,hkd->thk', q[..., PEER_HALF:], keys2)
        v1, i1 = lax.top_k(s1, PEER_TOPK)
        v2, i2 = lax.top_k(s2, PEER_TOPK)
        cand = (v1[..., :, None] + v2[..., None, :]).reshape(PEER_BLOCK, PEER_HEADS, PEER_TOPK * PEER_TOPK)
        top_s, top_c = lax.top_k(cand, PEER_TOPK)
        e1 = jnp.take_along_axis(i1, top_c // PEER_TOPK, axis=-1)
        e2 = jnp.take_along_axis(i2, top_c % PEER_TOPK, axis=-1)
        expert = e1 * PEER_NKEYS + e2
        g = jax.nn.softmax(top_s.astype(jnp.float32), axis=-1).astype(ht.dtype)
        act = jax.nn.gelu(jnp.einsum('thkd,td->thk', u_tab[expert], ht))
        return jnp.einsum('thk,thkd->td', g * act, v_tab[expert])

    return lax.map(token_block, hb).reshape(bsz, L, dm)

def setup_inputs(seed: int = 0) -> dict:
    key = jax.random.key(seed)
    ks = jax.random.split(key, 40)
    nrm = jax.random.normal
    f32 = jnp.float32
    x = nrm(ks[0], (BATCH, SEQ, D_MODEL), f32)
    c = nrm(ks[1], (BATCH, D_MODEL), f32)
    offset = jax.random.randint(ks[2], (BATCH, 1), 0, 4096, dtype=jnp.int32)
    positions = (offset + jnp.arange(SEQ, dtype=jnp.int32)[None, :]).astype(jnp.int32)
    w_ada = nrm(ks[3], (DEPTH, D_MODEL, 6 * D_MODEL), f32) * (0.5 * D_MODEL ** -0.5)
    b_ada = 0.02 * nrm(ks[4], (DEPTH, 6 * D_MODEL), f32)
    w_in = nrm(ks[5], (DEPTH, D_MODEL, D_IN), f32) * D_MODEL ** -0.5
    s5_lambda_re = -0.5 + 0.01 * nrm(ks[6], (DEPTH, S5_GROUPS, S5_STATE), f32)
    s5_lambda_im = jnp.broadcast_to(math.pi * jnp.arange(S5_STATE, dtype=f32), (DEPTH, S5_GROUPS, S5_STATE)) + 0.0
    s5_log_dt = jax.random.uniform(ks[7], (DEPTH, S5_GROUPS), f32, math.log(S5_DT_MIN), math.log(S5_DT_MAX))
    s5_b_re = nrm(ks[8], (DEPTH, S5_GROUPS, S5_STATE, S5_GROUP), f32) * (2.0 * S5_GROUP) ** -0.5
    s5_b_im = nrm(ks[9], (DEPTH, S5_GROUPS, S5_STATE, S5_GROUP), f32) * (2.0 * S5_GROUP) ** -0.5
    s5_c_re = nrm(ks[10], (DEPTH, S5_GROUPS, S5_GROUP, S5_STATE), f32) * (2.0 * S5_STATE) ** -0.5
    s5_c_im = nrm(ks[11], (DEPTH, S5_GROUPS, S5_GROUP, S5_STATE), f32) * (2.0 * S5_STATE) ** -0.5
    s5_d = nrm(ks[12], (DEPTH, S5_WIDTH), f32)
    s5_w_glu = nrm(ks[13], (DEPTH, S5_WIDTH, S5_WIDTH), f32) * S5_WIDTH ** -0.5
    s5_b_glu = 0.02 * nrm(ks[14], (DEPTH, S5_WIDTH), f32)
    mla_q_norm = 1.0 + 0.02 * nrm(ks[15], (DEPTH, Q_LORA), f32)
    mla_w_uq = nrm(ks[16], (DEPTH, Q_LORA, MLA_HEADS * (MLA_NOPE + MLA_ROPE)), f32) * Q_LORA ** -0.5
    mla_kv_norm = 1.0 + 0.02 * nrm(ks[17], (DEPTH, KV_LORA), f32)
    mla_w_ukv = nrm(ks[18], (DEPTH, KV_LORA, MLA_HEADS * (MLA_NOPE + MLA_V)), f32) * KV_LORA ** -0.5
    gn_s5 = 1.0 + 0.02 * nrm(ks[19], (DEPTH, S5_WIDTH), f32)
    gn_mla = 1.0 + 0.02 * nrm(ks[20], (DEPTH, MLA_WIDTH), f32)
    w_out = nrm(ks[21], (DEPTH, D_MIX, D_MODEL), f32) * (D_MIX ** -0.5 * DEEPNORM_BETA)
    ln1_g = 1.0 + 0.02 * nrm(ks[22], (DEPTH, D_MODEL), f32)
    ln1_b = 0.02 * nrm(ks[23], (DEPTH, D_MODEL), f32)
    peer_w_query = nrm(ks[24], (DEPTH, D_MODEL, PEER_HEADS * PEER_QDIM), f32) * D_MODEL ** -0.5
    peer_keys1 = nrm(ks[25], (DEPTH, PEER_HEADS, PEER_NKEYS, PEER_HALF), f32) * PEER_HALF ** -0.5
    peer_keys2 = nrm(ks[26], (DEPTH, PEER_HEADS, PEER_NKEYS, PEER_HALF), f32) * PEER_HALF ** -0.5
    peer_u = nrm(ks[27], (DEPTH, PEER_EXPERTS, D_MODEL), f32) * D_MODEL ** -0.5
    peer_v = nrm(ks[28], (DEPTH, PEER_EXPERTS, D_MODEL), f32) * DEEPNORM_BETA
    ln2_g = 1.0 + 0.02 * nrm(ks[29], (DEPTH, D_MODEL), f32)
    ln2_b = 0.02 * nrm(ks[30], (DEPTH, D_MODEL), f32)
    return {"x": x, "c": c, "positions": positions, "w_ada": w_ada, "b_ada": b_ada, "w_in": w_in,
            "s5_lambda_re": s5_lambda_re, "s5_lambda_im": s5_lambda_im, "s5_log_dt": s5_log_dt,
            "s5_b_re": s5_b_re, "s5_b_im": s5_b_im, "s5_c_re": s5_c_re, "s5_c_im": s5_c_im,
            "s5_d": s5_d, "s5_w_glu": s5_w_glu, "s5_b_glu": s5_b_glu,
            "mla_q_norm": mla_q_norm, "mla_w_uq": mla_w_uq, "mla_kv_norm": mla_kv_norm, "mla_w_ukv": mla_w_ukv,
            "gn_s5": gn_s5, "gn_mla": gn_mla, "w_out": w_out, "ln1_g": ln1_g, "ln1_b": ln1_b,
            "peer_w_query": peer_w_query, "peer_keys1": peer_keys1, "peer_keys2": peer_keys2,
            "peer_u": peer_u, "peer_v": peer_v, "ln2_g": ln2_g, "ln2_b": ln2_b}

def reference(x, c, positions, w_ada, b_ada, w_in,
              s5_lambda_re, s5_lambda_im, s5_log_dt, s5_b_re, s5_b_im, s5_c_re, s5_c_im,
              s5_d, s5_w_glu, s5_b_glu,
              mla_q_norm, mla_w_uq, mla_kv_norm, mla_w_ukv,
              gn_s5, gn_mla, w_out, ln1_g, ln1_b,
              peer_w_query, peer_keys1, peer_keys2, peer_u, peer_v, ln2_g, ln2_b):
    cos, sin = _rope_angles(positions)
    c_act = jax.nn.silu(c)
    splits = [S5_WIDTH, S5_WIDTH + Q_LORA, S5_WIDTH + Q_LORA + KV_LORA]
    for l in range(DEPTH):
        mod = c_act @ w_ada[l] + b_ada[l]
        sh1, sc1, g1, sh2, sc2, g2 = jnp.split(mod[:, None, :], 6, axis=-1)
        h = x * (1.0 + sc1) + sh1
        proj = h @ w_in[l]
        u, cq, ckv, kr = jnp.split(proj, splits, axis=-1)
        y_s5 = _s5_mixer(u, s5_lambda_re[l], s5_lambda_im[l], s5_log_dt[l], s5_b_re[l], s5_b_im[l],
                         s5_c_re[l], s5_c_im[l], s5_d[l], s5_w_glu[l], s5_b_glu[l])
        y_mla = _mla_mixer(cq, ckv, kr, cos, sin, mla_q_norm[l], mla_w_uq[l], mla_kv_norm[l], mla_w_ukv[l])
        y_mix = jnp.concatenate([_rmsnorm(y_s5, gn_s5[l]), _rmsnorm(y_mla, gn_mla[l])], axis=-1) @ w_out[l]
        x = _layernorm(DEEPNORM_ALPHA * x + (1.0 + g1) * y_mix, ln1_g[l], ln1_b[l])
        h = x * (1.0 + sc2) + sh2
        y_ff = _peer(h, peer_w_query[l], peer_keys1[l], peer_keys2[l], peer_u[l], peer_v[l])
        x = _layernorm(DEEPNORM_ALPHA * x + (1.0 + g2) * y_ff, ln2_g[l], ln2_b[l])
    return x


_drawn_inputs = setup_inputs


def setup_inputs(seed=0):
    import zlib

    import numpy as np

    out = dict(_drawn_inputs(seed))
    spreads = {}
    factors = {'s5_lambda_re': 8.0, 's5_b_glu': 3.728, 'mla_q_norm': 3.45, 'ln2_g': 2.955, 'ln2_b': 2.768}
    for name, (base, spread) in spreads.items():
        noise = np.random.default_rng([zlib.crc32(name.encode()), seed]).standard_normal(out[name].shape)
        drawn = base * np.exp(spread * noise) if base else spread * noise
        out[name] = __import__('jax').numpy.asarray(drawn.astype(out[name].dtype))
    for name, factor in factors.items():
        out[name] = (out[name] * factor).astype(out[name].dtype)
    return out
```

```python
import numpy as np
import concourse.bass as bass
from concourse import mybir

F32 = mybir.dt.float32
F32R = mybir.dt.float32r
U32 = mybir.dt.uint32
I32 = mybir.dt.int32
ACT = mybir.ActivationFunctionType
ALU = mybir.AluOpType
AXX = mybir.AxisListType.X

P = 128
KB = 1024
T = 512
TT = T // P
D = 1024
DK = D // P
S5W, GROUPS, GH, NS = 512, 32, 16, 64
SK = S5W // P
NQ = GROUPS // 2
CH = 8
NC = T // CH
QL, KVL, ROPE, NOPE, HEADS, VD = 384, 256, 32, 64, 8, 64
QK, KK = QL // P, KVL // P
D_IN = S5W + QL + KVL + ROPE
NMOD = 6 * D // P
PH, PKEYS, PTOP, PHALF = 8, 128, 16, 128
ALPHA = 2.0 ** 0.25
EPS = 1e-6
SCALE = float(NOPE + ROPE) ** -0.5
MASKED = -1e30
TWO_PI = 2.0 * np.pi
PI_1 = 6.28125
PI_2 = float(round((TWO_PI - PI_1) * 2**20)) / 2**20
PI_3 = float(np.float32(TWO_PI - PI_1 - PI_2))
ROUND = 1.5 * 2**23
SIN_MAX = 3.1415925

ROWS = [("c", 8), ("b_ada", 48), ("s5_d", 4), ("s5_b_glu", 4), ("gn_s5", 4), ("gn_mla", 4),
        ("mla_q_norm", 3), ("mla_kv_norm", 2), ("s5_lambda_re", 16), ("s5_lambda_im", 16)]
ROW_AT, _n = {}, 0
for _name, _m in ROWS:
    ROW_AT[_name] = _n
    _n += _m
NROWS = _n


class Plan:

    def __init__(self, nc):
        self.nc = nc
        self.u_scr = nc.dram_tensor("u_scr", (S5W, T), F32).ap()
        self.y_scr = nc.dram_tensor("y_scr", (S5W, T), F32).ap()
        self.x1_scr = nc.dram_tensor("x1_scr", (T, D), F32).ap()
        self.g_scr = nc.dram_tensor("g_scr", (PKEYS, PKEYS, T), F32).ap()
        self.dve_steps = Steps(self.sem("dve_stepped"))
        self.pool_steps = Steps(self.sem("pool_stepped"))
        self.base = (nc.sbuf_base + 63) // 64 * 64

    def sb(self, name, shape, at, dtype=F32):
        return self.nc.alloc_sbuf_tensor_at(name, shape, dtype, offset=self.base + int(round(at * KB)))

    def sem(self, name):
        return self.nc.alloc_semaphore(name)

    def sems(self, names):
        return [self.sem(n) for n in names.split()]


class Steps:

    def __init__(self, sem):
        self.eng, self.sem, self.n = None, sem, 0

    def on(self, eng):
        self.eng = eng
        return self

    def __call__(self, ins):
        self.n += 1
        ins.then_inc(self.sem, 1)
        self.eng.wait_ge(self.sem, self.n)

    def tell(self, ins, sem, n=1, by=1):
        ins.then_inc(sem, by)
        self.eng.wait_ge(sem, n)


def place(k):
    k.ident = k.sb("ident", [P, P], 0)
    k.ones = k.sb("ones", [P, P], 0.5)
    k.cols = k.sb("cols", [P, NROWS + NQ], 1)
    k.modc = k.sb("modc", [P, NMOD], 1.5)
    k.ccol = k.sb("ccol", [P, DK], 1.75)
    k.consts = k.sb("consts", [P, 2], 1.8125)
    k.eps = k.sb("eps", [P, 3], 1.84375)
    k.negrow = k.sb("negrow", [1, P], 2)
    k.onerow = k.sb("onerow", [1, NOPE], 2.5)
    k.rows = k.sb("rows", [NROWS, P], 3)
    k.ldt2 = k.sb("ldt2", [NQ, 2], 3.5)
    k.ldt_row = k.sb("ldt_row", [NQ, 2, NS], 3.625)
    k.mod_rows = k.sb("mod_rows", [16, P], 4)
    k.x_tok = k.sb("x_tok", [P, TT, D], 6)
    k.hT = k.sb("hT", [P, DK, T], 22)
    k.w_in = k.sb("w_in", [P, DK, D_IN], 38)
    k.w_ada = k.sb("w_ada", [P, 3, DK, 512], 75)
    k.uT = k.sb("uT", [P, SK, CH, NC], 123)
    k.cqT = k.sb("cqT", [P, QK, T], 131)
    k.ckvT = k.sb("ckvT", [P, KK, T], 137)
    k.krT = k.sb("krT", [P, 2, T], 141)
    k.rcos = k.sb("rcos", [P, T], 145)
    k.rsin = k.sb("rsin", [P, T], 147)
    k.w_kr = k.sb("w_kr", [P, DK, 2, 4, ROPE], 149)
    k.modrow = k.sb("modrow", [1, 2 * D], 131)
    k.mod_acc = k.sb("mod_acc", [P, 4 * D], 6)
    k.posi = k.sb("posi", [P, T], 123, I32)
    k.ang = k.sb("ang", [P, T], 125)
    k.rtmp = k.sb("rtmp", [P, T], 127)
    k.rtmp2 = k.sb("rtmp2", [P, T], 129)
    k.zr = k.sb("zr", [P, NQ, CH + 1, GH], 157)
    k.zn = k.sb("zn", [P, NQ, CH + 1, GH], 166)
    k.xr = k.sb("xr", [P, NQ, CH, GH], 175)
    k.xi = k.sb("xi", [P, NQ, CH, GH], 183)
    k.br = k.sb("br", [P, NQ, GH], 191)
    k.bi = k.sb("bi", [P, NQ, GH], 192)
    k.sv = k.sb("sv", [P, 24, NQ], 193)
    k.apr = k.sb("apr", [P, 9, NQ], 194.5)
    k.api = k.sb("api", [P, 9, NQ], 195.25)
    k.c_tok = k.sb("c_tok", [P, 2, SK, 2, NS], 196)
    k.dtmp = k.sb("dtmp", [P, 2, NQ, GH], 200)
    k.ptmp = k.sb("ptmp", [P, 2, NQ, GH], 202)


def bc(ap, shape):
    return ap.broadcast_to(shape)


def condition(nc, io, k, ps):
    k.s_rows, k.s_x, k.s_s5in, k.s_crep, k.s_ropein, k.s_win1 = k.sems("s_rows s_x s_s5in s_crep s_ropein s_win1")
    k.s_win2, k.s_win3, k.s_ident, k.s_tab, k.s_ldt, k.ldt_wide = k.sems("s_win2 s_win3 s_ident s_tab s_ldt ldt_wide")
    k.cols_copied, k.modrow_evac, k.s_modrows, k.mod_acc_ready, k.mod_tail = k.sems("cols_copied modrow_evac s_modrows mod_acc_ready mod_tail")
    wa = [k.sem(f"w_ada_in{i}") for i in range(3)]
    k.seq_out, k.seq_evac, k.rows_T, k.ccol_ready, k.cols_ready, k.mod_mm = k.sems("seq_out seq_evac rows_T ccol_ready cols_ready mod_mm")
    k.mod_head, k.ht_ready, k.w_kr_ready, k.dt_ready, k.lrd_ready, k.mag_ready = k.sems("mod_head ht_ready w_kr_ready dt_ready lrd_ready mag_ready")
    k.red_ready, k.sin_ready, k.rope_red, k.rope_sin, k.bb_ready = k.sems("red_ready sin_ready rope_red rope_sin bb_ready")

    def row_view(name, m):
        a = io[name]
        return bass.AP(a.tensor, a.offset, [[P, m], [1, P]])

    w_ada = io["w_ada"][0].rearrange("(kt p) n -> p kt n", p=P)

    @k.block.sync
    def _(sp):
        for name, m in ROWS:
            at = ROW_AT[name]
            sp.dma_start(k.rows[at:at + m, :], row_view(name, m)).then_inc(k.s_rows, 16)
        sp.dma_start(k.x_tok[:, :, :], io["x"][0].rearrange("(t p) d -> p t d", p=P)).then_inc(k.s_x, 16)
        for j in range(12):
            if j == 3:
                w_in = io["w_in"][0].rearrange("(kt p) n -> p kt n", p=P)
                for s, (a, b) in zip((k.s_win1, k.s_win2, k.s_win3), ((896, D_IN), (512, 896), (0, 512))):
                    sp.dma_start(k.w_in[:, :, a:b], w_in[:, :, a:b]).then_inc(s, 16)
            if j >= 3:
                sp.wait_ge(k.mod_mm, j - 2) if j < 7 else sp.wait_ge(k.mod_acc_ready, j - 6)
            sp.dma_start(k.w_ada[:, j % 3], w_ada[:, :, j * 512:(j + 1) * 512]).then_inc(wa[j % 3], 16)

    names = "dt lrd mag th kk rs rc sn cs den rden nr t1 t2 cr ci".split()
    sv = {n: k.sv[:, i, :] for i, n in enumerate(names)}
    sv["lre"] = k.cols[:, ROW_AT["s5_lambda_re"]:ROW_AT["s5_lambda_re"] + NQ]
    sv["lim"] = k.cols[:, ROW_AT["s5_lambda_im"]:ROW_AT["s5_lambda_im"] + NQ]

    dsts = ([k.krT[:, i, :] for i in range(2)] + [k.ckvT[:, i, :] for i in range(KK)] + [k.cqT[:, i, :] for i in range(QK)]
            + [k.uT[:, m] for m in range(SK)])

    @k.block.scalar
    def _(act):
        act.dma_start(k.ldt2[:, :], io["s5_log_dt"][0].rearrange("(q two) -> q two", two=2)).then_inc(k.s_ldt, 16)
        for g2 in range(2):
            half = slice(g2 * NS, (g2 + 1) * NS)
            for dst, name in ((k.br, "s5_b_re"), (k.bi, "s5_b_im")):
                act.dma_start(dst[half, :, :], io[name][0].rearrange("(q two) p h -> two p q h", two=2)[g2]).then_inc(k.s_s5in, 16)
        po = io["positions"]
        act.dma_start(k.posi[:, :], bass.AP(po.tensor, po.offset, [[0, P], [1, T]])).then_inc(k.s_ropein, 16)
        act.dma_start(k.consts[:, :], io["rope_rows"]).then_inc(k.s_ropein, 16)
        for part, name in enumerate(("s5_c_re", "s5_c_im")):
            src = io[name][0].rearrange("g h p -> (g h) p").rearrange("(m r) p -> r m p", r=P)
            for dup in range(2):
                act.dma_start(k.c_tok[:, part, :, dup, :], src).then_inc(k.s_crep, 16)
        act.wait_ge(k.cols_copied, 1)
        nc.scalar.activation(sv["dt"], k.cols[:, NROWS:NROWS + NQ], ACT.Exp).then_inc(k.dt_ready, 1)
        act.wait_ge(k.lrd_ready, 1)
        nc.scalar.activation(sv["mag"], sv["lrd"], ACT.Exp).then_inc(k.mag_ready, 1)
        act.wait_ge(k.red_ready, 1)
        nc.scalar.activation(sv["sn"], sv["rs"], ACT.Sin)
        nc.scalar.activation(sv["cs"], sv["rc"], ACT.Sin).then_inc(k.sin_ready, 1)
        act.wait_ge(k.rope_red, 1)
        nc.scalar.activation(k.rsin[:, :], k.ang[:, :], ACT.Sin)
        nc.scalar.activation(k.rcos[:, :], k.rtmp[:, :], ACT.Sin).then_inc(k.rope_sin, 1)
        nc.scalar.activation(k.ccol[:, :], k.cols[:, 0:DK], ACT.Silu).then_inc(k.ccol_ready, 1)
        for part, dst, sign in ((0, k.zr, 1.0), (1, k.zn, -1.0)):
            act.wait_ge(k.seq_out, part + 1)
            src = ps[:, 1 + part, :].rearrange("p (q two h) -> p q two h", two=2, h=GH)
            for g2 in range(2):
                half = slice(g2 * NS, (g2 + 1) * NS)
                ins = nc.scalar.activation(dst[half, :, 0, :], src[half, :, g2, :], ACT.Copy, scale=sign)
            ins.then_inc(k.seq_evac, 1)
        for kt in range(DK):
            n = 2 + kt
            act.wait_ge(k.seq_out, n + 1)
            nc.scalar.activation(k.hT[:, kt, :], ps[:, 1 + n % 7, :], ACT.Copy).then_inc(k.seq_evac, 1)
        for j in range(4):
            act.wait_ge(k.mod_mm, j + 1)
            nc.scalar.activation(k.modrow[:, j * 512:(j + 1) * 512], ps[0:1, 0, :], ACT.Copy).then_inc(k.modrow_evac, 1)
        act.wait_ge(k.modrow_evac, 4)
        act.dma_start(k.mod_rows[:, :], k.modrow[:, :].rearrange("a (m p) -> a m p", p=P)).then_inc(k.s_modrows, 16)
        for i, dst in enumerate(dsts):
            n = 10 + i
            act.wait_ge(k.seq_out, n + 1)
            src = ps[:, 1 + n % 7, :]
            if i >= 7:
                src = src.rearrange("p (c s) -> p s c", s=CH)
            elif i == 0:
                act.wait_ge(k.cols_ready, 1)
            nc.scalar.activation(dst, src, ACT.Copy).then_inc(k.seq_evac, 1)

    @k.block.gpsimd
    def _(pool):
        nc.gpsimd.memset(k.ident[:, :], 0.0).then_inc(k.s_ident, 1)
        nc.gpsimd.memset(k.negrow[:, :], 0.0).then_inc(k.s_ident, 1)
        nc.gpsimd.memset(k.ones[:, :], 1.0)
        nc.gpsimd.memset(k.onerow[:, :], 1.0)
        nc.gpsimd.memset(k.eps[:, 0:1], EPS)
        nc.gpsimd.memset(k.eps[:, 1:2], EPS / SCALE ** 2).then_inc(k.s_ident, 1)
        pool.wait_ge(k.s_ident, 3)
        nc.gpsimd.memset(k.negrow[:, 0:P // 2], MASKED)
        nc.gpsimd.affine_select(out=k.ident[:, :], in_=k.ident[:, :], compare_op=ALU.not_equal, fill=1.0, base=0,
                                pattern=[[-1, P]], channel_multiplier=1).then_inc(k.s_tab, 1)
        pool.wait_ge(k.s_win1, 16)
        src = k.w_in[:, :, D_IN - ROPE:D_IN]
        hr = ROPE // 2
        for r in range(4):
            nc.gpsimd.tensor_copy(k.w_kr[:, :, 0, r, :], src)
            nc.gpsimd.tensor_copy(k.w_kr[:, :, 1, r, 0:hr], src[:, :, hr:ROPE])
            ins = nc.gpsimd.tensor_copy(k.w_kr[:, :, 1, r, hr:ROPE], src[:, :, 0:hr])
        ins.then_inc(k.w_kr_ready, 1)
        step = k.pool_steps.on(pool)
        pool.wait_ge(k.bb_ready, 2)
        ar = k.apr[:, 0, :].unsqueeze(2).broadcast_to([P, NQ, GH])
        ai = k.api[:, 0, :].unsqueeze(2).broadcast_to([P, NQ, GH])
        for j in range(CH - 2, -1, -1):
            r0, i0, r1, i1 = k.xr[:, :, j + 1], k.xi[:, :, j + 1], k.xr[:, :, j], k.xi[:, :, j]
            nc.gpsimd.tensor_tensor(r1, r0, ar, ALU.mult)
            nc.gpsimd.tensor_tensor(k.ptmp[:, 0], i0, ai, ALU.mult)
            nc.gpsimd.tensor_tensor(i1, r0, ai, ALU.mult)
            step(nc.gpsimd.tensor_tensor(k.ptmp[:, 1], i0, ar, ALU.mult))
            nc.gpsimd.tensor_tensor(r1, r1, k.ptmp[:, 0], ALU.subtract)
            step(nc.gpsimd.tensor_tensor(i1, i1, k.ptmp[:, 1], ALU.add))

    @k.block.vector
    def _(dve):
        step = k.dve_steps.on(dve)
        v = nc.vector
        tt = v.tensor_tensor

        def reduce_angle(x, r_sin, r_cos, whole, done):
            step(v.tensor_scalar(whole, x, 1.0 / TWO_PI, ROUND, ALU.mult, ALU.add))
            step(v.tensor_scalar(whole, whole, -ROUND, None, ALU.add))
            for part in (PI_1, PI_2, PI_3):
                step(v.scalar_tensor_tensor(r_sin, whole, -part, x if part == PI_1 else r_sin, ALU.mult, ALU.add))
            step(v.tensor_scalar(whole, r_sin, np.pi / 2, -TWO_PI, ALU.is_gt, ALU.mult))
            step(v.scalar_tensor_tensor(r_cos, r_sin, np.pi / 2, whole, ALU.add, ALU.add))
            v.tensor_scalar(r_cos, r_cos, SIN_MAX, -SIN_MAX, ALU.min, ALU.max)
            step.tell(v.tensor_scalar(r_sin, r_sin, SIN_MAX, -SIN_MAX, ALU.min, ALU.max), done)

        dve.wait_ge(k.s_ldt, 16)
        v.tensor_copy(k.ldt_row[:, :, :], k.ldt2[:, :].unsqueeze(2).broadcast_to([NQ, 2, NS])).then_inc(k.ldt_wide, 1)
        dve.wait_ge(k.rows_T, 1)
        step.tell(v.tensor_copy(k.cols[:, :], ps[:, 0, 0:NROWS + NQ]), k.cols_copied)
        dve.wait_ge(k.dt_ready, 1)
        tt(sv["lrd"], sv["lre"], sv["dt"], ALU.mult).then_inc(k.lrd_ready, 1)
        step(tt(sv["th"], sv["lim"], sv["dt"], ALU.mult))
        reduce_angle(sv["th"], sv["rs"], sv["rc"], sv["kk"], k.red_ready)
        dve.wait_ge(k.s_s5in, 64)
        tt(sv["den"], sv["lre"], sv["lre"], ALU.mult)
        step(tt(sv["t1"], sv["lim"], sv["lim"], ALU.mult))
        step(tt(sv["den"], sv["den"], sv["t1"], ALU.add))
        step(v.reciprocal(sv["rden"], sv["den"]))
        dve.wait_ge(k.s_ropein, 32)
        step(v.tensor_copy(k.rtmp2[:, :], k.posi[:, :]))
        step(v.tensor_scalar(k.rtmp2[:, :], k.rtmp2[:, :], k.consts[:, 0:1], None, ALU.mult))
        reduce_angle(k.rtmp2[:, :], k.ang[:, :], k.rtmp[:, :], k.posi[:, :].bitcast(F32), k.rope_red)
        dve.wait_ge(k.sin_ready, 1)
        dve.wait_ge(k.mag_ready, 1)
        are, aim = k.apr[:, 0, :], k.api[:, 0, :]
        tt(are, sv["mag"], sv["cs"], ALU.mult)
        step(tt(aim, sv["mag"], sv["sn"], ALU.mult))
        step(v.tensor_scalar(sv["nr"], are, -1.0, None, ALU.add))
        for dst, x1, x2, y1, y2, op in (("cr", sv["nr"], sv["lre"], aim, sv["lim"], ALU.add),
                                        ("ci", aim, sv["lre"], sv["nr"], sv["lim"], ALU.subtract)):
            tt(sv["t1"], x1, x2, ALU.mult)
            step(tt(sv["t2"], y1, y2, ALU.mult))
            step(tt(sv["t1"], sv["t1"], sv["t2"], op))
            step(tt(sv[dst], sv["t1"], sv["rden"], ALU.mult))
        cr = sv["cr"].unsqueeze(2).broadcast_to([P, NQ, GH])
        ci = sv["ci"].unsqueeze(2).broadcast_to([P, NQ, GH])
        for dst, m1, m2, op in ((k.xr, cr, ci, ALU.subtract), (k.xi, ci, cr, ALU.add)):
            tt(k.dtmp[:, 0], k.br[:, :, :], m1, ALU.mult)
            step(tt(k.dtmp[:, 1], k.bi[:, :, :], m2, ALU.mult))
            step.tell(tt(dst[:, :, CH - 1, :], k.dtmp[:, 0], k.dtmp[:, 1], op), k.bb_ready, 1 + (dst is k.xi))
        dve.wait_ge(k.rope_sin, 1)
        v.tensor_scalar(k.rsin[:, :], k.rsin[:, :], k.consts[:, 1:2], None, ALU.mult).then_inc(k.cols_ready, 1)
        b_ada = k.cols[:, ROW_AT["b_ada"]:ROW_AT["b_ada"] + NMOD]

        def scales(a, b):
            for part in (1, 2, 4, 5):
                if a <= part * DK < b:
                    step(v.tensor_scalar(k.modc[:, part * DK:(part + 1) * DK], k.modc[:, part * DK:(part + 1) * DK],
                                         1.0, None, ALU.add))

        dve.wait_ge(k.mod_head, 1)
        step(tt(k.modc[:, 0:16], ps[:, 0, 0:16], b_ada[:, 0:16], ALU.add))
        scales(0, 16)
        for kt in range(DK):
            dve.wait_ge(k.seq_evac, 3 + kt)
            ins = v.tensor_scalar(k.hT[:, kt, :], k.hT[:, kt, :], k.modc[:, DK + kt:DK + kt + 1], k.modc[:, kt:kt + 1],
                                  ALU.mult, ALU.add)
        ins.then_inc(k.ht_ready, 1)
        for i in range(8):
            r, m, r2, m2 = k.apr[:, i], k.api[:, i], k.apr[:, i + 1], k.api[:, i + 1]
            tt(sv["t1"], r, r, ALU.mult)
            tt(sv["t2"], m, m, ALU.mult)
            step(tt(m2, r, m, ALU.mult))
            tt(r2, sv["t1"], sv["t2"], ALU.subtract)
            step(v.tensor_scalar(m2, m2, 2.0, None, ALU.mult))
        dve.wait_ge(k.seq_evac, 2)
        ar = are.unsqueeze(2).broadcast_to([P, NQ, GH])
        ai = aim.unsqueeze(2).broadcast_to([P, NQ, GH])
        for j in range(CH):
            r0, n0, r1, n1 = k.zr[:, :, j], k.zn[:, :, j], k.zr[:, :, j + 1], k.zn[:, :, j + 1]
            tt(r1, r0, ar, ALU.mult)
            tt(k.dtmp[:, 0], n0, ai, ALU.mult)
            tt(n1, n0, ar, ALU.mult)
            step(tt(k.dtmp[:, 1], r0, ai, ALU.mult))
            tt(r1, r1, k.dtmp[:, 0], ALU.add)
            step(tt(n1, n1, k.dtmp[:, 1], ALU.subtract))
        for j in range(4, 12):
            dve.wait_ge(wa[j % 3], 16 * (j // 3 + 1))
            acc = k.mod_acc[:, (j - 4) * 512:(j - 3) * 512]
            for kt in range(DK):
                w, c = k.w_ada[:, j % 3, kt, :], k.ccol[:, kt:kt + 1]
                ins = v.tensor_scalar(acc, w, c, None, ALU.mult) if kt == 0 else \
                    v.scalar_tensor_tensor(acc, w, c, acc, ALU.mult, ALU.add)
                if kt < DK - 1:
                    step(ins)
                else:
                    ins.then_inc(k.mod_acc_ready, 1)
        dve.wait_ge(k.mod_tail, 1)
        step(tt(k.modc[:, 16:NMOD], ps[:, 0, 16:NMOD], b_ada[:, 16:NMOD], ALU.add))
        scales(16, NMOD)

    @k.block.tensor
    def _(pe):
        mm = nc.tensor.matmul
        pe.wait_ge(k.s_tab, 1)
        pe.wait_ge(k.s_rows, 16 * len(ROWS))
        nc.tensor.transpose(ps[:, 0, 0:NROWS], k.rows[:, :], k.ident[0:NROWS, 0:NROWS])
        pe.wait_ge(k.ldt_wide, 1)
        nc.tensor.transpose(ps[:, 0, NROWS:NROWS + NQ], k.ldt_row[:, :, :].rearrange("q a b -> q (a b)"),
                            k.ident[0:NQ, 0:NQ]).then_inc(k.rows_T, 1)
        pe.wait_ge(k.s_crep, 64)
        for part in range(2):
            for m in range(SK):
                ins = nc.tensor.transpose(ps[:, 1 + part, m * P:(m + 1) * P],
                                          k.c_tok[:, part, m].rearrange("p a b -> p (a b)"), k.ident[:, :])
            ins.then_inc(k.seq_out, 1)
        pe.wait_ge(k.s_x, 16)
        for kt in range(DK):
            n = 2 + kt
            if n >= 7:
                pe.wait_ge(k.seq_evac, n - 6)
            for t in range(TT):
                ins = nc.tensor.transpose(ps[:, 1 + n % 7, t * P:(t + 1) * P], k.x_tok[:, t, kt * P:(kt + 1) * P],
                                          k.ident[:, :])
            ins.then_inc(k.seq_out, 1)
        pe.wait_ge(k.ccol_ready, 1)

        for j in range(4):
            pe.wait_ge(wa[j % 3], 16 * (j // 3 + 1))
            if j >= 1:
                pe.wait_ge(k.modrow_evac, j)
            for kt in range(DK):
                ins = mm(ps[0:1, 0, :], k.ccol[:, kt:kt + 1], k.w_ada[:, j % 3, kt, :],
                         start=(kt == 0), stop=(kt == DK - 1))
            ins.then_inc(k.mod_mm, 1)
        pe.wait_ge(k.s_modrows, 16)
        nc.tensor.transpose(ps[:, 0, 0:16], k.mod_rows[:, :], k.ident[0:16, 0:16]).then_inc(k.mod_head, 1)
        pe.wait_ge(k.ht_ready, 1)
        stat = ([k.w_kr[:, :, i].rearrange("p kt a b -> p kt (a b)") for i in range(2)]
                + [k.w_in[:, :, S5W + QL + i * P:S5W + QL + (i + 1) * P] for i in range(KK)]
                + [k.w_in[:, :, S5W + i * P:S5W + (i + 1) * P] for i in range(QK)]
                + [k.w_in[:, :, i * P:(i + 1) * P] for i in range(SK)])
        for i, w in enumerate(stat):
            n = 10 + i
            if i == 0:
                pe.wait_ge(k.w_kr_ready, 1)
            elif i == 4:
                pe.wait_ge(k.s_win2, 16)
            elif i == 7:
                pe.wait_ge(k.s_win3, 16)
            pe.wait_ge(k.seq_evac, n - 6)
            for kt in range(DK):
                ins = mm(ps[:, 1 + n % 7, :], w[:, kt, :], k.hT[:, kt, :], start=(kt == 0), stop=(kt == DK - 1))
            ins.then_inc(k.seq_out, 1)
        pe.wait_ge(k.mod_acc_ready, 8)
        for m in range(16, NMOD):
            ins = mm(ps[:, 0, m:m + 1], k.mod_acc[:, (m - 16) * P:(m - 15) * P], k.ones[:, 0:1], start=True, stop=True)
        ins.then_inc(k.mod_tail, 1)


def place_attention(k):
    k.xtr = k.sb("xtr", [P, NQ, P], 22)
    k.xti = k.sb("xti", [P, NQ, P], 30)
    k.kt32 = k.sb("kt32", [2 * GH, NQ, CH * GH], 38)
    k.kpe = k.sb("kpe", [P, 4, T], 46)
    k.m1 = k.sb("m1", [P, GROUPS, CH * GH], 54)
    k.ut = k.sb("ut", [P, GROUPS, NC], 70)
    k.w_qn = k.sb("w_qn", [P, QK, HEADS, NOPE], 78)
    k.w_qr = k.sb("w_qr", [P, QK, HEADS, ROPE], 84)
    k.w_sw = k.sb("w_sw", [P, QK, HEADS, ROPE], 87)
    k.w_kn = k.sb("w_kn", [P, KK, HEADS, NOPE], 90)
    k.w_v = k.sb("w_v", [P, KK, HEADS, VD], 94)
    k.ir = k.sb("ir", [P, NQ, NC + 1], 98)
    k.ii = k.sb("ii", [P, NQ, NC + 1], 102.125)
    k.sq = k.sb("sq", [P, QK + KK, T], 98)
    k.cqn = k.sb("cqn", [P, QK, T], 109)
    k.ckvn = k.sb("ckvn", [P, KK, T], 115)
    k.rq = k.sb("rq", [P, T], 119)
    k.rkv = k.sb("rkv", [P, T], 121)
    k.qn = k.sb("qn", [P, HEADS // 2, T], 149)
    k.qr = k.sb("qr", [P, HEADS // 4, T], 196)
    k.kn = k.sb("kn", [P, HEADS, T], 6)
    k.v = k.sb("v", [P, TT, HEADS, VD], 131)
    k.bpad = k.sb("bpad", [P, 2, NQ, 2, GH], 200)
    k.ropet = k.sb("ropet", [P, T], 204)
    k.sct = k.sb("sct", [P, 4, NQ, NC], 22)
    k.prob = k.sb("prob", [P, 3, T], 78)
    k.probT = k.sb("probT", [P, 2, TT, P], 84)
    k.y_mla = k.sb("y_mla", [P, TT, HEADS * VD], 107)
    k.nmax = k.sb("nmax", [P, TT * HEADS], 115)
    k.rsum = k.sb("rsum", [P, TT * HEADS], 115.125)
    k.rinv = k.sb("rinv", [P, TT * HEADS], 115.25)
    k.spad = k.sb("spad", [P, 2, NQ, 2, NC], 175)


def project(nc, io, k, ps):
    k.s_wuq, k.s_wukv, k.s_uout, k.s_m1, k.wsw_ready, k.sq_ready = k.sems("s_wuq s_wukv s_uout s_m1 wsw_ready sq_ready")
    k.a2_out, k.a2_evac, k.d2_out, k.d2_evac, k.cqn_ready, k.ckvn_ready = k.sems("a2_out a2_evac d2_out d2_evac cqn_ready ckvn_ready")
    k.bpad_zero, k.bpad_ready, k.m1_zero, k.kn_zero, k.kpe_ready, k.kpe_zero = k.sems("bpad_zero bpad_ready m1_zero kn_zero kpe_ready kpe_zero")
    s_ut = k.sem("s_ut")
    H2 = ROPE // 2
    mm = nc.tensor.matmul
    u_scr = k.u_scr

    @k.block.sync
    def _(sp):
        w_uq = io["mla_w_uq"][0].rearrange("(kt p) (h c) -> p kt h c", p=P, h=HEADS)
        w_ukv = io["mla_w_ukv"][0].rearrange("(kt p) (h c) -> p kt h c", p=P, h=HEADS)
        for kt in range(QK):
            sp.dma_start(k.w_qr[:, kt], w_uq[:, kt, :, NOPE:]).then_inc(k.s_wuq, 16)
            sp.dma_start(k.w_qn[:, kt], w_uq[:, kt, :, 0:NOPE]).then_inc(k.s_wuq, 16)
        for kt in range(KK):
            sp.dma_start(k.w_kn[:, kt], w_ukv[:, kt, :, 0:NOPE]).then_inc(k.s_wukv, 16)
            sp.dma_start(k.w_v[:, kt], w_ukv[:, kt, :, NOPE:]).then_inc(k.s_wukv, 16)
        sp.dma_start(u_scr.rearrange("(m p) t -> p m t", p=P),
                     k.uT[:, :, :, :].rearrange("p m s c -> p m (s c)")).then_inc(k.s_uout, 16)
        sp.wait_ge(k.s_uout, 16)
        for s in range(CH):
            sp.dma_start(k.ut[s * GH:(s + 1) * GH, :, :],
                         u_scr.rearrange("(g h) (s c) -> h g s c", h=GH, s=CH)[:, :, s, :]).then_inc(s_ut, 16)
        sp.wait_ge(k.d2_evac, 8)
        sp.wait_ge(k.m1_zero, 1)
        m1 = k.m1[:, :, :].rearrange("p (q two) n -> p q two n", two=2)
        for s in range(CH):
            for g2 in range(2):
                sp.dma_start(m1[s * GH:(s + 1) * GH, :, g2, s * GH:],
                             k.kt32[g2 * GH:(g2 + 1) * GH, :, 0:(CH - s) * GH]).then_inc(k.s_m1, 16)
        sp.wait_ge(k.s_m1, 16 * 2 * CH)

    @k.block.gpsimd
    def _(pool):
        nc.gpsimd.memset(k.bpad[:, :, :, :, :], 0.0).then_inc(k.bpad_zero, 1)
        for i in range(QK):
            ins = nc.gpsimd.tensor_tensor(k.sq[:, i], k.cqT[:, i], k.cqT[:, i], ALU.mult)
        ins.then_inc(k.sq_ready, 1)
        nc.gpsimd.memset(k.kn[:, :, :], 0.0).then_inc(k.kn_zero, 1)
        nc.gpsimd.memset(k.kpe[:, :, :], 0.0).then_inc(k.kpe_zero, 1)
        pool.wait_ge(k.s_wuq, 16 * 2 * QK)
        nc.gpsimd.tensor_copy(k.w_sw[:, :, :, 0:H2], k.w_qr[:, :, :, H2:])
        nc.gpsimd.tensor_copy(k.w_sw[:, :, :, H2:], k.w_qr[:, :, :, 0:H2]).then_inc(k.wsw_ready, 1)
        nc.gpsimd.memset(k.m1[:, :, :], 0.0).then_inc(k.m1_zero, 1)

    @k.block.scalar
    def _(act):
        for i in range(KK):
            ins = nc.scalar.activation(k.sq[:, QK + i], k.ckvT[:, i], ACT.Square)
        ins.then_inc(k.sq_ready, 1)
        act.wait_ge(k.bpad_zero, 1)
        for part, x in enumerate((k.xr, k.xi)):
            for g2 in range(2):
                half = slice(g2 * NS, (g2 + 1) * NS)
                ins = nc.scalar.activation(k.bpad[half, part, :, g2, :], x[half, :, CH - 1, :], ACT.Copy)
        ins.then_inc(k.bpad_ready, 1)
        act.wait_ge(k.a2_out, 1)
        nc.scalar.activation(k.rq[:, :], ps[:, 0], ACT.Sqrt, scale=1.0 / (QL * SCALE ** 2), bias=k.eps[:, 1:2]).then_inc(k.a2_evac, 1)
        act.wait_ge(k.a2_out, 2)
        nc.scalar.activation(k.rkv[:, :], ps[:, 1], ACT.Sqrt, scale=1.0 / KVL, bias=k.eps[:, 0:1]).then_inc(k.a2_evac, 1)
        n = 2

        def evac(pairs, n):
            act.wait_ge(k.a2_out, n + 1)
            for dst, src in pairs:
                ins = nc.scalar.activation(dst, src, ACT.Copy)
            ins.then_inc(k.a2_evac, 1)

        for dst in (k.xtr, k.xti):
            for b in range(4):
                evac([(dst[:, 4 * b:4 * b + 4].rearrange("p q n -> p (q n)"), ps[:, n % 4])], n)
                n += 1
        for i in range(4):
            evac([(k.qn[:, i], ps[:, n % 4])], n)
            n += 1
        act.wait_ge(k.kn_zero, 1)
        for i in range(4):
            evac([(k.kn[0:NOPE, 2 * i], ps[0:NOPE, n % 4]), (k.kn[NOPE:P, 2 * i + 1], ps[NOPE:P, n % 4])], n)
            n += 1
        for i in range(TT):
            evac([(k.v[:, i].rearrange("p h c -> p (h c)"), ps[:, n % 4])], n)
            n += 1

    @k.block.vector
    def _(dve):
        step = k.dve_steps.on(dve)
        v = nc.vector
        tt = v.tensor_tensor
        qcol = k.cols[:, ROW_AT["mla_q_norm"]:]
        kcol = k.cols[:, ROW_AT["mla_kv_norm"]:]
        tt(k.ropet[:, :], k.krT[:, 1], k.rsin[:, :], ALU.mult)
        step(tt(k.krT[:, 0], k.krT[:, 0], k.rcos[:, :], ALU.mult))
        dve.wait_ge(k.kpe_zero, 1)
        for r in range(4):
            rows = slice(r * ROPE, (r + 1) * ROPE)
            ins = tt(k.kpe[rows, r], k.krT[rows, 0], k.ropet[rows, :], ALU.add)
        ins.then_inc(k.kpe_ready, 1)
        dve.wait_ge(k.a2_evac, 2)
        v.reciprocal(k.rq[:, :], k.rq[:, :])
        step(v.reciprocal(k.rkv[:, :], k.rkv[:, :]))
        for i in range(QK):
            ins = v.scalar_tensor_tensor(k.cqn[:, i], k.cqT[:, i], qcol[:, i:i + 1], k.rq[:, :], ALU.mult, ALU.mult)
        ins.then_inc(k.cqn_ready, 1)
        for i in range(KK):
            ins = v.scalar_tensor_tensor(k.ckvn[:, i], k.ckvT[:, i], kcol[:, i:i + 1], k.rkv[:, :], ALU.mult, ALU.mult)
        ins.then_inc(k.ckvn_ready, 1)
        for i in range(2):
            dve.wait_ge(k.d2_out, 2 * i + 2)
            if i == 0:
                dve.wait_ge(k.kpe_ready, 1)
            tt(k.ropet[:, :], ps[:, 4 + 2 * i + 1], k.rsin[:, :], ALU.mult)
            step(tt(k.qr[:, i], ps[:, 4 + 2 * i], k.rcos[:, :], ALU.mult))
            step.tell(tt(k.qr[:, i], k.qr[:, i], k.ropet[:, :], ALU.add), k.d2_evac, 2 * i + 2, by=2)
        for b in range(4):
            dve.wait_ge(k.d2_out, 4 + b + 1)
            v.tensor_copy(k.kt32[:, 4 * b:4 * b + 4].rearrange("p q n -> p (q n)"), ps[0:2 * GH, 4 + b]).then_inc(k.d2_evac, 1)
        v.memset(k.ir[:, :, 0:1], 0.0)
        v.memset(k.ii[:, :, 0:1], 0.0)
        for j in range(8):
            part, b = j // 4, j % 4
            dve.wait_ge(k.d2_out, 8 + j + 1)
            src = ps[:, 4 + b].rearrange("p (q two c) -> p q two c", two=2, c=NC)
            for g2 in range(2):
                half = slice(g2 * NS, (g2 + 1) * NS)
                ins = v.tensor_copy((k.ir, k.ii)[part][half, 4 * b:4 * b + 4, 1:], src[half, :, g2, :])
            ins.then_inc(k.d2_evac, 1)

    @k.block.tensor
    def _(pe):
        pe.wait_ge(k.sq_ready, 2)
        for i in range(QK):
            ins = mm(ps[:, 0], k.ones[:, :], k.sq[:, i], start=(i == 0), stop=(i == QK - 1))
        ins.then_inc(k.a2_out, 1)
        for i in range(KK):
            ins = mm(ps[:, 1], k.ones[:, :], k.sq[:, QK + i], start=(i == 0), stop=(i == KK - 1))
        ins.then_inc(k.a2_out, 1)
        n = 2
        for src in (k.xr, k.xi):
            for b in range(4):
                if n >= 4:
                    pe.wait_ge(k.a2_evac, n - 3)
                for q in range(4):
                    ins = nc.tensor.transpose(ps[:, n % 4, q * P:(q + 1) * P],
                                              src[:, 4 * b + q].rearrange("p s h -> p (s h)"), k.ident[:, :])
                ins.then_inc(k.a2_out, 1)
                n += 1
        pe.wait_ge(k.cqn_ready, 1)
        pe.wait_ge(k.wsw_ready, 1)
        for i in range(2):
            for sw in range(2):
                for kt in range(QK):
                    w = (k.w_sw if sw else k.w_qr)[:, kt, 4 * i:4 * i + 4, :].rearrange("p h c -> p (h c)")
                    ins = mm(ps[:, 4 + 2 * i + sw], w, k.cqn[:, kt], start=(kt == 0), stop=(kt == QK - 1))
                ins.then_inc(k.d2_out, 1)
        for i in range(4):
            pe.wait_ge(k.a2_evac, n - 3)
            for kt in range(QK):
                ins = mm(ps[:, n % 4], k.w_qn[:, kt, 2 * i:2 * i + 2].rearrange("p h c -> p (h c)"), k.cqn[:, kt],
                         start=(kt == 0), stop=(kt == QK - 1))
            ins.then_inc(k.a2_out, 1)
            n += 1
        pe.wait_ge(k.bpad_ready, 1)
        for b in range(4):
            pe.wait_ge(k.d2_evac, 2 * (b // 2) + 2)
            for q in range(4 * b, 4 * b + 4):
                out = ps[0:2 * GH, 4 + b, (q % 4) * P:(q % 4 + 1) * P]
                for part, z in enumerate((k.zr, k.zn)):
                    ins = mm(out, k.bpad[:, part, q].rearrange("p a b -> p (a b)"),
                             z[:, q, 0:CH].rearrange("p s h -> p (s h)"), start=(part == 0), stop=(part == 1))
            ins.then_inc(k.d2_out, 1)
        pe.wait_ge(k.s_wukv, 16 * 2 * KK)
        pe.wait_ge(k.ckvn_ready, 1)
        for i in range(4):
            pe.wait_ge(k.a2_evac, n - 3)
            for kt in range(KK):
                ins = mm(ps[:, n % 4], k.w_kn[:, kt, 2 * i:2 * i + 2].rearrange("p h c -> p (h c)"), k.ckvn[:, kt],
                         start=(kt == 0), stop=(kt == KK - 1))
            ins.then_inc(k.a2_out, 1)
            n += 1
        for i in range(TT):
            pe.wait_ge(k.a2_evac, n - 3)
            for kt in range(KK):
                ins = mm(ps[:, n % 4], k.ckvn[:, kt, i * P:(i + 1) * P], k.w_v[:, kt].rearrange("p h c -> p (h c)"),
                         start=(kt == 0), stop=(kt == KK - 1))
            ins.then_inc(k.a2_out, 1)
            n += 1
        pe.wait_ge(s_ut, 16 * CH)
        for j in range(8):
            part, b = j // 4, j % 4
            pe.wait_ge(k.d2_evac, 4 + j + 1)
            for q in range(4 * b, 4 * b + 4):
                ins = mm(ps[:, 4 + b, (q % 4) * P:(q % 4 + 1) * P], (k.xtr, k.xti)[part][:, q],
                         k.ut[:, 2 * q:2 * q + 2].rearrange("p a b -> p (a b)"), start=True, stop=True)
            ins.then_inc(k.d2_out, 1)


def attend(nc, io, k, ps):
    k.sc_out, k.pt_out, k.pv_out, k.nmax_ready, k.exp_done, k.pt_evac = k.sems("sc_out pt_out pv_out nmax_ready exp_done pt_evac")
    k.o_evac, k.sc_prod_d, k.sc_prod_p, k.sc_upd_d, k.sc_upd_p, k.spad_zero = k.sems("o_evac sc_prod_d sc_prod_p sc_upd_d sc_upd_p spad_zero")
    k.rinv_done, k.m3_ready = k.sems("rinv_done m3_ready")
    mm = nc.tensor.matmul
    jobs = [(qb, h) for qb in range(TT) for h in range(HEADS)]
    SCAN_AT = {2 + 5 * s: s for s in range(6)}

    @k.block.tensor
    def _(pe):
        def scores(i):
            qb, h = jobs[i]
            n = (qb + 1) * P
            if i >= 3:
                pe.wait_ge(k.exp_done, i - 2)
            out = ps[:, i % 3, 0:n]
            mm(out, k.qn[:, h // 2, qb * P:n], k.kn[:, h, 0:n], start=True, stop=False)
            mm(out, k.qr[:, h // 4, qb * P:n], k.kpe[:, h % 4, 0:n], start=False, stop=False)
            mm(out[:, n - P // 2:n], k.negrow[0:1, :], k.onerow[0:1, :], start=False, stop=True).then_inc(k.sc_out, 1)

        def transposes(i):
            qb, h = jobs[i]
            pe.wait_ge(k.exp_done, i + 1)
            if i >= 2:
                pe.wait_ge(k.pt_evac, i - 1)
            for kb in range(qb + 1):
                ins = nc.tensor.transpose(ps[:, 3 + i % 2, kb * P:(kb + 1) * P], k.prob[:, i % 3, kb * P:(kb + 1) * P],
                                          k.ident[:, :])
            ins.then_inc(k.pt_out, 1)

        def values(i):
            qb, h = jobs[i]
            pe.wait_ge(k.pt_evac, i + 1)
            if h == 0 and qb >= 2:
                pe.wait_ge(k.o_evac, qb - 1)
            for kb in range(qb + 1):
                ins = mm(ps[:, 5 + qb % 2, h * VD:(h + 1) * VD], k.probT[:, i % 2, kb], k.v[:, kb, h, :],
                         start=(kb == 0), stop=(kb == qb))
            ins.then_inc(k.pv_out, 1)

        for i in range(len(jobs) + 2):
            if i < len(jobs):
                scores(i)
            if 1 <= i <= len(jobs):
                transposes(i - 1)
            if i >= 2:
                values(i - 2)

    @k.block.scalar
    def _(act):
        for i, (qb, h) in enumerate(jobs):
            n = (qb + 1) * P
            act.wait_ge(k.nmax_ready, i + 1)
            if i >= 3:
                act.wait_ge(k.pt_out, i - 2)
            nc.scalar.activation(k.prob[:, i % 3, 0:n], ps[:, i % 3, 0:n], ACT.Exp, bias=k.nmax[:, i:i + 1],
                                 accum_out=k.rsum[:, i:i + 1]).then_inc(k.exp_done, 1)
        act.wait_ge(k.sc_upd_d, 6)
        act.wait_ge(k.sc_upd_p, 12)
        act.wait_ge(k.spad_zero, 1)
        for part, x in enumerate((k.ir, k.ii)):
            for g2 in range(2):
                half = slice(g2 * NS, (g2 + 1) * NS)
                ins = nc.scalar.activation(k.spad[half, part, :, g2, :], x[half, :, 0:NC], ACT.Copy)
        ins

    def multiplier(vec, c):
        return vec.unsqueeze(2).broadcast_to([P, NQ, c])

    @k.block.vector
    def _(dve):
        v = nc.vector
        tt = v.tensor_tensor

        def scan(s):
            sh = 1 << s
            w = NC - sh
            if s:
                dve.wait_ge(k.sc_upd_d, s)
                dve.wait_ge(k.sc_upd_p, 2 * s)
            tt(k.sct[:, 0, :, 0:w], k.ir[:, :, 1:1 + w], multiplier(k.apr[:, 3 + s], w), ALU.mult)
            tt(k.sct[:, 1, :, 0:w], k.ii[:, :, 1:1 + w], multiplier(k.api[:, 3 + s], w), ALU.mult).then_inc(k.sc_prod_d, 1)
            dve.wait_ge(k.sc_prod_d, s + 1)
            tt(k.sct[:, 0, :, 0:w], k.sct[:, 0, :, 0:w], k.sct[:, 1, :, 0:w], ALU.subtract).then_inc(k.m3_ready, 1)
            dve.wait_ge(k.m3_ready, s + 1)
            dve.wait_ge(k.sc_prod_p, s + 1)
            tt(k.ir[:, :, 1 + sh:], k.ir[:, :, 1 + sh:], k.sct[:, 0, :, 0:w], ALU.add).then_inc(k.sc_upd_d, 1)

        def evac_probs(i):
            qb, h = jobs[i]
            dve.wait_ge(k.pt_out, i + 1)
            if i >= 2:
                dve.wait_ge(k.pv_out, i - 1)
            n = (qb + 1) * P
            v.tensor_copy(k.probT[:, i % 2, 0:qb + 1].rearrange("p b n -> p (b n)"), ps[:, 3 + i % 2, 0:n]).then_inc(k.pt_evac, 1)

        def evac_out(qb):
            dve.wait_ge(k.exp_done, HEADS * (qb + 1))
            v.reciprocal(k.rinv[:, qb * HEADS:(qb + 1) * HEADS], k.rsum[:, qb * HEADS:(qb + 1) * HEADS]).then_inc(k.rinv_done, 1)
            dve.wait_ge(k.rinv_done, qb + 1)
            dve.wait_ge(k.pv_out, HEADS * (qb + 1))
            tt(k.y_mla[:, qb].rearrange("p (h c) -> p h c", c=VD), ps[:, 5 + qb % 2].rearrange("p (h c) -> p h c", c=VD),
               k.rinv[:, qb * HEADS:(qb + 1) * HEADS].unsqueeze(2).broadcast_to([P, HEADS, VD]), ALU.mult).then_inc(k.o_evac, 1)

        for i in range(len(jobs) + 2):
            if i < len(jobs):
                qb, h = jobs[i]
                dve.wait_ge(k.sc_out, i + 1)
                v.tensor_reduce(k.nmax[:, i:i + 1], ps[:, i % 3, 0:(qb + 1) * P], AXX, ALU.max, negate=True).then_inc(k.nmax_ready, 1)
            if 1 <= i <= len(jobs):
                evac_probs(i - 1)
            if i in SCAN_AT:
                scan(SCAN_AT[i])
            if i >= 2 + HEADS and (i - 2) % HEADS == 0:
                evac_out((i - 2) // HEADS - 1)
        evac_out(TT - 1)

    @k.block.gpsimd
    def _(pool):
        tt = nc.gpsimd.tensor_tensor
        nc.gpsimd.memset(k.spad[:, :, :, :, :], 0.0).then_inc(k.spad_zero, 1)
        for s in range(6):
            sh = 1 << s
            w = NC - sh
            if s:
                pool.wait_ge(k.sc_upd_d, s)
                pool.wait_ge(k.sc_upd_p, 2 * s)
            tt(k.sct[:, 2, :, 0:w], k.ii[:, :, 1:1 + w], multiplier(k.apr[:, 3 + s], w), ALU.mult)
            tt(k.sct[:, 3, :, 0:w], k.ir[:, :, 1:1 + w], multiplier(k.api[:, 3 + s], w), ALU.mult).then_inc(k.sc_prod_p, 1)
            pool.wait_ge(k.sc_prod_p, s + 1)
            tt(k.sct[:, 2, :, 0:w], k.sct[:, 2, :, 0:w], k.sct[:, 3, :, 0:w], ALU.add).then_inc(k.sc_upd_p, 1)
            pool.wait_ge(k.sc_upd_p, 2 * s + 1)
            pool.wait_ge(k.sc_prod_d, s + 1)
            tt(k.ii[:, :, 1 + sh:], k.ii[:, :, 1 + sh:], k.sct[:, 2, :, 0:w], ALU.add).then_inc(k.sc_upd_p, 1)


def place_mix(k):
    k.w_glu = k.sb("w_glu", [P, SK, S5W], 6)
    k.sq5 = k.sb("sq5", [P, SK, T], 14)
    k.w_out = k.sb("w_out", [P, DK, D], 22)
    k.ln_g = k.sb("ln_g", [P, D], 54)
    k.ln_b = k.sb("ln_b", [P, D], 58)
    k.h2T = k.sb("h2T", [P, DK, T], 62)
    k.x_re = k.sb("x_re", [P, TT, D], 78)
    k.r5 = k.sb("r5", [P, T], 94)
    k.ssq = k.sb("ssq", [P, TT], 96)
    k.stats = k.sb("stats", [P, TT, 2, 6], 96.25)
    k.mv = k.sb("mv", [P, TT, 2], 96.5)
    k.rstd = k.sb("rstd", [P, TT], 96.625)
    k.yt = k.sb("yt", [P, GROUPS, NC], 98)
    k.gate = k.sb("gate", [P, D], 115)
    k.gcol = k.sb("gcol", [P, DK, P], 119)
    k.yT = k.sb("yT", [P, SK, CH, NC], 131)
    k.gT = k.sb("gT", [P, SK, T], 139)
    k.sig = k.sb("sig", [P, SK, T], 149)
    k.x1 = k.sb("x1", [P, TT, D], 160)
    k.y5n = k.sb("y5n", [P, SK, T], 191)
    k.ymT = k.sb("ymT", [P, SK, T], 199)


def mix(nc, io, k, ps):
    k.s_wglu, k.s_wout, k.s_xre, k.s_ln1, k.s_yout, k.s_yin = k.sems("s_wglu s_wout s_xre s_ln1 s_yout s_yin")
    k.s_x1out, k.y_out, k.y_evac, k.gate_out, k.gate_evac, k.gcol_ready = k.sems("s_x1out y_out y_evac gate_out gate_evac gcol_ready")
    k.ym_ready, k.ym_out, k.ym_evac, k.ssq_ready, k.mla_rt, k.d_done = k.sems("ym_ready ym_out ym_evac ssq_ready mla_rt d_done")
    k.gelu4_done, k.z_out, k.sig_done, k.y5_ready, k.sq5_ready, k.r5_out = k.sems("gelu4_done z_out sig_done y5_ready sq5_ready r5_out")
    k.r5_rt, k.y5n_ready, k.op_out, k.op_evac, k.rt1, k.ln_sq = k.sems("r5_rt y5n_ready op_out op_evac rt1 ln_sq")
    k.ln_gain, k.x1_ready, k.x1t_out = k.sems("ln_gain x1_ready x1t_out")
    mm = nc.tensor.matmul
    y_scr = k.y_scr

    @k.block.sync
    def _(sp):
        sp.dma_start(k.w_glu[:, :, :], io["s5_w_glu"][0].rearrange("(kt p) n -> p kt n", p=P)).then_inc(k.s_wglu, 16)
        sp.dma_start(k.w_out[:, :, :], io["w_out"][0].rearrange("(kt p) n -> p kt n", p=P)).then_inc(k.s_wout, 16)
        sp.dma_start(k.x_re[:, :, :], io["x"][0].rearrange("(t p) d -> p t d", p=P)).then_inc(k.s_xre, 16)
        sp.wait_ge(k.y_evac, 4)
        for s in range(CH):
            sp.dma_start(y_scr.rearrange("(g h) (s c) -> h g s c", h=GH, s=CH)[:, :, s, :],
                         k.yt[s * GH:(s + 1) * GH, :, :]).then_inc(k.s_yout, 16)
        sp.wait_ge(k.s_yout, 16 * CH)
        sp.dma_start(k.yT[:, :, :, :].rearrange("p m s c -> p m (s c)"),
                     y_scr.rearrange("(m p) t -> p m t", p=P)).then_inc(k.s_yin, 16)
        for name, dst in (("ln1_g", k.ln_g), ("ln1_b", k.ln_b)):
            a = io[name]
            sp.dma_start(dst[:, :], bass.AP(a.tensor, a.offset, [[0, P], [1, D]])).then_inc(k.s_ln1, 16)
        for t in range(TT):
            sp.wait_ge(k.x1_ready, t + 1)
            sp.dma_start(k.x1_scr[t * P:(t + 1) * P, :], k.x1[:, t, :]).then_inc(k.s_x1out, 16)
        sp.wait_ge(k.s_x1out, 16 * TT)

    @k.block.gpsimd
    def _(pool):
        nc.gpsimd.tensor_copy(k.gcol[:, :, :], k.modc[:, 2 * DK:3 * DK].unsqueeze(2).broadcast_to([P, DK, P])).then_inc(k.gcol_ready, 1)
        pool.wait_ge(k.y5_ready, 1)
        for m in range(SK):
            ins = nc.gpsimd.tensor_tensor(k.sq5[:, m], k.sig[:, m], k.sig[:, m], ALU.mult)
        ins.then_inc(k.sq5_ready, 1)
        pool.wait_ge(k.s_ln1, 32)
        for t in range(TT):
            pool.wait_ge(k.ln_gain, t + 1)
            nc.gpsimd.tensor_tensor(k.x1[:, t], k.x1[:, t], k.ln_b[:, :], ALU.add).then_inc(k.x1_ready, 1)

    @k.block.scalar
    def _(act):
        gn = k.cols[:, ROW_AT["gn_mla"]:]
        bglu = k.cols[:, ROW_AT["s5_b_glu"]:]
        for t in range(TT):
            ins = nc.scalar.activation(k.sig[:, t], k.y_mla[:, t], ACT.Square, accum_out=k.ssq[:, t:t + 1])
        ins.then_inc(k.ssq_ready, 1)
        act.wait_ge(k.ssq_ready, 1)
        nc.scalar.activation(k.rstd[:, :], k.ssq[:, :], ACT.Sqrt, scale=1.0 / (HEADS * VD), bias=k.eps[:, 0:1]).then_inc(k.mla_rt, 1)
        for b in range(4):
            act.wait_ge(k.y_out, b + 1)
            nc.scalar.activation(k.yt[:, 8 * b:8 * b + 8].rearrange("p g c -> p (g c)"), ps[:, b], ACT.Copy).then_inc(k.y_evac, 1)
        act.wait_ge(k.gate_out, 1)
        nc.scalar.activation(k.gate[:, 0:512], ps[:, 4], ACT.Copy)
        nc.scalar.activation(k.gate[:, 512:], ps[:, 5], ACT.Copy).then_inc(k.gate_evac, 1)
        for m in range(SK):
            act.wait_ge(k.ym_out, m + 1)
            nc.scalar.activation(k.ymT[:, m], ps[:, (6, 7, 4, 5)[m]], ACT.Copy, scale=gn[:, m:m + 1]).then_inc(k.ym_evac, 1)
        for m in range(SK):
            act.wait_ge(k.d_done, m + 1)
            nc.scalar.activation(k.gT[:, m], k.yT[:, m].rearrange("p s c -> p (s c)"), ACT.Gelu_apprx_tanh).then_inc(k.gelu4_done, 1)
        for m in range(SK):
            act.wait_ge(k.z_out, m + 1)
            nc.scalar.activation(k.sig[:, m], ps[:, m], ACT.Sigmoid, bias=bglu[:, m:m + 1]).then_inc(k.sig_done, 1)
        act.wait_ge(k.r5_out, 1)
        nc.scalar.activation(k.r5[:, :], ps[:, 4], ACT.Sqrt, scale=1.0 / S5W, bias=k.eps[:, 0:1]).then_inc(k.r5_rt, 1)
        for t in range(TT):
            act.wait_ge(k.rt1, t + 1)
            nc.scalar.activation(k.rstd[:, t:t + 1], k.mv[:, t, 1:2], ACT.Sqrt, bias=k.eps[:, 0:1]).then_inc(k.ln_sq, 1)

    @k.block.vector
    def _(dve):
        step = k.dve_steps.on(dve)
        v = nc.vector
        tt = v.tensor_tensor
        dcol = k.cols[:, ROW_AT["s5_d"]:]
        gn = k.cols[:, ROW_AT["gn_s5"]:]
        dve.wait_ge(k.mla_rt, 1)
        step(v.reciprocal(k.rstd[:, :], k.rstd[:, :]))
        for t in range(TT):
            ins = v.tensor_scalar(k.y_mla[:, t], k.y_mla[:, t], k.rstd[:, t:t + 1], None, ALU.mult)
        ins.then_inc(k.ym_ready, 1)
        dve.wait_ge(k.s_yin, 16)
        for m in range(SK):
            v.scalar_tensor_tensor(k.yT[:, m], k.uT[:, m], dcol[:, m:m + 1], k.yT[:, m], ALU.mult, ALU.add).then_inc(k.d_done, 1)
        for m in range(SK):
            dve.wait_ge(k.sig_done, m + 1)
            ins = tt(k.sig[:, m], k.gT[:, m], k.sig[:, m], ALU.mult)
        step.tell(ins, k.y5_ready)
        dve.wait_ge(k.r5_rt, 1)
        step(v.reciprocal(k.r5[:, :], k.r5[:, :]))
        for m in range(SK):
            ins = v.scalar_tensor_tensor(k.y5n[:, m].rearrange("p (c s) -> p s c", s=CH),
                                         k.sig[:, m].rearrange("p (s c) -> p s c", s=CH), gn[:, m:m + 1],
                                         k.r5[:, :].rearrange("p (s c) -> p s c", s=CH), ALU.mult, ALU.mult)
        ins.then_inc(k.y5n_ready, 1)
        dve.wait_ge(k.s_xre, 16)
        dve.wait_ge(k.gate_evac, 1)
        dve.wait_ge(k.s_ln1, 32)
        for t in range(TT):
            for half in range(2):
                n = 2 * t + half
                cols = slice(half * 512, (half + 1) * 512)
                dve.wait_ge(k.op_out, n + 1)
                step.tell(tt(k.x1[:, t, cols], ps[:, n], k.gate[:, cols], ALU.mult), k.op_evac, n + 1)
                step(v.scalar_tensor_tensor(k.x1[:, t, cols], k.x_re[:, t, cols], ALPHA, k.x1[:, t, cols], ALU.mult, ALU.add))
                step(v.bn_stats(k.stats[:, t, half], k.x1[:, t, cols]))
            step.tell(v.bn_aggr(k.mv[:, t], k.stats[:, t].rearrange("p a b -> p (a b)")), k.rt1, t + 1)
            dve.wait_ge(k.ln_sq, t + 1)
            step(v.reciprocal(k.rstd[:, t:t + 1], k.rstd[:, t:t + 1]))
            step(v.tensor_scalar(k.x1[:, t], k.x1[:, t], k.mv[:, t, 0:1], k.rstd[:, t:t + 1], ALU.subtract, ALU.mult))
            tt(k.x1[:, t], k.x1[:, t], k.ln_g[:, :], ALU.mult).then_inc(k.ln_gain, 1)
        for kt in range(DK):
            dve.wait_ge(k.x1t_out, kt + 1)
            v.tensor_scalar(k.h2T[:, kt], ps[:, kt], k.modc[:, 4 * DK + kt:4 * DK + kt + 1], k.modc[:, 3 * DK + kt:3 * DK + kt + 1],
                            ALU.mult, ALU.add)

    @k.block.tensor
    def _(pe):
        for b in range(4):
            for q in range(4 * b, 4 * b + 4):
                out = ps[:, b, (q % 4) * P:(q % 4 + 1) * P]
                for part, z in enumerate((k.zr, k.zn)):
                    mm(out, z[:, q, 1:].rearrange("p s h -> p (s h)"), k.spad[:, part, q].rearrange("p a c -> p (a c)"),
                       start=(part == 0), stop=False)
                for g2 in range(2):
                    ins = mm(out[:, g2 * NC:(g2 + 1) * NC], k.m1[:, 2 * q + g2], k.ut[:, 2 * q + g2], start=False, stop=(g2 == 1))
            ins.then_inc(k.y_out, 1)
        pe.wait_ge(k.gcol_ready, 1)
        for i in range(DK):
            ins = mm(ps[:, 4 + i // 4, (i % 4) * P:(i % 4 + 1) * P], k.gcol[:, i], k.ident[:, :], start=True, stop=True)
        ins.then_inc(k.gate_out, 1)
        pe.wait_ge(k.ym_ready, 1)
        for m in range(SK):
            if m == 2:
                pe.wait_ge(k.gate_evac, 1)
            for t in range(TT):
                ins = nc.tensor.transpose(ps[:, (6, 7, 4, 5)[m], t * P:(t + 1) * P], k.y_mla[:, t, m * P:(m + 1) * P], k.ident[:, :])
            ins.then_inc(k.ym_out, 1)
        pe.wait_ge(k.gelu4_done, 4)
        pe.wait_ge(k.s_wglu, 16)
        pe.wait_ge(k.y_evac, 4)
        for m in range(SK):
            for kt in range(SK):
                ins = mm(ps[:, m], k.w_glu[:, kt, m * P:(m + 1) * P], k.gT[:, kt], start=(kt == 0), stop=(kt == SK - 1))
            ins.then_inc(k.z_out, 1)
        pe.wait_ge(k.sq5_ready, 1)
        pe.wait_ge(k.ym_evac, 4)
        for m in range(SK):
            ins = mm(ps[:, 4], k.ones[:, :], k.sq5[:, m], start=(m == 0), stop=(m == SK - 1))
        ins.then_inc(k.r5_out, 1)
        pe.wait_ge(k.y5n_ready, 1)
        pe.wait_ge(k.s_wout, 16)
        for t in range(TT):
            for half in range(2):
                n = 2 * t + half
                for kt in range(DK):
                    y = (k.ymT if kt < SK else k.y5n)[:, kt % SK, t * P:(t + 1) * P]
                    w = k.w_out[:, (kt + SK) % DK, half * 512:(half + 1) * 512]
                    ins = mm(ps[:, n], y, w, start=(kt == 0), stop=(kt == DK - 1))
                ins.then_inc(k.op_out, 1)
        pe.wait_ge(k.x1_ready, TT)
        for kt in range(DK):
            pe.wait_ge(k.op_evac, kt + 1)
            for t in range(TT):
                ins = nc.tensor.transpose(ps[:, kt, t * P:(t + 1) * P], k.x1[:, t, kt * P:(kt + 1) * P], k.ident[:, :])
            ins.then_inc(k.x1t_out, 1)


BIG_NEG = -3.0e38
RING = 32
NBLK = PKEYS
CHK = 64


def place_peer(k):
    k.iota = k.sb("iota", [P, PKEYS], 3)
    k.iota16 = k.sb("iota16", [P, PTOP], 3.5)
    k.iotai = k.sb("iotai", [P, PKEYS], 4, I32)
    k.h2h = k.sb("h2h", [P, DK, T], 6, F32R)
    k.h2l = k.sb("h2l", [P, DK, T], 22, F32R)
    k.w_q = k.sb("w_q", [P, 4, DK, 2 * PHALF], 78)
    k.keys = k.sb("keys", [P, 2, PH, PHALF], 110)
    k.keysT = k.sb("keysT", [P, PH, 2, PKEYS], 174)
    k.qT = k.sb("qT", [P, 2 * PH, T], 142)
    k.u_raw = k.sb("u_raw", [P, 2, D], 38)
    k.uth = k.sb("uth", [P, 2, DK, P], 46, F32R)
    k.utl = k.sb("utl", [P, 2, DK, P], 54, F32R)
    k.yacc = k.sb("yacc", [P, TT, D], 62)
    k.ring = k.sb("ring", [P, RING, T], 78)
    k.qs = k.sb("qs", [P, 2 * PH, P], 182)
    k.s_tt = k.sb("s_tt", [P, PH, 2, PKEYS], 190)
    k.eq = k.sb("eq", [P, PH * PTOP, PTOP], 190)
    k.cand = k.sb("cand", [P, PTOP, PTOP], 62)
    k.cand2 = k.sb("cand2", [P, PTOP * PTOP], 63)
    k.s2 = k.sb("s2", [P, PKEYS], 64)
    k.vals = k.sb("vals", [P, PH, 2, PTOP], 65)
    k.idx = k.sb("idx", [P, PH, 2, PTOP], 66, U32)
    k.idxf = k.sb("idxf", [P, PH, 2, PTOP], 67)
    k.tops = k.sb("tops", [P, PH, PTOP], 68)
    k.topc = k.sb("topc", [P, PH, PTOP], 68.5, U32)
    k.cab = k.sb("cab", [P, 2, PH * PTOP], 69, U32)
    k.cabf = k.sb("cabf", [P, 2, PH * PTOP], 70)
    k.route = k.sb("route", [P, 3, PH * PTOP], 71)
    k.gsum = k.sb("gsum", [P, PH], 72.5)
    k.routeT = k.sb("routeT", [P, 3, T], 198)
    k.hot2 = k.sb("hot2", [P, 16, P], 62)
    k.hot1 = k.sb("hot1", [P, 16, P], 70)
    k.stage = k.sb("stage", [P, PKEYS, CHK], 142)
    k.g_in = k.sb("g_in", [P, 2, 2, T], 142)
    k.v_raw = k.sb("v_raw", [P, 2, 2, 512], 150)
    k.vh = k.sb("vh", [P, 2, 2, 512], 158, F32R)
    k.vl = k.sb("vl", [P, 2, 2, 512], 166, F32R)
    k.w_f = k.sb("w_f", [P, 2, T], 174)
    k.wh = k.sb("wh", [P, 2, 2, T], 178, F32R)
    k.wl = k.sb("wl", [P, 2, 2, T], 186, F32R)


def place_end(k):
    k.x1b = k.sb("x1b", [P, TT, D], 78)
    k.ln2_g = k.sb("ln2_g", [P, D], 94)
    k.ln2_b = k.sb("ln2_b", [P, D], 98)
    k.gate2 = k.sb("gate2", [P, D], 102)
    k.gcol2 = k.sb("gcol2", [P, DK, P], 106)
    k.stats2 = k.sb("stats2", [P, TT, 2, 6], 110)
    k.mv2 = k.sb("mv2", [P, TT, 2], 110.25)
    k.rstd2 = k.sb("rstd2", [P, TT], 110.5)


def query(nc, io, k, ps):
    k.s_keys, k.q_out, k.q_evac, k.h2h_done, k.iota_done = k.sems("s_keys q_out q_evac h2h_done iota_done")
    wq = [k.sem(f"s_wq{i}") for i in range(4)]
    mm = nc.tensor.matmul

    @k.block.sync
    def _(sp):
        for side, name in enumerate(("peer_keys1", "peer_keys2")):
            sp.dma_start(k.keys[:, side], io[name][0].rearrange("h k d -> k h d")).then_inc(k.s_keys, 16)
        w = io["peer_w_query"][0].rearrange("(kt p) n -> p kt n", p=P)
        for h in range(PH):
            if h >= 4:
                sp.wait_ge(k.q_out, 4 + 2 * (h - 3))
            sp.dma_start(k.w_q[:, h % 4], w[:, :, h * 2 * PHALF:(h + 1) * 2 * PHALF]).then_inc(wq[h % 4], 16)

    @k.block.gpsimd
    def _(pool):
        nc.gpsimd.iota(k.iotai[:, :], [[1, PKEYS]], base=0, channel_multiplier=0).then_inc(k.iota_done, 1)
        pool.wait_ge(k.iota_done, 1)
        nc.gpsimd.tensor_copy(k.iota[:, :], k.iotai[:, :])
        nc.gpsimd.tensor_copy(k.iota16[:, :], k.iotai[:, 0:PTOP])

    @k.block.tensor
    def _(pe):
        pe.wait_ge(k.s_keys, 32)
        for n in range(4):
            for i in range(4):
                h, side = 2 * n + i // 2, i % 2
                ins = nc.tensor.transpose(ps[:, n, i * P:(i + 1) * P], k.keys[:, side, h], k.ident[:, :])
            ins.then_inc(k.q_out, 1)
        for j in range(2 * PH):
            n = 4 + j
            h, side = j // 2, j % 2
            if side == 0:
                pe.wait_ge(wq[h % 4], 16 * (h // 4 + 1))
            if n >= 8:
                pe.wait_ge(k.q_evac, n - 7)
            for kt in range(DK):
                ins = mm(ps[:, n % 8], k.w_q[:, h % 4, kt, side * PHALF:(side + 1) * PHALF], k.h2T[:, kt],
                         start=(kt == 0), stop=(kt == DK - 1))
            ins.then_inc(k.q_out, 1)

    @k.block.scalar
    def _(act):
        for kt in range(DK):
            nc.scalar.activation(k.h2h[:, kt], k.h2T[:, kt], ACT.Copy).then_inc(k.h2h_done, 1)
        for n in range(4 + 2 * PH):
            act.wait_ge(k.q_out, n + 1)
            dst = k.keysT[:, 2 * n:2 * n + 2].rearrange("p a b c -> p (a b c)") if n < 4 else k.qT[:, n - 4]
            nc.scalar.activation(dst, ps[:, n % 8], ACT.Copy).then_inc(k.q_evac, 1)

    @k.block.vector
    def _(dve):
        for kt in range(DK):
            dve.wait_ge(k.h2h_done, kt + 1)
            nc.vector.tensor_tensor(k.h2l[:, kt], k.h2T[:, kt], k.h2h[:, kt].bitcast(F32), ALU.subtract)


class Blocks:
    UT_OUT, UTL, ACT_OUT, GELU, W, WL, Y_MM, YACC, VL = 4, 2, 2, 2, RING, 2, 9, 4, 2

    def __init__(self, nc, io, k, ps):
        self.nc, self.k, self.ps = nc, k, ps
        self.u = io["peer_u"][0].rearrange("(e p) d -> p e d", p=P)
        self.v = io["peer_v"][0].rearrange("(e p) d -> p e d", p=P)
        k.ut_out, k.uth_done, k.utl_done, k.act_out, k.gelu_done, k.w_done = k.sems("ut_out uth_done utl_done act_out gelu_done w_done")
        k.wh_done, k.wl_done, k.vh_done, k.vl_done, k.y_mm, k.yacc_done = k.sems("wh_done wl_done vh_done vl_done y_mm yacc_done")
        k.yacc_zero, = k.sems("yacc_zero")
        self.u_in = [k.sem(f"s_u_in{i}") for i in range(2)]
        self.g_in = [k.sem(f"s_g_in{i}") for i in range(2)]
        self.v_in = [k.sem(f"s_v_in{i}") for i in range(2)]

    def credits_pe(self, pe):
        pe.sem_inc(self.k.ut_out, self.UT_OUT)
        pe.sem_inc(self.k.act_out, self.ACT_OUT)
        pe.sem_inc(self.k.y_mm, self.Y_MM)

    def credits_act(self, act):
        act.sem_inc(self.k.gelu_done, self.GELU)

    def credits_dve(self, dve):
        dve.sem_inc(self.k.utl_done, self.UTL)
        dve.sem_inc(self.k.w_done, self.W)
        dve.sem_inc(self.k.yacc_done, self.YACC)

    def credits_pool(self, pool):
        pool.sem_inc(self.k.wl_done, self.WL)
        pool.sem_inc(self.k.vl_done, self.VL)

    def load_u(self, sp, b, i):
        k = self.k
        sp.wait_ge(k.ut_out, self.UT_OUT + 2 * b - 2)
        sp.dma_start(k.u_raw[:, i % 2], self.u[:, bass.ds(b, 1), :].rearrange("p a d -> p (a d)")).then_inc(self.u_in[i % 2], 16)

    def transpose_u(self, pe, b, half_b, i):
        k = self.k
        pe.wait_ge(self.u_in[i % 2], 16 * half_b + 16)
        for hf in range(2):
            pe.wait_ge(k.utl_done, self.UTL + 2 * b - 1 + hf)
            for c in range(4):
                ins = self.nc.tensor.transpose(self.ps[:, hf, c * P:(c + 1) * P],
                                               k.u_raw[:, i % 2, (4 * hf + c) * P:(4 * hf + c + 1) * P], k.ident[:, :])
            ins.then_inc(k.ut_out, 1)

    def split_u_high(self, act, b, i):
        k = self.k
        act.wait_ge(k.act_out, self.ACT_OUT + b - 1)
        for hf in range(2):
            act.wait_ge(k.ut_out, self.UT_OUT + 2 * b + 1 + hf)
            self.nc.scalar.activation(k.uth[:, i % 2, 4 * hf:4 * hf + 4].rearrange("p c n -> p (c n)"), self.ps[:, hf],
                                      ACT.Copy).then_inc(k.uth_done, 1)

    def split_u_low(self, dve, b, i):
        k = self.k
        for hf in range(2):
            dve.wait_ge(k.uth_done, 2 * b + 1 + hf)
            hi = k.uth[:, i % 2, 4 * hf:4 * hf + 4].rearrange("p c n -> p (c n)")
            lo = k.utl[:, i % 2, 4 * hf:4 * hf + 4].rearrange("p c n -> p (c n)")
            self.nc.vector.tensor_tensor(lo, self.ps[:, hf], hi.bitcast(F32), ALU.subtract).then_inc(k.utl_done, 1)

    def activations(self, pe, b, i):
        k = self.k
        pe.wait_ge(k.utl_done, self.UTL + 2 * b + 2)
        pe.wait_ge(k.gelu_done, self.GELU + b - 1)
        out = self.ps[:, 2 + i % 2]
        for kt in range(DK):
            hi, lo = k.uth[:, i % 2, kt], k.utl[:, i % 2, kt]
            self.nc.tensor.matmul(out, hi, k.h2h[:, kt], start=(kt == 0), stop=False)
            self.nc.tensor.matmul(out, hi, k.h2l[:, kt], start=False, stop=False)
            ins = self.nc.tensor.matmul(out, lo, k.h2h[:, kt], start=False, stop=(kt == DK - 1))
        ins.then_inc(k.act_out, 1)

    def gelu(self, act, b, slot, i):
        k = self.k
        act.wait_ge(k.act_out, self.ACT_OUT + b + 1)
        act.wait_ge(k.w_done, self.W + b - RING + 1)
        self.nc.scalar.activation(k.ring[:, bass.ds(slot, 1), :].rearrange("p a t -> p (a t)"), self.ps[:, 2 + i % 2],
                                  ACT.Gelu_apprx_tanh).then_inc(k.gelu_done, 1)

    def load_g(self, sp, p, half_p, i):
        k = self.k
        sp.wait_ge(k.w_done, self.W + 2 * p - 2)
        sp.dma_start(k.g_in[:, i % 2], k.g_scr[bass.ds(2 * p, 2)].rearrange("e p t -> p e t")).then_inc(self.g_in[i % 2], 16)

    def load_v(self, sp, p, half):
        k = self.k
        sp.wait_ge(k.vl_done, self.VL + 2 * p + half - 1)
        sp.dma_start(k.v_raw[:, half], self.v[:, bass.ds(2 * p, 2), half * 512:(half + 1) * 512]).then_inc(self.v_in[half], 16)

    def weight(self, dve, b, half_p, slot, i):
        k = self.k
        pr, e = i // 2, i % 2
        if e == 0:
            dve.wait_ge(self.g_in[pr], 16 * half_p + 16)
        dve.wait_ge(k.gelu_done, self.GELU + b + 1)
        dve.wait_ge(k.wl_done, self.WL + b - 1)
        self.nc.vector.tensor_tensor(k.w_f[:, e], k.ring[:, bass.ds(slot, 1), :].rearrange("p a t -> p (a t)"),
                                     k.g_in[:, pr, e], ALU.mult).then_inc(k.w_done, 1)

    def split_w_high(self, act, b, p, i):
        k = self.k
        act.wait_ge(k.w_done, self.W + b + 1)
        act.wait_ge(k.y_mm, self.Y_MM + 8 * p - 8)
        self.nc.scalar.activation(k.wh[:, i // 2, i % 2], k.w_f[:, i % 2], ACT.Copy).then_inc(k.wh_done, 1)

    def split_w_low(self, pool, b, i):
        k = self.k
        pool.wait_ge(k.wh_done, b + 1)
        self.nc.gpsimd.tensor_tensor(k.wl[:, i // 2, i % 2], k.w_f[:, i % 2], k.wh[:, i // 2, i % 2].bitcast(F32),
                                     ALU.subtract).then_inc(k.wl_done, 1)

    def split_v_high(self, act, p, half):
        k = self.k
        act.wait_ge(self.v_in[half], 16 * p + 16)
        act.wait_ge(k.y_mm, self.Y_MM + 8 * p - 4 + 4 * half)
        self.nc.scalar.activation(k.vh[:, half].rearrange("p e d -> p (e d)"), k.v_raw[:, half].rearrange("p e d -> p (e d)"),
                                  ACT.Copy).then_inc(k.vh_done, 1)

    def split_v_low(self, pool, p, half):
        k = self.k
        pool.wait_ge(k.vh_done, 2 * p + half + 1)
        f = "p e d -> p (e d)"
        self.nc.gpsimd.tensor_tensor(k.vl[:, half].rearrange(f), k.v_raw[:, half].rearrange(f),
                                     k.vh[:, half].bitcast(F32).rearrange(f), ALU.subtract).then_inc(k.vl_done, 1)

    def products(self, pe, p, pr, half):
        k, mm = self.k, self.nc.tensor.matmul
        pe.wait_ge(k.wl_done, self.WL + 2 * p + 2)
        pe.wait_ge(k.vl_done, self.VL + 2 * p + half + 1)
        for t in range(TT):
            pe.wait_ge(k.yacc_done, self.YACC + 8 * p + 4 * half - 3 + t)
            out = self.ps[:, 4 + t]
            for e in range(2):
                hi, lo = k.wh[:, pr, e, t * P:(t + 1) * P], k.wl[:, pr, e, t * P:(t + 1) * P]
                mm(out, hi, k.vh[:, half, e], start=(e == 0), stop=False)
                mm(out, hi, k.vl[:, half, e], start=False, stop=False)
                ins = mm(out, lo, k.vh[:, half, e], start=False, stop=(e == 1))
            ins.then_inc(k.y_mm, 1)

    def add_products(self, dve, p, half):
        k = self.k
        for t in range(TT):
            dve.wait_ge(k.y_mm, self.Y_MM + 8 * p + 4 * half + t + 1)
            y = k.yacc[:, t, half * 512:(half + 1) * 512]
            self.nc.vector.tensor_tensor(y, y, self.ps[:, 4 + t], ALU.add).then_inc(k.yacc_done, 1)


def route(nc, io, k, ps, bl):
    k.qs_ready, k.sc6_out, k.s_ready, k.steps6, k.route_ready, k.rt_out = k.sems("qs_ready sc6_out s_ready steps6 route_ready rt_out")
    k.rt_evac, k.exp6_in, k.exp6_done = k.sems("rt_evac exp6_in exp6_done")
    mm = nc.tensor.matmul

    @k.block.sync
    def _(sp):
        with sp.Fori(0, TT) as it:
            for i in range(PH):
                bl.load_u(sp, it * PH + i, i)

    @k.block.scalar
    def _(act):
        bl.credits_act(act)
        act.sem_inc(k.rt_evac, 1)
        with act.Fori(0, TT) as it:
            act.wait_ge(k.sc6_out, 1 + 4 * it)
            nc.scalar.activation(k.qs[:, :, :], k.qT[:, :, bass.ds(it * P, P)], ACT.Copy).then_inc(k.qs_ready, 1)
            act.wait_ge(k.route_ready, 1 + 2 * it)
            for j in range(4):
                act.wait_ge(k.sc6_out, 1 + 4 * it + j + 1)
                nc.scalar.activation(k.s_tt[:, 2 * j:2 * j + 2].rearrange("p a b c -> p (a b c)"), ps[:, 4 + j], ACT.Copy).then_inc(k.s_ready, 1)
            for i in range(PH):
                bl.split_u_high(act, it * PH + i, i)
                bl.gelu(act, it * PH + i, it * PH + i, i)
            act.wait_ge(k.exp6_in, it + 1)
            nc.scalar.activation(k.tops[:, :, :], k.tops[:, :, :], ACT.Exp).then_inc(k.exp6_done, 1)
            act.wait_ge(k.rt_out, it + 1)
            nc.scalar.activation(k.routeT[:, :, bass.ds(it * P, P)], ps[:, 4, 0:3 * P].rearrange("p (a t) -> p a t", a=3),
                                 ACT.Copy).then_inc(k.rt_evac, 1)

    @k.block.tensor
    def _(pe):
        bl.credits_pe(pe)
        pe.sem_inc(k.sc6_out, 1)
        with pe.Fori(0, TT) as it:
            pe.wait_ge(k.qs_ready, it + 1)
            pe.wait_ge(k.rt_evac, 1 + it)
            for j in range(4):
                for h in (2 * j, 2 * j + 1):
                    for side in range(2):
                        at = ((h % 2) * 2 + side) * PKEYS
                        ins = mm(ps[:, 4 + j, at:at + PKEYS], k.qs[:, 2 * h + side], k.keysT[:, h, side], start=True, stop=True)
                ins.then_inc(k.sc6_out, 1)
            for i in range(PH):
                b = it * PH + i
                bl.transpose_u(pe, b, it * (PH // 2) + i // 2, i)
                bl.activations(pe, b, i)
            pe.wait_ge(k.route_ready, 1 + 2 * it + 2)
            for a in range(3):
                ins = nc.tensor.transpose(ps[:, 4, a * P:(a + 1) * P], k.route[:, a], k.ident[:, :])
            ins.then_inc(k.rt_out, 1)

    @k.block.vector
    def _(dve):
        v = nc.vector
        tt = v.tensor_tensor
        bl.credits_dve(dve)
        dve.sem_inc(k.route_ready, 1)
        with dve.Fori(0, TT) as it:
            dve.sem_clear(k.steps6)
            dve.wait_ge(k.s_ready, 4 * it + 1)
            v.memset(k.gsum[:, :], 0.0)
            step = Steps(k.steps6).on(dve)
            for h in range(PH):
                for side in range(2):
                    s, vals, idx = k.s_tt[:, h, side], k.vals[:, h, side], k.idx[:, h, side]
                    step(v.max(vals[:, 0:8], s))
                    v.max_index(idx[:, 0:8], vals[:, 0:8], s)
                    step(v.match_replace(k.s2[:, :], vals[:, 0:8], s, BIG_NEG))
                    step(v.max(vals[:, 8:16], k.s2[:, :]))
                    step(v.max_index(idx[:, 8:16], vals[:, 8:16], k.s2[:, :]))
                bl.split_u_low(dve, it * PH + h, h)
                if h % 2 == 1 and h < PH - 1:
                    dve.wait_ge(k.s_ready, 4 * it + h // 2 + 2)
                step(tt(k.cand[:, :, :], k.vals[:, h, 0].unsqueeze(2).broadcast_to([P, PTOP, PTOP]),
                        k.vals[:, h, 1].unsqueeze(1).broadcast_to([P, PTOP, PTOP]), ALU.add))
                c = k.cand[:, :, :].rearrange("p a b -> p (a b)")
                step(v.max(k.tops[:, h, 0:8], c))
                v.max_index(k.topc[:, h, 0:8], k.tops[:, h, 0:8], c)
                step(v.match_replace(k.cand2[:, :], k.tops[:, h, 0:8], c, BIG_NEG))
                step(v.max(k.tops[:, h, 8:16], k.cand2[:, :]))
                v.max_index(k.topc[:, h, 8:16], k.tops[:, h, 8:16], k.cand2[:, :])
            tops = k.tops[:, :, :]
            cm = k.cabf[:, 0, 0:PH]
            step(v.tensor_copy(cm, k.tops[:, :, 0]))
            tt(tops, tops, cm.unsqueeze(2).broadcast_to([P, PH, PTOP]), ALU.subtract).then_inc(k.exp6_in, 1)
            c = k.topc[:, :, :].rearrange("p h c -> p (h c)")
            v.tensor_scalar(k.cab[:, 0], c, 4, None, ALU.logical_shift_right)
            v.tensor_scalar(k.cab[:, 1], c, PTOP - 1, None, ALU.bitwise_and)
            step(v.tensor_copy(k.idxf[:, :, :, :], k.idx[:, :, :, :]))
            dve.wait_ge(k.exp6_in, it + 1)
            step(v.tensor_copy(k.cabf[:, :, :], k.cab[:, :, :]))
            for side in range(2):
                e3 = k.eq[:, :, :]
                e4 = e3.rearrange("p (h c) a -> p h c a", h=PH)
                step(tt(e3, k.cabf[:, side].unsqueeze(2).broadcast_to([P, PH * PTOP, PTOP]),
                        k.iota16[:, :].unsqueeze(1).broadcast_to([P, PH * PTOP, PTOP]), ALU.is_equal))
                step(tt(e4, e4, k.idxf[:, :, side, :].unsqueeze(2).broadcast_to([P, PH, PTOP, PTOP]), ALU.mult))
                step(v.tensor_reduce(k.route[:, side], e3, AXX, ALU.add)) if side == 0 else \
                    v.tensor_reduce(k.route[:, side], e3, AXX, ALU.add).then_inc(k.route_ready, 1)
            dve.wait_ge(k.exp6_done, it + 1)
            step(v.tensor_reduce(k.gsum[:, :], tops, AXX, ALU.add))
            step(v.reciprocal(k.gsum[:, :], k.gsum[:, :]))
            dve.wait_ge(k.rt_evac, 1 + it)
            tt(k.route[:, 2].rearrange("p (h c) -> p h c", h=PH), tops, k.gsum[:, :].unsqueeze(2).broadcast_to([P, PH, PTOP]),
               ALU.mult).then_inc(k.route_ready, 1)
            dve.wait_ge(k.route_ready, 1 + 2 * it + 2)


def spread(nc, io, k, ps):
    k.hot_ready, k.g_out, k.g_evac, k.s_gout = k.sems("hot_ready g_out g_evac s_gout")
    mm = nc.tensor.matmul
    GRP = 16
    NCH = T // CHK
    RPC = CHK // GRP

    @k.block.vector
    def _(dve):
        v = nc.vector
        with dve.Fori(0, T // GRP) as it:
            for j in range(GRP):
                if j % 4 == 0:
                    dve.wait_ge(k.g_out, 4 * it + j // 4 + 1)
                e1 = k.routeT[:, 0, bass.ds(it * GRP + j, 1)]
                e2 = k.routeT[:, 1, bass.ds(it * GRP + j, 1)]
                w = k.routeT[:, 2, bass.ds(it * GRP + j, 1)]
                v.tensor_scalar(k.hot2[:, j], k.iota[:, :], e2, None, ALU.is_equal)
                ins = v.tensor_scalar(k.hot1[:, j], k.iota[:, :], e1, w, ALU.is_equal, ALU.mult)
                if j % 4 == 3:
                    ins.then_inc(k.hot_ready, 1)

    @k.block.tensor
    def _(pe):
        pe.sem_inc(k.g_out, 4)
        with pe.Fori(0, T // GRP) as it:
            for j in range(GRP):
                if j % 4 == 0:
                    pe.wait_ge(k.hot_ready, 4 * it + j // 4 + 1)
                    pe.wait_ge(k.g_evac, 4 * it + j // 4 + 1)
                ins = mm(ps[:, 4 + j // 4, (j % 4) * P:(j % 4 + 1) * P], k.hot2[:, j], k.hot1[:, j], start=True, stop=True)
                if j % 4 == 3:
                    ins.then_inc(k.g_out, 1)

    @k.block.scalar
    def _(act):
        act.sem_inc(k.g_evac, 4)
        with act.Fori(0, NCH) as ch:
            act.wait_ge(k.s_gout, 1 + 16 * ch)
            with act.Fori(0, RPC) as r:
                for j in range(4):
                    act.wait_ge(k.g_out, 4 + 4 * RPC * ch + 4 * r + j + 1)
                    nc.scalar.activation(k.stage[:, :, bass.ds(r * GRP + 4 * j, 4)].rearrange("p e t -> p t e"),
                                         ps[:, 4 + j].rearrange("p (t e) -> p t e", t=4), ACT.Copy).then_inc(k.g_evac, 1)

    @k.block.sync
    def _(sp):
        sp.sem_inc(k.s_gout, 1)
        with sp.Fori(0, NCH) as ch:
            sp.wait_ge(k.g_evac, 4 + 4 * RPC * (ch + 1))
            sp.dma_start(k.g_scr.rearrange("e p t -> p e t")[:, :, bass.ds(ch * CHK, CHK)], k.stage[:, :, :]).then_inc(k.s_gout, 16)
        sp.wait_ge(k.s_gout, 1 + 16 * NCH)


def experts(nc, io, k, ps, bl):
    QUADS = RING // 4
    ROUNDS = NBLK // RING

    @k.block.sync
    def _(sp):
        def second(Q):
            for pr in range(2):
                bl.load_g(sp, 2 * Q + pr, Q, pr)
                for half in range(2):
                    bl.load_v(sp, 2 * Q + pr, half)

        with sp.Fori(0, NBLK // 4 - QUADS) as Q:
            for i in range(4):
                bl.load_u(sp, RING + 4 * Q + i, i)
                if i % 2 == 0:
                    bl.load_g(sp, 2 * Q + i // 2, Q, i // 2)
                    for half in range(2):
                        bl.load_v(sp, 2 * Q + i // 2, half)
        with sp.Fori(NBLK // 4 - QUADS, NBLK // 4) as Q:
            second(Q)

    @k.block.gpsimd
    def _(pool):
        bl.credits_pool(pool)
        with pool.Fori(0, NBLK // 4) as Q:
            for i in range(4):
                bl.split_v_low(pool, 2 * Q + i // 2, i % 2)
                bl.split_w_low(pool, 4 * Q + i, i)

    @k.block.scalar
    def _(act):
        with act.Fori(0, ROUNDS - 1) as r:
            with act.Fori(0, QUADS) as q:
                for i in range(4):
                    b = r * RING + q * 4 + i
                    bl.split_u_high(act, b + RING, i)
                    bl.split_v_high(act, r * (RING // 2) + q * 2 + i // 2, i % 2)
                    bl.split_w_high(act, b, r * (RING // 2) + q * 2 + i // 2, i)
                    bl.gelu(act, b + RING, q * 4 + i, i)
        with act.Fori(NBLK // 4 - QUADS, NBLK // 4) as Q:
            for i in range(4):
                bl.split_v_high(act, 2 * Q + i // 2, i % 2)
                bl.split_w_high(act, 4 * Q + i, 2 * Q + i // 2, i)

    @k.block.vector
    def _(dve):
        nc.vector.memset(k.yacc[:, :, :], 0.0).then_inc(k.yacc_zero, 1)
        dve.wait_ge(k.yacc_zero, 1)

        def quad(Q, slot0, with_first, with_last):
            for i in range(4):
                if with_first:
                    bl.split_u_low(dve, RING + 4 * Q + i, i)
                bl.weight(dve, 4 * Q + i, Q, slot0 + i, i)
                if i >= 2 or with_last:
                    bl.add_products(dve, 2 * Q + i // 2 - 1, i % 2)

        quad(0, 0, True, False)
        with dve.Fori(1, QUADS) as q:
            quad(q, 4 * q, True, True)
        with dve.Fori(1, ROUNDS - 1) as r:
            with dve.Fori(0, QUADS) as q:
                quad(r * QUADS + q, 4 * q, True, True)
        with dve.Fori(0, QUADS) as q:
            quad(q + (ROUNDS - 1) * QUADS, 4 * q, False, True)
        for half in range(2):
            bl.add_products(dve, NBLK // 2 - 1, half)

    @k.block.tensor
    def _(pe):
        def quad(Q, with_first, with_last):
            for i in range(4):
                b = RING + 4 * Q + i
                if with_first:
                    bl.transpose_u(pe, b, RING // 2 + 2 * Q + i // 2, i)
                if i >= 2 or with_last:
                    bl.products(pe, 2 * Q + i // 2 - 1, (i // 2 + 1) % 2, i % 2)
                if with_first:
                    bl.activations(pe, b, i)

        quad(0, True, False)
        with pe.Fori(1, NBLK // 4 - QUADS) as Q:
            quad(Q, True, True)
        with pe.Fori(NBLK // 4 - QUADS, NBLK // 4) as Q:
            quad(Q, False, True)
        for half in range(2):
            bl.products(pe, NBLK // 2 - 1, 1, half)


def finish(nc, io, k, ps, out):
    k.s_x1b, k.s_ln2, k.s_out, k.gcol2_ready, k.gate2_out, k.gate2_evac = k.sems("s_x1b s_ln2 s_out gcol2_ready gate2_out gate2_evac")
    k.rt9, k.sq9, k.gain9, k.out9 = k.sems("rt9 sq9 gain9 out9")
    mm = nc.tensor.matmul

    @k.block.sync
    def _(sp):
        for name, dst in (("ln2_g", k.ln2_g), ("ln2_b", k.ln2_b)):
            a = io[name]
            sp.dma_start(dst[:, :], bass.AP(a.tensor, a.offset, [[0, P], [1, D]])).then_inc(k.s_ln2, 16)
        sp.dma_start(k.x1b[:, :, :], k.x1_scr.rearrange("(t p) d -> p t d", p=P)).then_inc(k.s_x1b, 16)
        for t in range(TT):
            sp.wait_ge(k.out9, t + 1)
            sp.dma_start(out[0, t * P:(t + 1) * P, :], k.yacc[:, t, :]).then_inc(k.s_out, 16)
        sp.wait_ge(k.s_out, 16 * TT)

    @k.block.gpsimd
    def _(pool):
        nc.gpsimd.tensor_copy(k.gcol2[:, :, :], k.modc[:, 5 * DK:6 * DK].unsqueeze(2).broadcast_to([P, DK, P])).then_inc(k.gcol2_ready, 1)
        pool.wait_ge(k.s_ln2, 32)
        for t in range(TT):
            pool.wait_ge(k.gain9, t + 1)
            nc.gpsimd.tensor_tensor(k.yacc[:, t], k.yacc[:, t], k.ln2_b[:, :], ALU.add).then_inc(k.out9, 1)

    @k.block.tensor
    def _(pe):
        pe.wait_ge(k.gcol2_ready, 1)
        for i in range(DK):
            ins = mm(ps[:, i // 4, (i % 4) * P:(i % 4 + 1) * P], k.gcol2[:, i], k.ident[:, :], start=True, stop=True)
        ins.then_inc(k.gate2_out, 1)

    @k.block.scalar
    def _(act):
        act.wait_ge(k.gate2_out, 1)
        for half in range(2):
            ins = nc.scalar.activation(k.gate2[:, half * 512:(half + 1) * 512], ps[:, half], ACT.Copy)
        ins.then_inc(k.gate2_evac, 1)
        for t in range(TT):
            act.wait_ge(k.rt9, t + 1)
            nc.scalar.activation(k.rstd2[:, t:t + 1], k.mv2[:, t, 1:2], ACT.Sqrt, bias=k.eps[:, 0:1]).then_inc(k.sq9, 1)

    @k.block.vector
    def _(dve):
        step = k.dve_steps.on(dve)
        v = nc.vector
        tt = v.tensor_tensor
        dve.wait_ge(k.gate2_evac, 1)
        dve.wait_ge(k.s_x1b, 16)
        dve.wait_ge(k.s_ln2, 32)

        def stats(t):
            y = k.yacc[:, t]
            step(tt(y, y, k.gate2[:, :], ALU.mult))
            step(v.scalar_tensor_tensor(y, k.x1b[:, t], ALPHA, y, ALU.mult, ALU.add))
            for half in range(2):
                ins = v.bn_stats(k.stats2[:, t, half], k.yacc[:, t, half * 512:(half + 1) * 512])
            step(ins)
            step.tell(v.bn_aggr(k.mv2[:, t], k.stats2[:, t].rearrange("p a b -> p (a b)")), k.rt9, t + 1)

        def normalise(t):
            y = k.yacc[:, t]
            dve.wait_ge(k.sq9, t + 1)
            step(v.reciprocal(k.rstd2[:, t:t + 1], k.rstd2[:, t:t + 1]))
            step(v.tensor_scalar(y, y, k.mv2[:, t, 0:1], k.rstd2[:, t:t + 1], ALU.subtract, ALU.mult))
            tt(y, y, k.ln2_g[:, :], ALU.mult).then_inc(k.gain9, 1)

        for t in range(TT):
            stats(t)
            if t:
                normalise(t - 1)
        normalise(TT - 1)


def build(nc, io, out, upto=9):
    k = Plan(nc)
    for f in (place, place_attention, place_mix, place_peer, place_end):
        f(k)
    ps = nc.alloc_psum_tensor("ps", [P, 8, 512], F32)

    bl = Blocks(nc, io, k, ps)
    parts = [lambda: condition(nc, io, k, ps), lambda: project(nc, io, k, ps), lambda: attend(nc, io, k, ps),
             lambda: mix(nc, io, k, ps), lambda: query(nc, io, k, ps), lambda: route(nc, io, k, ps, bl),
             lambda: spread(nc, io, k, ps), lambda: experts(nc, io, k, ps, bl), lambda: finish(nc, io, k, ps, out)]
    for part in parts[:upto]:
        with nc.Block() as block:
            k.block = block
            part()
    return k, ps


_INS = ["x", "c", "positions", "w_ada", "b_ada", "w_in",
        "s5_lambda_re", "s5_lambda_im", "s5_log_dt", "s5_b_re", "s5_b_im", "s5_c_re", "s5_c_im",
        "s5_d", "s5_w_glu", "s5_b_glu", "mla_q_norm", "mla_w_uq", "mla_kv_norm", "mla_w_ukv",
        "gn_s5", "gn_mla", "w_out", "ln1_g", "ln1_b",
        "peer_w_query", "peer_keys1", "peer_keys2", "peer_u", "peer_v", "ln2_g", "ln2_b"]


def rope_rows():
    inv = np.float32(10000.0) ** (-np.arange(0, ROPE, 2, dtype=np.float32) / np.float32(ROPE))
    sign = np.repeat(np.array([-1.0, 1.0], np.float32), ROPE // 2)
    return np.stack([np.tile(inv, 8), np.tile(sign, 4)], 1).astype(np.float32)


def kernel(**inputs):
    import concourse.bacc as bacc
    from concourse.bass_utils import run_bass_kernel_spmd as run

    nc = bacc.Bacc("TRN2", target_bir_lowering=False, num_devices=1)
    arrays, io = {}, {}
    for name in _INS + ["rope_rows"]:
        a = rope_rows() if name == "rope_rows" else np.ascontiguousarray(inputs[name])
        arrays["in_" + name] = a
        io[name] = nc.dram_tensor("in_" + name, a.shape, mybir.dt.from_np(a.dtype), kind="ExternalInput").ap()
    out = nc.dram_tensor("out", (1, T, D), F32, kind="ExternalOutput").ap()
    build(nc, io, out)
    return run(nc, [arrays], core_ids=[0]).results[0]["out"]
```

```python
import numpy as np
import concourse.bass as bass
from concourse import mybir

F32 = mybir.dt.float32
F32R = mybir.dt.float32r
U32 = mybir.dt.uint32
I32 = mybir.dt.int32
ACT = mybir.ActivationFunctionType
ALU = mybir.AluOpType
AXX = mybir.AxisListType.X

P = 128
KB = 1024
T = 512
TT = T // P
D = 1024
DK = D // P
S5W, GROUPS, GH, NS = 512, 32, 16, 64
SK = S5W // P
NQ = GROUPS // 2
CH = 8
NC = T // CH
QL, KVL, ROPE, NOPE, HEADS, VD = 384, 256, 32, 64, 8, 64
QK, KK = QL // P, KVL // P
D_IN = S5W + QL + KVL + ROPE
NMOD = 6 * D // P
PH, PKEYS, PTOP, PHALF = 8, 128, 16, 128
ALPHA = 2.0 ** 0.25
EPS = 1e-6
SCALE = float(NOPE + ROPE) ** -0.5
MASKED = -1e30
TWO_PI = 2.0 * np.pi
PI_1 = 6.28125
PI_2 = float(round((TWO_PI - PI_1) * 2**20)) / 2**20
PI_3 = float(np.float32(TWO_PI - PI_1 - PI_2))
ROUND = 1.5 * 2**23
SIN_MAX = 3.1415925

ROWS = [("c", 8), ("b_ada", 48), ("s5_d", 4), ("s5_b_glu", 4), ("gn_s5", 4), ("gn_mla", 4),
        ("mla_q_norm", 3), ("mla_kv_norm", 2), ("s5_lambda_re", 16), ("s5_lambda_im", 16)]
ROW_AT, _n = {}, 0
for _name, _m in ROWS:
    ROW_AT[_name] = _n
    _n += _m
NROWS = _n


class Plan:

    def __init__(self, nc):
        self.nc = nc
        self.u_scr = nc.dram_tensor("u_scr", (S5W, T), F32).ap()
        self.y_scr = nc.dram_tensor("y_scr", (S5W, T), F32).ap()
        self.x1_scr = nc.dram_tensor("x1_scr", (T, D), F32).ap()
        self.g_scr = nc.dram_tensor("g_scr", (PKEYS, PKEYS, T), F32).ap()
        self.act_scr = nc.dram_tensor("act_scr", (LEAD, P, T), F32).ap()
        self.dve_steps = Steps(self.sem("dve_stepped"))
        self.pool_steps = Steps(self.sem("pool_stepped"))
        self.base = (nc.sbuf_base + 63) // 64 * 64

    def sb(self, name, shape, at, dtype=F32):
        return self.nc.alloc_sbuf_tensor_at(name, shape, dtype, offset=self.base + int(round(at * KB)))

    def sem(self, name):
        return self.nc.alloc_semaphore(name)

    def sems(self, names):
        return [self.sem(n) for n in names.split()]


class Steps:

    def __init__(self, sem):
        self.eng, self.sem, self.n = None, sem, 0

    def on(self, eng):
        self.eng = eng
        return self

    def __call__(self, ins):
        self.n += 1
        ins.then_inc(self.sem, 1)
        self.eng.wait_ge(self.sem, self.n)

    def tell(self, ins, sem, n=1, by=1):
        ins.then_inc(sem, by)
        self.eng.wait_ge(sem, n)


def place(k):
    k.ident = k.sb("ident", [P, P], 0)
    k.ones = k.sb("ones", [P, P], 0.5)
    k.cols = k.sb("cols", [P, NROWS + NQ], 1)
    k.modc = k.sb("modc", [P, NMOD], 1.5)
    k.ccol = k.sb("ccol", [P, DK], 1.75)
    k.consts = k.sb("consts", [P, 2], 1.8125)
    k.eps = k.sb("eps", [P, 3], 1.84375)
    k.negrow = k.sb("negrow", [1, P], 2)
    k.onerow = k.sb("onerow", [1, NOPE], 2.5)
    k.rows = k.sb("rows", [NROWS, P], 3)
    k.ldt2 = k.sb("ldt2", [NQ, 2], 3.5)
    k.ldt_row = k.sb("ldt_row", [NQ, 2, NS], 3.625)
    k.x_tok = k.sb("x_tok", [P, TT, D], 6)
    k.hT = k.sb("hT", [P, DK, T], 22)
    k.w_in = k.sb("w_in", [P, DK, D_IN], 38)
    k.w_ada = k.sb("w_ada", [P, 3, DK, 512], 75)
    k.uT = k.sb("uT", [P, SK, CH, NC], 123)
    k.cqT = k.sb("cqT", [P, QK, T], 131)
    k.ckvT = k.sb("ckvT", [P, KK, T], 137)
    k.krT = k.sb("krT", [P, 2, T], 141)
    k.rcos = k.sb("rcos", [P, T], 145)
    k.rsin = k.sb("rsin", [P, T], 147)
    k.w_kr = k.sb("w_kr", [P, DK, 2, 4, ROPE], 149)
    k.modrow = k.sb("modrow", [1, 2 * D], 131)
    k.mod_acc = k.sb("mod_acc", [P, 4 * D], 6)
    k.posi = k.sb("posi", [P, T], 123, I32)
    k.ang = k.sb("ang", [P, T], 125)
    k.rtmp = k.sb("rtmp", [P, T], 127)
    k.rtmp2 = k.sb("rtmp2", [P, T], 129)
    k.zr = k.sb("zr", [P, NQ, CH + 1, GH], 157)
    k.zn = k.sb("zn", [P, NQ, CH + 1, GH], 166)
    k.xr = k.sb("xr", [P, NQ, CH, GH], 175)
    k.xi = k.sb("xi", [P, NQ, CH, GH], 183)
    k.br = k.sb("br", [P, NQ, GH], 191)
    k.bi = k.sb("bi", [P, NQ, GH], 192)
    k.sv = k.sb("sv", [P, 24, NQ], 193)
    k.apr = k.sb("apr", [P, 9, NQ], 194.5)
    k.api = k.sb("api", [P, 9, NQ], 195.25)
    k.c_tok = k.sb("c_tok", [P, 2, SK, 2, NS], 196)
    k.dtmp = k.sb("dtmp", [P, 2, NQ, GH], 200)
    k.ptmp = k.sb("ptmp", [P, 2, NQ, GH], 202)


def one_plus(v, k, step, parts):
    for part in parts:
        at = k.modc[:, part * DK:(part + 1) * DK]
        step(v.tensor_scalar(at, at, 1.0, None, ALU.add))


def condition(nc, io, k, ps):
    k.s_rows, k.s_x, k.s_s5in, k.s_crep, k.s_ropein, k.s_win1 = k.sems("s_rows s_x s_s5in s_crep s_ropein s_win1")
    k.s_win2, k.s_win3, k.s_ident, k.s_tab, k.s_ldt, k.ldt_wide = k.sems("s_win2 s_win3 s_ident s_tab s_ldt ldt_wide")
    k.cols_copied, k.modrow_evac, k.mod_acc_ready, k.mod_tail = k.sems("cols_copied modrow_evac mod_acc_ready mod_tail")
    wa = [k.sem(f"w_ada_in{i}") for i in range(3)]
    k.seq_out, k.seq_evac, k.rows_T, k.ccol_ready, k.cols_ready, k.mod_mm = k.sems("seq_out seq_evac rows_T ccol_ready cols_ready mod_mm")
    k.mod_head, k.ht_ready, k.w_kr_ready, k.dt_ready, k.lrd_ready, k.mag_ready = k.sems("mod_head ht_ready w_kr_ready dt_ready lrd_ready mag_ready")
    k.red_ready, k.sin_ready, k.rope_red, k.rope_sin, k.bb_ready = k.sems("red_ready sin_ready rope_red rope_sin bb_ready")

    def row_view(name, m):
        a = io[name]
        return bass.AP(a.tensor, a.offset, [[P, m], [1, P]])

    k.s_wuq, k.s_wukv = k.sems("s_wuq s_wukv")
    w_ada = io["w_ada"][0].rearrange("(kt p) n -> p kt n", p=P)
    w_in = io["w_in"][0].rearrange("(kt p) n -> p kt n", p=P)

    @k.block.sync
    def _(sp):
        for name, m in ROWS:
            at = ROW_AT[name]
            sp.dma_start(k.rows[at:at + m, :], row_view(name, m)).then_inc(k.s_rows, 16)
        sp.dma_start(k.x_tok[:, :, :], io["x"][0].rearrange("(t p) d -> p t d", p=P)).then_inc(k.s_x, 16)
        for j in range(12):
            if j == 3:
                sp.dma_start(k.w_in[:, :, S5W + QL:D_IN], w_in[:, :, S5W + QL:D_IN]).then_inc(k.s_win1, 16)
            elif j == 4:
                for s, (a, b) in zip((k.s_win2, k.s_win3), ((S5W, S5W + QL), (0, S5W))):
                    sp.dma_start(k.w_in[:, :, a:b], w_in[:, :, a:b]).then_inc(s, 16)
            if j >= 3:
                sp.wait_ge(k.mod_mm, j - 2) if j < 7 else sp.wait_ge(k.mod_acc_ready, j - 6)
            sp.dma_start(k.w_ada[:, j % 3], w_ada[:, :, j * 512:(j + 1) * 512]).then_inc(wa[j % 3], 16)
        w_uq = io["mla_w_uq"][0].rearrange("(kt p) (h c) -> p kt h c", p=P, h=HEADS)
        w_ukv = io["mla_w_ukv"][0].rearrange("(kt p) (h c) -> p kt h c", p=P, h=HEADS)
        sp.wait_ge(k.mod_acc_ready, 6)
        for kt in range(QK):
            sp.dma_start(k.w_qr[:, kt], w_uq[:, kt, :, NOPE:]).then_inc(k.s_wuq, 16)
            sp.dma_start(k.w_qn[:, kt], w_uq[:, kt, :, 0:NOPE]).then_inc(k.s_wuq, 16)
        sp.wait_ge(k.mod_acc_ready, 7)
        for kt in range(KK):
            sp.dma_start(k.w_kn[:, kt], w_ukv[:, kt, :, 0:NOPE]).then_inc(k.s_wukv, 16)
            sp.dma_start(k.w_v[:, kt], w_ukv[:, kt, :, NOPE:]).then_inc(k.s_wukv, 16)

    names = "dt lrd mag th kk rs rc sn cs den rden nr t1 t2 cr ci".split()
    sv = {n: k.sv[:, i, :] for i, n in enumerate(names)}
    sv["lre"] = k.cols[:, ROW_AT["s5_lambda_re"]:ROW_AT["s5_lambda_re"] + NQ]
    sv["lim"] = k.cols[:, ROW_AT["s5_lambda_im"]:ROW_AT["s5_lambda_im"] + NQ]

    dsts = ([k.krT[:, i, :] for i in range(2)] + [k.ckvT[:, i, :] for i in range(KK)] + [k.cqT[:, i, :] for i in range(QK)]
            + [k.uT[:, m] for m in range(SK)])

    @k.block.scalar
    def _(act):
        act.dma_start(k.ldt2[:, :], io["s5_log_dt"][0].rearrange("(q two) -> q two", two=2)).then_inc(k.s_ldt, 16)
        for g2 in range(2):
            half = slice(g2 * NS, (g2 + 1) * NS)
            for dst, name in ((k.br, "s5_b_re"), (k.bi, "s5_b_im")):
                act.dma_start(dst[half, :, :], io[name][0].rearrange("(q two) p h -> two p q h", two=2)[g2]).then_inc(k.s_s5in, 16)
        po = io["positions"]
        act.dma_start(k.posi[:, :], bass.AP(po.tensor, po.offset, [[0, P], [1, T]])).then_inc(k.s_ropein, 16)
        act.dma_start(k.consts[:, :], io["rope_rows"]).then_inc(k.s_ropein, 16)
        for part, name in enumerate(("s5_c_re", "s5_c_im")):
            src = io[name][0].rearrange("g h p -> (g h) p").rearrange("(m r) p -> r m p", r=P)
            for dup in range(2):
                act.dma_start(k.c_tok[:, part, :, dup, :], src).then_inc(k.s_crep, 16)
        act.wait_ge(k.cols_copied, 1)
        nc.scalar.activation(sv["dt"], k.cols[:, NROWS:NROWS + NQ], ACT.Exp).then_inc(k.dt_ready, 1)
        act.wait_ge(k.lrd_ready, 1)
        nc.scalar.activation(sv["mag"], sv["lrd"], ACT.Exp).then_inc(k.mag_ready, 1)
        act.wait_ge(k.red_ready, 1)
        nc.scalar.activation(sv["sn"], sv["rs"], ACT.Sin)
        nc.scalar.activation(sv["cs"], sv["rc"], ACT.Sin).then_inc(k.sin_ready, 1)
        act.wait_ge(k.rope_red, 1)
        nc.scalar.activation(k.rsin[:, :], k.ang[:, :], ACT.Sin)
        nc.scalar.activation(k.rcos[:, :], k.rtmp[:, :], ACT.Sin).then_inc(k.rope_sin, 1)
        nc.scalar.activation(k.ccol[:, :], k.cols[:, 0:DK], ACT.Silu).then_inc(k.ccol_ready, 1)
        for part, dst, sign in ((0, k.zr, 1.0), (1, k.zn, -1.0)):
            act.wait_ge(k.seq_out, part + 1)
            src = ps[:, 1 + part, :].rearrange("p (q two h) -> p q two h", two=2, h=GH)
            for g2 in range(2):
                half = slice(g2 * NS, (g2 + 1) * NS)
                ins = nc.scalar.activation(dst[half, :, 0, :], src[half, :, g2, :], ACT.Copy, scale=sign)
            ins.then_inc(k.seq_evac, 1)
        for kt in range(DK):
            n = 2 + kt
            act.wait_ge(k.seq_out, n + 1)
            nc.scalar.activation(k.hT[:, kt, :], ps[:, 1 + n % 7, :], ACT.Copy).then_inc(k.seq_evac, 1)
        for j in range(4):
            act.wait_ge(k.mod_mm, j + 1)
            nc.scalar.activation(k.modrow[:, j * 512:(j + 1) * 512], ps[0:1, 0, :], ACT.Copy).then_inc(k.modrow_evac, 1)
        for i, dst in enumerate(dsts):
            n = 10 + i
            act.wait_ge(k.seq_out, n + 1)
            src = ps[:, 1 + n % 7, :]
            if i >= 7:
                src = src.rearrange("p (c s) -> p s c", s=CH)
            elif i == 0:
                act.wait_ge(k.cols_ready, 1)
            nc.scalar.activation(dst, src, ACT.Copy).then_inc(k.seq_evac, 1)

    @k.block.gpsimd
    def _(pool):
        nc.gpsimd.memset(k.ident[:, :], 0.0).then_inc(k.s_ident, 1)
        nc.gpsimd.memset(k.negrow[:, :], 0.0).then_inc(k.s_ident, 1)
        nc.gpsimd.memset(k.ones[:, :], 1.0)
        nc.gpsimd.memset(k.onerow[:, :], 1.0)
        nc.gpsimd.memset(k.eps[:, 0:1], EPS)
        nc.gpsimd.memset(k.eps[:, 1:2], EPS / SCALE ** 2).then_inc(k.s_ident, 1)
        pool.wait_ge(k.s_ident, 3)
        nc.gpsimd.memset(k.negrow[:, 0:P // 2], MASKED)
        nc.gpsimd.affine_select(out=k.ident[:, :], in_=k.ident[:, :], compare_op=ALU.not_equal, fill=1.0, base=0,
                                pattern=[[-1, P]], channel_multiplier=1).then_inc(k.s_tab, 1)
        pool.wait_ge(k.s_win1, 16)
        src = k.w_in[:, :, D_IN - ROPE:D_IN]
        hr = ROPE // 2
        for r in range(4):
            nc.gpsimd.tensor_copy(k.w_kr[:, :, 0, r, :], src)
            nc.gpsimd.tensor_copy(k.w_kr[:, :, 1, r, 0:hr], src[:, :, hr:ROPE])
            ins = nc.gpsimd.tensor_copy(k.w_kr[:, :, 1, r, hr:ROPE], src[:, :, 0:hr])
        ins.then_inc(k.w_kr_ready, 1)
        step = k.pool_steps.on(pool)
        pool.wait_ge(k.bb_ready, 2)
        ar = k.apr[:, 0, :].unsqueeze(2).broadcast_to([P, NQ, GH])
        ai = k.api[:, 0, :].unsqueeze(2).broadcast_to([P, NQ, GH])
        for j in range(CH - 2, -1, -1):
            r0, i0, r1, i1 = k.xr[:, :, j + 1], k.xi[:, :, j + 1], k.xr[:, :, j], k.xi[:, :, j]
            nc.gpsimd.tensor_tensor(r1, r0, ar, ALU.mult)
            nc.gpsimd.tensor_tensor(k.ptmp[:, 0], i0, ai, ALU.mult)
            nc.gpsimd.tensor_tensor(i1, r0, ai, ALU.mult)
            step(nc.gpsimd.tensor_tensor(k.ptmp[:, 1], i0, ar, ALU.mult))
            nc.gpsimd.tensor_tensor(r1, r1, k.ptmp[:, 0], ALU.subtract)
            step(nc.gpsimd.tensor_tensor(i1, i1, k.ptmp[:, 1], ALU.add))

    @k.block.vector
    def _(dve):
        step = k.dve_steps.on(dve)
        v = nc.vector
        tt = v.tensor_tensor

        def reduce_angle(x, r_sin, r_cos, whole, done):
            step(v.tensor_scalar(whole, x, 1.0 / TWO_PI, ROUND, ALU.mult, ALU.add))
            step(v.tensor_scalar(whole, whole, -ROUND, None, ALU.add))
            for part in (PI_1, PI_2, PI_3):
                step(v.scalar_tensor_tensor(r_sin, whole, -part, x if part == PI_1 else r_sin, ALU.mult, ALU.add))
            step(v.tensor_scalar(whole, r_sin, np.pi / 2, -TWO_PI, ALU.is_gt, ALU.mult))
            step(v.scalar_tensor_tensor(r_cos, r_sin, np.pi / 2, whole, ALU.add, ALU.add))
            v.tensor_scalar(r_cos, r_cos, SIN_MAX, -SIN_MAX, ALU.min, ALU.max)
            step.tell(v.tensor_scalar(r_sin, r_sin, SIN_MAX, -SIN_MAX, ALU.min, ALU.max), done)

        dve.wait_ge(k.s_ldt, 16)
        v.tensor_copy(k.ldt_row[:, :, :], k.ldt2[:, :].unsqueeze(2).broadcast_to([NQ, 2, NS])).then_inc(k.ldt_wide, 1)
        dve.wait_ge(k.rows_T, 1)
        step.tell(v.tensor_copy(k.cols[:, :], ps[:, 0, 0:NROWS + NQ]), k.cols_copied)
        dve.wait_ge(k.dt_ready, 1)
        tt(sv["lrd"], sv["lre"], sv["dt"], ALU.mult).then_inc(k.lrd_ready, 1)
        step(tt(sv["th"], sv["lim"], sv["dt"], ALU.mult))
        reduce_angle(sv["th"], sv["rs"], sv["rc"], sv["kk"], k.red_ready)
        dve.wait_ge(k.s_s5in, 64)
        tt(sv["den"], sv["lre"], sv["lre"], ALU.mult)
        step(tt(sv["t1"], sv["lim"], sv["lim"], ALU.mult))
        step(tt(sv["den"], sv["den"], sv["t1"], ALU.add))
        step(v.reciprocal(sv["rden"], sv["den"]))
        dve.wait_ge(k.s_ropein, 32)
        step(v.tensor_copy(k.rtmp2[:, :], k.posi[:, :]))
        step(v.tensor_scalar(k.rtmp2[:, :], k.rtmp2[:, :], k.consts[:, 0:1], None, ALU.mult))
        reduce_angle(k.rtmp2[:, :], k.ang[:, :], k.rtmp[:, :], k.posi[:, :].bitcast(F32), k.rope_red)
        dve.wait_ge(k.sin_ready, 1)
        dve.wait_ge(k.mag_ready, 1)
        are, aim = k.apr[:, 0, :], k.api[:, 0, :]
        tt(are, sv["mag"], sv["cs"], ALU.mult)
        step(tt(aim, sv["mag"], sv["sn"], ALU.mult))
        step(v.tensor_scalar(sv["nr"], are, -1.0, None, ALU.add))
        for dst, x1, x2, y1, y2, op in (("cr", sv["nr"], sv["lre"], aim, sv["lim"], ALU.add),
                                        ("ci", aim, sv["lre"], sv["nr"], sv["lim"], ALU.subtract)):
            tt(sv["t1"], x1, x2, ALU.mult)
            step(tt(sv["t2"], y1, y2, ALU.mult))
            step(tt(sv["t1"], sv["t1"], sv["t2"], op))
            step(tt(sv[dst], sv["t1"], sv["rden"], ALU.mult))
        cr = sv["cr"].unsqueeze(2).broadcast_to([P, NQ, GH])
        ci = sv["ci"].unsqueeze(2).broadcast_to([P, NQ, GH])
        for dst, m1, m2, op in ((k.xr, cr, ci, ALU.subtract), (k.xi, ci, cr, ALU.add)):
            tt(k.dtmp[:, 0], k.br[:, :, :], m1, ALU.mult)
            step(tt(k.dtmp[:, 1], k.bi[:, :, :], m2, ALU.mult))
            step.tell(tt(dst[:, :, CH - 1, :], k.dtmp[:, 0], k.dtmp[:, 1], op), k.bb_ready, 1 + (dst is k.xi))
        dve.wait_ge(k.rope_sin, 1)
        v.tensor_scalar(k.rsin[:, :], k.rsin[:, :], k.consts[:, 1:2], None, ALU.mult).then_inc(k.cols_ready, 1)
        b_ada = k.cols[:, ROW_AT["b_ada"]:ROW_AT["b_ada"] + NMOD]

        dve.wait_ge(k.mod_head, 1)
        step(tt(k.modc[:, 0:16], ps[:, 0, 0:16], b_ada[:, 0:16], ALU.add))
        one_plus(v, k, step, (1,))
        for kt in range(DK):
            dve.wait_ge(k.seq_evac, 3 + kt)
            ins = v.tensor_scalar(k.hT[:, kt, :], k.hT[:, kt, :], k.modc[:, DK + kt:DK + kt + 1], k.modc[:, kt:kt + 1],
                                  ALU.mult, ALU.add)
        ins.then_inc(k.ht_ready, 1)
        for i in range(8):
            r, m, r2, m2 = k.apr[:, i], k.api[:, i], k.apr[:, i + 1], k.api[:, i + 1]
            tt(sv["t1"], r, r, ALU.mult)
            tt(sv["t2"], m, m, ALU.mult)
            step(tt(m2, r, m, ALU.mult))
            tt(r2, sv["t1"], sv["t2"], ALU.subtract)
            step(v.tensor_scalar(m2, m2, 2.0, None, ALU.mult))
        dve.wait_ge(k.seq_evac, 2)
        ar = are.unsqueeze(2).broadcast_to([P, NQ, GH])
        ai = aim.unsqueeze(2).broadcast_to([P, NQ, GH])
        for j in range(CH):
            r0, n0, r1, n1 = k.zr[:, :, j], k.zn[:, :, j], k.zr[:, :, j + 1], k.zn[:, :, j + 1]
            tt(r1, r0, ar, ALU.mult)
            tt(k.dtmp[:, 0], n0, ai, ALU.mult)
            tt(n1, n0, ar, ALU.mult)
            step(tt(k.dtmp[:, 1], r0, ai, ALU.mult))
            tt(r1, r1, k.dtmp[:, 0], ALU.add)
            step(tt(n1, n1, k.dtmp[:, 1], ALU.subtract))
        for j in range(4, 12):
            dve.wait_ge(wa[j % 3], 16 * (j // 3 + 1))
            acc = k.mod_acc[:, (j - 4) * 512:(j - 3) * 512]
            for kt in range(DK):
                w, c = k.w_ada[:, j % 3, kt, :], k.ccol[:, kt:kt + 1]
                ins = v.tensor_scalar(acc, w, c, None, ALU.mult) if kt == 0 else \
                    v.scalar_tensor_tensor(acc, w, c, acc, ALU.mult, ALU.add)
                if kt < DK - 1:
                    step(ins)
                else:
                    ins.then_inc(k.mod_acc_ready, 1)

    @k.block.tensor
    def _(pe):
        mm = nc.tensor.matmul
        pe.wait_ge(k.s_tab, 1)
        pe.wait_ge(k.s_rows, 16 * len(ROWS))
        nc.tensor.transpose(ps[:, 0, 0:NROWS], k.rows[:, :], k.ident[0:NROWS, 0:NROWS])
        pe.wait_ge(k.ldt_wide, 1)
        nc.tensor.transpose(ps[:, 0, NROWS:NROWS + NQ], k.ldt_row[:, :, :].rearrange("q a b -> q (a b)"),
                            k.ident[0:NQ, 0:NQ]).then_inc(k.rows_T, 1)
        pe.wait_ge(k.s_crep, 64)
        for part in range(2):
            for m in range(SK):
                ins = nc.tensor.transpose(ps[:, 1 + part, m * P:(m + 1) * P],
                                          k.c_tok[:, part, m].rearrange("p a b -> p (a b)"), k.ident[:, :])
            ins.then_inc(k.seq_out, 1)
        pe.wait_ge(k.s_x, 16)
        for kt in range(DK):
            n = 2 + kt
            if n >= 7:
                pe.wait_ge(k.seq_evac, n - 6)
            for t in range(TT):
                ins = nc.tensor.transpose(ps[:, 1 + n % 7, t * P:(t + 1) * P], k.x_tok[:, t, kt * P:(kt + 1) * P],
                                          k.ident[:, :])
            ins.then_inc(k.seq_out, 1)
        pe.wait_ge(k.ccol_ready, 1)

        for j in range(4):
            pe.wait_ge(wa[j % 3], 16 * (j // 3 + 1))
            if j >= 1:
                pe.wait_ge(k.modrow_evac, j)
            for kt in range(DK):
                ins = mm(ps[0:1, 0, :], k.ccol[:, kt:kt + 1], k.w_ada[:, j % 3, kt, :],
                         start=(kt == 0), stop=(kt == DK - 1))
            ins.then_inc(k.mod_mm, 1)
        pe.wait_ge(k.modrow_evac, 4)
        for m in range(16):
            ins = mm(ps[:, 0, m:m + 1], k.modrow[:, m * P:(m + 1) * P], k.onerow[:, 0:1], start=True, stop=True)
        ins.then_inc(k.mod_head, 1)
        pe.wait_ge(k.ht_ready, 1)
        stat = ([k.w_kr[:, :, i].rearrange("p kt a b -> p kt (a b)") for i in range(2)]
                + [k.w_in[:, :, S5W + QL + i * P:S5W + QL + (i + 1) * P] for i in range(KK)]
                + [k.w_in[:, :, S5W + i * P:S5W + (i + 1) * P] for i in range(QK)]
                + [k.w_in[:, :, i * P:(i + 1) * P] for i in range(SK)])
        for i, w in enumerate(stat):
            n = 10 + i
            if i == 0:
                pe.wait_ge(k.w_kr_ready, 1)
            elif i == 4:
                pe.wait_ge(k.s_win2, 16)
            elif i == 7:
                pe.wait_ge(k.s_win3, 16)
            pe.wait_ge(k.seq_evac, n - 6)
            for kt in range(DK):
                ins = mm(ps[:, 1 + n % 7, :], w[:, kt, :], k.hT[:, kt, :], start=(kt == 0), stop=(kt == DK - 1))
            ins.then_inc(k.seq_out, 1)


def place_attention(k):
    k.xtr = k.sb("xtr", [P, NQ, P], 22)
    k.xti = k.sb("xti", [P, NQ, P], 30)
    k.kt32 = k.sb("kt32", [2 * GH, NQ, CH * GH], 38)
    k.kpe = k.sb("kpe", [P, 4, T], 46)
    k.m1 = k.sb("m1", [P, GROUPS, CH * GH], 54)
    k.ut = k.sb("ut", [P, GROUPS, NC], 70)
    k.w_qn = k.sb("w_qn", [P, QK, HEADS, NOPE], 78)
    k.w_qr = k.sb("w_qr", [P, QK, HEADS, ROPE], 84)
    k.w_sw = k.sb("w_sw", [P, QK, HEADS, ROPE], 87)
    k.w_kn = k.sb("w_kn", [P, KK, HEADS, NOPE], 90)
    k.w_v = k.sb("w_v", [P, KK, HEADS, VD], 94)
    k.ir = k.sb("ir", [P, NQ, NC + 1], 98)
    k.ii = k.sb("ii", [P, NQ, NC + 1], 102.125)
    k.sq = k.sb("sq", [P, QK + KK, T], 98)
    k.cqn = k.sb("cqn", [P, QK, T], 109)
    k.ckvn = k.sb("ckvn", [P, KK, T], 115)
    k.rq = k.sb("rq", [P, T], 119)
    k.rkv = k.sb("rkv", [P, T], 121)
    k.qn = k.sb("qn", [P, HEADS // 2, T], 149)
    k.qr = k.sb("qr", [P, HEADS // 4, T], 196)
    k.kn = k.sb("kn", [P, HEADS, T], 6)
    k.v = k.sb("v", [P, TT, HEADS, VD], 131)
    k.bpad = k.sb("bpad", [P, 2, NQ, 2, GH], 200)
    k.ropet = k.sb("ropet", [P, T], 204)
    k.sct = k.sb("sct", [P, 4, NQ, NC], 22)
    k.prob = k.sb("prob", [P, 3, T], 78)
    k.probT = k.sb("probT", [P, 2, TT, P], 84)
    k.y_mla = k.sb("y_mla", [P, TT, HEADS * VD], 107)
    k.nmax = k.sb("nmax", [P, TT * HEADS], 115)
    k.rsum = k.sb("rsum", [P, TT * HEADS], 115.125)
    k.rinv = k.sb("rinv", [P, TT * HEADS], 115.25)
    k.spad = k.sb("spad", [P, 2, NQ, 2, NC], 175)


def project(nc, io, k, ps):
    k.s_uout, k.s_m1, k.wsw_ready, k.sq_ready = k.sems("s_uout s_m1 wsw_ready sq_ready")
    k.a2_out, k.a2_evac, k.d2_out, k.d2_evac, k.cqn_ready, k.ckvn_ready = k.sems("a2_out a2_evac d2_out d2_evac cqn_ready ckvn_ready")
    k.bpad_zero, k.bpad_ready, k.m1_zero, k.kn_zero, k.kpe_zero = k.sems("bpad_zero bpad_ready m1_zero kn_zero kpe_zero")
    s_ut = k.sem("s_ut")
    H2 = ROPE // 2
    mm = nc.tensor.matmul
    u_scr = k.u_scr

    @k.block.sync
    def _(sp):
        sp.dma_start(u_scr.rearrange("(m p) t -> p m t", p=P),
                     k.uT[:, :, :, :].rearrange("p m s c -> p m (s c)")).then_inc(k.s_uout, 16)
        sp.wait_ge(k.s_uout, 16)
        for s in range(CH):
            sp.dma_start(k.ut[s * GH:(s + 1) * GH, :, :],
                         u_scr.rearrange("(g h) (s c) -> h g s c", h=GH, s=CH)[:, :, s, :]).then_inc(s_ut, 16)
        sp.wait_ge(k.d2_evac, 8)
        sp.wait_ge(k.m1_zero, 1)
        m1 = k.m1[:, :, :].rearrange("p (q two) n -> p q two n", two=2)
        for s in range(CH):
            for g2 in range(2):
                sp.dma_start(m1[s * GH:(s + 1) * GH, :, g2, s * GH:],
                             k.kt32[g2 * GH:(g2 + 1) * GH, :, 0:(CH - s) * GH]).then_inc(k.s_m1, 16)
        sp.wait_ge(k.s_m1, 16 * 2 * CH)

    @k.block.gpsimd
    def _(pool):
        nc.gpsimd.memset(k.bpad[:, :, :, :, :], 0.0).then_inc(k.bpad_zero, 1)
        pool.wait_ge(k.s_wuq, 16 * 2 * QK)
        nc.gpsimd.tensor_copy(k.w_sw[:, :, :, 0:H2], k.w_qr[:, :, :, H2:])
        nc.gpsimd.tensor_copy(k.w_sw[:, :, :, H2:], k.w_qr[:, :, :, 0:H2]).then_inc(k.wsw_ready, 1)
        pool.wait_ge(k.mod_tail, 1)
        nc.gpsimd.memset(k.kn[:, :, :], 0.0).then_inc(k.kn_zero, 1)
        nc.gpsimd.memset(k.kpe[:, :, :], 0.0).then_inc(k.kpe_zero, 1)
        nc.gpsimd.memset(k.m1[:, :, :], 0.0).then_inc(k.m1_zero, 1)

    @k.block.scalar
    def _(act):
        for i in range(QK + KK):
            ins = nc.scalar.activation(k.sq[:, i], k.cqT[:, i] if i < QK else k.ckvT[:, i - QK], ACT.Square)
        ins.then_inc(k.sq_ready, 1)
        act.wait_ge(k.bpad_zero, 1)
        for part, x in enumerate((k.xr, k.xi)):
            for g2 in range(2):
                half = slice(g2 * NS, (g2 + 1) * NS)
                ins = nc.scalar.activation(k.bpad[half, part, :, g2, :], x[half, :, CH - 1, :], ACT.Copy)
        ins.then_inc(k.bpad_ready, 1)
        n = 0

        def evac(pairs, n):
            act.wait_ge(k.a2_out, n + 1)
            for dst, src in pairs:
                ins = nc.scalar.activation(dst, src, ACT.Copy)
            ins.then_inc(k.a2_evac, 1)

        for dst in (k.xtr, k.xti):
            for b in range(4):
                evac([(dst[:, 4 * b:4 * b + 4].rearrange("p q n -> p (q n)"), ps[:, n % 4])], n)
                n += 1
        act.wait_ge(k.a2_out, n + 1)
        nc.scalar.activation(k.rq[:, :], ps[:, 0], ACT.Sqrt, scale=1.0 / (QL * SCALE ** 2), bias=k.eps[:, 1:2]).then_inc(k.a2_evac, 1)
        act.wait_ge(k.a2_out, n + 2)
        nc.scalar.activation(k.rkv[:, :], ps[:, 1], ACT.Sqrt, scale=1.0 / KVL, bias=k.eps[:, 0:1]).then_inc(k.a2_evac, 1)
        n += 2
        for i in range(4):
            evac([(k.qn[:, i], ps[:, n % 4])], n)
            n += 1
        act.wait_ge(k.kn_zero, 1)
        for i in range(4):
            evac([(k.kn[0:NOPE, 2 * i], ps[0:NOPE, n % 4]), (k.kn[NOPE:P, 2 * i + 1], ps[NOPE:P, n % 4])], n)
            n += 1
        for i in range(TT):
            evac([(k.v[:, i].rearrange("p h c -> p (h c)"), ps[:, n % 4])], n)
            n += 1

    @k.block.vector
    def _(dve):
        step = k.dve_steps.on(dve)
        v = nc.vector
        tt = v.tensor_tensor
        qcol = k.cols[:, ROW_AT["mla_q_norm"]:]
        kcol = k.cols[:, ROW_AT["mla_kv_norm"]:]
        dve.wait_ge(k.a2_evac, 9)
        step(v.reciprocal(k.rq[:, :], k.rq[:, :]))
        for i in range(QK):
            ins = v.scalar_tensor_tensor(k.cqn[:, i], k.cqT[:, i], qcol[:, i:i + 1], k.rq[:, :], ALU.mult, ALU.mult)
        ins.then_inc(k.cqn_ready, 1)
        dve.wait_ge(k.a2_evac, 10)
        step(v.reciprocal(k.rkv[:, :], k.rkv[:, :]))
        for i in range(KK):
            ins = v.scalar_tensor_tensor(k.ckvn[:, i], k.ckvT[:, i], kcol[:, i:i + 1], k.rkv[:, :], ALU.mult, ALU.mult)
        ins.then_inc(k.ckvn_ready, 1)
        dve.wait_ge(k.mod_tail, 1)
        at = ROW_AT["b_ada"]
        step(tt(k.modc[:, 16:NMOD], ps[:, 7, 16:NMOD], k.cols[:, at + 16:at + NMOD], ALU.add))
        one_plus(v, k, step, (2, 4, 5))
        for i in range(2):
            dve.wait_ge(k.d2_out, 2 * i + 2)
            tt(k.ropet[:, :], ps[:, 4 + 2 * i + 1], k.rsin[:, :], ALU.mult)
            step(tt(k.qr[:, i], ps[:, 4 + 2 * i], k.rcos[:, :], ALU.mult))
            step.tell(tt(k.qr[:, i], k.qr[:, i], k.ropet[:, :], ALU.add), k.d2_evac, 2 * i + 2, by=2)
        for b in range(4):
            dve.wait_ge(k.d2_out, 4 + b + 1)
            v.tensor_copy(k.kt32[:, 4 * b:4 * b + 4].rearrange("p q n -> p (q n)"), ps[0:2 * GH, 4 + b]).then_inc(k.d2_evac, 1)
        tt(k.ropet[:, :], k.krT[:, 1], k.rsin[:, :], ALU.mult)
        step(tt(k.krT[:, 0], k.krT[:, 0], k.rcos[:, :], ALU.mult))
        dve.wait_ge(k.kpe_zero, 1)
        for r in range(4):
            rows = slice(r * ROPE, (r + 1) * ROPE)
            tt(k.kpe[rows, r], k.krT[rows, 0], k.ropet[rows, :], ALU.add)
        v.memset(k.ir[:, :, 0:1], 0.0)
        v.memset(k.ii[:, :, 0:1], 0.0)
        for j in range(8):
            part, b = j // 4, j % 4
            dve.wait_ge(k.d2_out, 8 + j + 1)
            src = ps[:, 4 + b].rearrange("p (q two c) -> p q two c", two=2, c=NC)
            for g2 in range(2):
                half = slice(g2 * NS, (g2 + 1) * NS)
                ins = v.tensor_copy((k.ir, k.ii)[part][half, 4 * b:4 * b + 4, 1:], src[half, :, g2, :])
            ins.then_inc(k.d2_evac, 1)

    @k.block.tensor
    def _(pe):
        n = 0
        for src in (k.xr, k.xi):
            for b in range(4):
                if n >= 4:
                    pe.wait_ge(k.a2_evac, n - 3)
                for q in range(4):
                    ins = nc.tensor.transpose(ps[:, n % 4, q * P:(q + 1) * P],
                                              src[:, 4 * b + q].rearrange("p s h -> p (s h)"), k.ident[:, :])
                ins.then_inc(k.a2_out, 1)
                n += 1
        pe.wait_ge(k.sq_ready, 1)
        for tiles in (range(QK), range(QK, QK + KK)):
            pe.wait_ge(k.a2_evac, n - 3)
            for i in tiles:
                ins = mm(ps[:, n % 4], k.ones[:, :], k.sq[:, i], start=(i == tiles[0]), stop=(i == tiles[-1]))
            ins.then_inc(k.a2_out, 1)
            n += 1
        for m in range(16, NMOD):
            ins = mm(ps[:, 7, m:m + 1], k.mod_acc[:, (m - 16) * P:(m - 15) * P], k.ones[:, 0:1], start=True, stop=True)
        ins.then_inc(k.mod_tail, 1)
        pe.wait_ge(k.cqn_ready, 1)
        pe.wait_ge(k.wsw_ready, 1)
        for i in range(2):
            for sw in range(2):
                if i == 1 and sw == 1:
                    pe.wait_ge(k.d2_evac, 2)
                for kt in range(QK):
                    w = (k.w_sw if sw else k.w_qr)[:, kt, 4 * i:4 * i + 4, :].rearrange("p h c -> p (h c)")
                    ins = mm(ps[:, 4 + 2 * i + sw], w, k.cqn[:, kt], start=(kt == 0), stop=(kt == QK - 1))
                ins.then_inc(k.d2_out, 1)
        for i in range(4):
            pe.wait_ge(k.a2_evac, n - 3)
            for kt in range(QK):
                ins = mm(ps[:, n % 4], k.w_qn[:, kt, 2 * i:2 * i + 2].rearrange("p h c -> p (h c)"), k.cqn[:, kt],
                         start=(kt == 0), stop=(kt == QK - 1))
            ins.then_inc(k.a2_out, 1)
            n += 1
        pe.wait_ge(k.bpad_ready, 1)
        for b in range(4):
            pe.wait_ge(k.d2_evac, 2 * (b // 2) + 2)
            for q in range(4 * b, 4 * b + 4):
                out = ps[0:2 * GH, 4 + b, (q % 4) * P:(q % 4 + 1) * P]
                for part, z in enumerate((k.zr, k.zn)):
                    ins = mm(out, k.bpad[:, part, q].rearrange("p a b -> p (a b)"),
                             z[:, q, 0:CH].rearrange("p s h -> p (s h)"), start=(part == 0), stop=(part == 1))
            ins.then_inc(k.d2_out, 1)
        pe.wait_ge(k.s_wukv, 16 * 2 * KK)
        pe.wait_ge(k.ckvn_ready, 1)
        for i in range(4):
            pe.wait_ge(k.a2_evac, n - 3)
            for kt in range(KK):
                ins = mm(ps[:, n % 4], k.w_kn[:, kt, 2 * i:2 * i + 2].rearrange("p h c -> p (h c)"), k.ckvn[:, kt],
                         start=(kt == 0), stop=(kt == KK - 1))
            ins.then_inc(k.a2_out, 1)
            n += 1
        for i in range(TT):
            pe.wait_ge(k.a2_evac, n - 3)
            for kt in range(KK):
                ins = mm(ps[:, n % 4], k.ckvn[:, kt, i * P:(i + 1) * P], k.w_v[:, kt].rearrange("p h c -> p (h c)"),
                         start=(kt == 0), stop=(kt == KK - 1))
            ins.then_inc(k.a2_out, 1)
            n += 1
        pe.wait_ge(s_ut, 16 * CH)
        for j in range(8):
            part, b = j // 4, j % 4
            pe.wait_ge(k.d2_evac, 4 + j + 1)
            for q in range(4 * b, 4 * b + 4):
                ins = mm(ps[:, 4 + b, (q % 4) * P:(q % 4 + 1) * P], (k.xtr, k.xti)[part][:, q],
                         k.ut[:, 2 * q:2 * q + 2].rearrange("p a b -> p (a b)"), start=True, stop=True)
            ins.then_inc(k.d2_out, 1)


def attend(nc, io, k, ps):
    k.sc_out, k.pt_out, k.pv_out, k.nmax_ready, k.exp_done, k.pt_evac = k.sems("sc_out pt_out pv_out nmax_ready exp_done pt_evac")
    k.o_evac, k.sc_prod_d, k.sc_prod_p, k.sc_upd_d, k.sc_upd_p, k.spad_zero = k.sems("o_evac sc_prod_d sc_prod_p sc_upd_d sc_upd_p spad_zero")
    k.rinv_done, k.m3_ready = k.sems("rinv_done m3_ready")
    mm = nc.tensor.matmul
    jobs = [(qb, h) for qb in range(TT) for h in range(HEADS)]
    SCAN_AT = {2 + 5 * s + j: (s, j) for s in range(6) for j in range(4)}

    @k.block.tensor
    def _(pe):
        def scores(i):
            qb, h = jobs[i]
            n = (qb + 1) * P
            if i >= 3:
                pe.wait_ge(k.exp_done, i - 2)
            out = ps[:, i % 3, 0:n]
            mm(out, k.qn[:, h // 2, qb * P:n], k.kn[:, h, 0:n], start=True, stop=False)
            mm(out, k.qr[:, h // 4, qb * P:n], k.kpe[:, h % 4, 0:n], start=False, stop=False)
            mm(out[:, n - P // 2:n], k.negrow[0:1, :], k.onerow[0:1, :], start=False, stop=True).then_inc(k.sc_out, 1)

        def transposes(i):
            qb, h = jobs[i]
            pe.wait_ge(k.exp_done, i + 1)
            if i >= 2:
                pe.wait_ge(k.pt_evac, i - 1)
            for kb in range(qb + 1):
                ins = nc.tensor.transpose(ps[:, 3 + i % 2, kb * P:(kb + 1) * P], k.prob[:, i % 3, kb * P:(kb + 1) * P],
                                          k.ident[:, :])
            ins.then_inc(k.pt_out, 1)

        def values(i):
            qb, h = jobs[i]
            pe.wait_ge(k.pt_evac, i + 1)
            if h == 0 and qb >= 2:
                pe.wait_ge(k.o_evac, qb - 1)
            for kb in range(qb + 1):
                ins = mm(ps[:, 5 + qb % 2, h * VD:(h + 1) * VD], k.probT[:, i % 2, kb], k.v[:, kb, h, :],
                         start=(kb == 0), stop=(kb == qb))
            ins.then_inc(k.pv_out, 1)

        for i in range(len(jobs) + 2):
            if i < len(jobs):
                scores(i)
            if 1 <= i <= len(jobs):
                transposes(i - 1)
            if i >= 2:
                values(i - 2)

    @k.block.scalar
    def _(act):
        for i, (qb, h) in enumerate(jobs):
            n = (qb + 1) * P
            act.wait_ge(k.nmax_ready, i + 1)
            if i >= 3:
                act.wait_ge(k.pt_out, i - 2)
            nc.scalar.activation(k.prob[:, i % 3, 0:n], ps[:, i % 3, 0:n], ACT.Exp, bias=k.nmax[:, i:i + 1],
                                 accum_out=k.rsum[:, i:i + 1]).then_inc(k.exp_done, 1)
        act.wait_ge(k.sc_upd_d, 6)
        act.wait_ge(k.sc_upd_p, 12)
        act.wait_ge(k.spad_zero, 1)
        for part, x in enumerate((k.ir, k.ii)):
            for g2 in range(2):
                half = slice(g2 * NS, (g2 + 1) * NS)
                nc.scalar.activation(k.spad[half, part, :, g2, :], x[half, :, 0:NC], ACT.Copy)

    def multiplier(vec, c):
        return vec.unsqueeze(2).broadcast_to([P, NQ, c])

    @k.block.vector
    def _(dve):
        v = nc.vector
        tt = v.tensor_tensor

        def scan(s, part):
            sh = 1 << s
            w = NC - sh
            if part == 0:
                if s:
                    dve.wait_ge(k.sc_upd_d, s)
                    dve.wait_ge(k.sc_upd_p, 2 * s)
                tt(k.sct[:, 0, :, 0:w], k.ir[:, :, 1:1 + w], multiplier(k.apr[:, 3 + s], w), ALU.mult)
            elif part == 1:
                tt(k.sct[:, 1, :, 0:w], k.ii[:, :, 1:1 + w], multiplier(k.api[:, 3 + s], w), ALU.mult).then_inc(k.sc_prod_d, 1)
            elif part == 2:
                dve.wait_ge(k.sc_prod_d, s + 1)
                tt(k.sct[:, 0, :, 0:w], k.sct[:, 0, :, 0:w], k.sct[:, 1, :, 0:w], ALU.subtract).then_inc(k.m3_ready, 1)
            else:
                dve.wait_ge(k.m3_ready, s + 1)
                dve.wait_ge(k.sc_prod_p, s + 1)
                tt(k.ir[:, :, 1 + sh:], k.ir[:, :, 1 + sh:], k.sct[:, 0, :, 0:w], ALU.add).then_inc(k.sc_upd_d, 1)

        def evac_probs(i):
            qb, h = jobs[i]
            dve.wait_ge(k.pt_out, i + 1)
            if i >= 2:
                dve.wait_ge(k.pv_out, i - 1)
            n = (qb + 1) * P
            v.tensor_copy(k.probT[:, i % 2, 0:qb + 1].rearrange("p b n -> p (b n)"), ps[:, 3 + i % 2, 0:n]).then_inc(k.pt_evac, 1)

        def evac_out(qb):
            dve.wait_ge(k.exp_done, HEADS * (qb + 1))
            v.reciprocal(k.rinv[:, qb * HEADS:(qb + 1) * HEADS], k.rsum[:, qb * HEADS:(qb + 1) * HEADS]).then_inc(k.rinv_done, 1)
            dve.wait_ge(k.rinv_done, qb + 1)
            dve.wait_ge(k.pv_out, HEADS * (qb + 1))
            tt(k.y_mla[:, qb].rearrange("p (h c) -> p h c", c=VD), ps[:, 5 + qb % 2].rearrange("p (h c) -> p h c", c=VD),
               k.rinv[:, qb * HEADS:(qb + 1) * HEADS].unsqueeze(2).broadcast_to([P, HEADS, VD]), ALU.mult).then_inc(k.o_evac, 1)

        for i in range(len(jobs) + 2):
            if i < len(jobs):
                qb, h = jobs[i]
                dve.wait_ge(k.sc_out, i + 1)
                v.tensor_reduce(k.nmax[:, i:i + 1], ps[:, i % 3, 0:(qb + 1) * P], AXX, ALU.max, negate=True).then_inc(k.nmax_ready, 1)
            if 1 <= i <= len(jobs):
                evac_probs(i - 1)
            if i in SCAN_AT:
                scan(*SCAN_AT[i])
            if i >= 2 + HEADS and (i - 2) % HEADS == 0:
                evac_out((i - 2) // HEADS - 1)
        evac_out(TT - 1)

    @k.block.gpsimd
    def _(pool):
        tt = nc.gpsimd.tensor_tensor
        nc.gpsimd.memset(k.spad[:, :, :, :, :], 0.0).then_inc(k.spad_zero, 1)
        for s in range(6):
            sh = 1 << s
            w = NC - sh
            if s:
                pool.wait_ge(k.sc_upd_d, s)
                pool.wait_ge(k.sc_upd_p, 2 * s)
            tt(k.sct[:, 2, :, 0:w], k.ii[:, :, 1:1 + w], multiplier(k.apr[:, 3 + s], w), ALU.mult)
            tt(k.sct[:, 3, :, 0:w], k.ir[:, :, 1:1 + w], multiplier(k.api[:, 3 + s], w), ALU.mult).then_inc(k.sc_prod_p, 1)
            pool.wait_ge(k.sc_prod_p, s + 1)
            tt(k.sct[:, 2, :, 0:w], k.sct[:, 2, :, 0:w], k.sct[:, 3, :, 0:w], ALU.add).then_inc(k.sc_upd_p, 1)
            pool.wait_ge(k.sc_upd_p, 2 * s + 1)
            pool.wait_ge(k.sc_prod_d, s + 1)
            tt(k.ii[:, :, 1 + sh:], k.ii[:, :, 1 + sh:], k.sct[:, 2, :, 0:w], ALU.add).then_inc(k.sc_upd_p, 1)


def place_mix(k):
    k.w_glu = k.sb("w_glu", [P, SK, S5W], 6)
    k.sq5 = k.sb("sq5", [P, SK, T], 14)
    k.w_out = k.sb("w_out", [P, DK, D], 22)
    k.ln_g = k.sb("ln_g", [P, D], 54)
    k.ln_b = k.sb("ln_b", [P, D], 58)
    k.h2T = k.sb("h2T", [P, DK, T], 62)
    k.x_re = k.sb("x_re", [P, TT, D], 78)
    k.r5 = k.sb("r5", [P, T], 94)
    k.ssq = k.sb("ssq", [P, TT], 96)
    k.stats = k.sb("stats", [P, TT, 2, 6], 96.25)
    k.mv = k.sb("mv", [P, TT, 2], 96.5)
    k.rstd = k.sb("rstd", [P, TT], 96.625)
    k.yt = k.sb("yt", [P, GROUPS, NC], 98)
    k.gate = k.sb("gate", [P, D], 115)
    k.gcol = k.sb("gcol", [P, DK, P], 119)
    k.yT = k.sb("yT", [P, SK, CH, NC], 131)
    k.gT = k.sb("gT", [P, SK, T], 139)
    k.sig = k.sb("sig", [P, SK, T], 149)
    k.x1 = k.sb("x1", [P, TT, D], 160)
    k.y5n = k.sb("y5n", [P, SK, T], 191)
    k.ymT = k.sb("ymT", [P, SK, T], 199)


def load_keys(sp, io, k):
    for side, name in enumerate(("peer_keys1", "peer_keys2")):
        sp.dma_start(k.keys[:, side], io[name][0].rearrange("h k d -> k h d")).then_inc(k.s_keys, 16)


def load_w_q(sp, io, k, h):
    w = io["peer_w_query"][0].rearrange("(kt p) n -> p kt n", p=P)
    sp.dma_start(k.w_q[:, h % 4], w[:, :, h * 2 * PHALF:(h + 1) * 2 * PHALF]).then_inc(k.s_wq[h % 4], 16)


def mix(nc, io, k, ps):
    k.s_wglu, k.s_wout, k.s_xre, k.s_ln1, k.s_yout, k.s_yin = k.sems("s_wglu s_wout s_xre s_ln1 s_yout s_yin")
    k.s_x1out, k.y_out, k.y_evac, k.gate_out, k.gate_evac, k.gcol_ready = k.sems("s_x1out y_out y_evac gate_out gate_evac gcol_ready")
    k.ym_ready, k.ym_out, k.ym_evac, k.ssq_ready, k.mla_rt, k.d_done = k.sems("ym_ready ym_out ym_evac ssq_ready mla_rt d_done")
    k.gelu4_done, k.z_out, k.sig_done, k.y5_ready, k.sq5_ready, k.r5_out = k.sems("gelu4_done z_out sig_done y5_ready sq5_ready r5_out")
    k.r5_rt, k.y5n_ready, k.op_out, k.op_evac, k.rt1, k.ln_sq = k.sems("r5_rt y5n_ready op_out op_evac rt1 ln_sq")
    k.ln_gain, k.x1_ready, k.x1t_out = k.sems("ln_gain x1_ready x1t_out")
    k.s_keys = k.sem("s_keys")
    k.s_wq = [k.sem(f"s_wq{i}") for i in range(4)]
    mm = nc.tensor.matmul
    y_scr = k.y_scr
    EARLY = 3
    OB = (5, 6, 7, 0, 1, 2, 3, 4)

    @k.block.sync
    def _(sp):
        sp.dma_start(k.w_glu[:, :, :], io["s5_w_glu"][0].rearrange("(kt p) n -> p kt n", p=P)).then_inc(k.s_wglu, 16)
        w_out = io["w_out"][0].rearrange("(kt p) n -> p kt n", p=P)
        sp.dma_start(k.w_out[:, SK:], w_out[:, SK:]).then_inc(k.s_wout, 16)
        sp.wait_ge(k.y_evac, 4)
        for s in range(CH):
            sp.dma_start(y_scr.rearrange("(g h) (s c) -> h g s c", h=GH, s=CH)[:, :, s, :],
                         k.yt[s * GH:(s + 1) * GH, :, :]).then_inc(k.s_yout, 16)
        sp.wait_ge(k.s_yout, 16 * CH)
        sp.dma_start(k.yT[:, :, :, :].rearrange("p m s c -> p m (s c)"),
                     y_scr.rearrange("(m p) t -> p m t", p=P)).then_inc(k.s_yin, 16)
        sp.dma_start(k.w_out[:, :SK], w_out[:, :SK]).then_inc(k.s_wout, 16)
        sp.dma_start(k.x_re[:, :, :], io["x"][0].rearrange("(t p) d -> p t d", p=P)).then_inc(k.s_xre, 16)
        for name, dst in (("ln1_g", k.ln_g), ("ln1_b", k.ln_b)):
            a = io[name]
            sp.dma_start(dst[:, :], bass.AP(a.tensor, a.offset, [[0, P], [1, D]])).then_inc(k.s_ln1, 16)
        load_keys(sp, io, k)
        sp.wait_ge(k.ym_evac, 4)
        for h in range(2):
            load_w_q(sp, io, k, h)
        for t in range(TT):
            sp.wait_ge(k.x1_ready, t + 1)
            sp.dma_start(k.x1_scr[t * P:(t + 1) * P, :], k.x1[:, t, :]).then_inc(k.s_x1out, 16)

    @k.block.gpsimd
    def _(pool):
        nc.gpsimd.tensor_copy(k.gcol[:, :, :], k.modc[:, 2 * DK:3 * DK].unsqueeze(2).broadcast_to([P, DK, P])).then_inc(k.gcol_ready, 1)
        pool.wait_ge(k.s_ln1, 32)
        for t in range(TT):
            pool.wait_ge(k.ln_gain, t + 1)
            nc.gpsimd.tensor_tensor(k.x1[:, t], k.x1[:, t], k.ln_b[:, :], ALU.add).then_inc(k.x1_ready, 1)

    @k.block.scalar
    def _(act):
        gn = k.cols[:, ROW_AT["gn_mla"]:]
        bglu = k.cols[:, ROW_AT["s5_b_glu"]:]
        for t in range(TT):
            ins = nc.scalar.activation(k.sig[:, t], k.y_mla[:, t], ACT.Square, accum_out=k.ssq[:, t:t + 1])
        ins.then_inc(k.ssq_ready, 1)
        act.wait_ge(k.ssq_ready, 1)
        nc.scalar.activation(k.rstd[:, :], k.ssq[:, :], ACT.Sqrt, scale=1.0 / (HEADS * VD), bias=k.eps[:, 0:1]).then_inc(k.mla_rt, 1)
        for b in range(4):
            act.wait_ge(k.y_out, b + 1)
            nc.scalar.activation(k.yt[:, 8 * b:8 * b + 8].rearrange("p g c -> p (g c)"), ps[:, b], ACT.Copy).then_inc(k.y_evac, 1)
        act.wait_ge(k.gate_out, 1)
        nc.scalar.activation(k.gate[:, 0:512], ps[:, 4], ACT.Copy)
        nc.scalar.activation(k.gate[:, 512:], ps[:, 5], ACT.Copy).then_inc(k.gate_evac, 1)
        for m in range(SK):
            act.wait_ge(k.ym_out, m + 1)
            nc.scalar.activation(k.ymT[:, m], ps[:, (6, 7, 4, 5)[m]], ACT.Copy, scale=gn[:, m:m + 1]).then_inc(k.ym_evac, 1)
        for m in range(SK):
            act.wait_ge(k.d_done, m + 1)
            nc.scalar.activation(k.gT[:, m], k.yT[:, m].rearrange("p s c -> p (s c)"), ACT.Gelu_apprx_tanh).then_inc(k.gelu4_done, 1)
        for m in range(SK):
            act.wait_ge(k.z_out, m + 1)
            nc.scalar.activation(k.sig[:, m], ps[:, m], ACT.Sigmoid, bias=bglu[:, m:m + 1]).then_inc(k.sig_done, 1)
        for m in range(SK):
            act.wait_ge(k.y5_ready, m + 1)
            nc.scalar.activation(k.sq5[:, m], k.sig[:, m], ACT.Square).then_inc(k.sq5_ready, 1)
        act.wait_ge(k.r5_out, 1)
        nc.scalar.activation(k.r5[:, :], ps[:, 4], ACT.Sqrt, scale=1.0 / S5W, bias=k.eps[:, 0:1]).then_inc(k.r5_rt, 1)
        for t in range(TT):
            act.wait_ge(k.rt1, t + 1)
            nc.scalar.activation(k.rstd[:, t:t + 1], k.mv[:, t, 1:2], ACT.Sqrt, bias=k.eps[:, 0:1]).then_inc(k.ln_sq, 1)

    @k.block.vector
    def _(dve):
        step = k.dve_steps.on(dve)
        v = nc.vector
        tt = v.tensor_tensor
        dcol = k.cols[:, ROW_AT["s5_d"]:]
        gn = k.cols[:, ROW_AT["gn_s5"]:]
        dve.wait_ge(k.mla_rt, 1)
        step(v.reciprocal(k.rstd[:, :], k.rstd[:, :]))
        for t in range(TT):
            ins = v.tensor_scalar(k.y_mla[:, t], k.y_mla[:, t], k.rstd[:, t:t + 1], None, ALU.mult)
        ins.then_inc(k.ym_ready, 1)
        dve.wait_ge(k.s_yin, 16)
        for m in range(SK):
            v.scalar_tensor_tensor(k.yT[:, m], k.uT[:, m], dcol[:, m:m + 1], k.yT[:, m], ALU.mult, ALU.add).then_inc(k.d_done, 1)
        for m in range(SK):
            dve.wait_ge(k.sig_done, m + 1)
            tt(k.sig[:, m], k.gT[:, m], k.sig[:, m], ALU.mult).then_inc(k.y5_ready, 1)
        dve.wait_ge(k.r5_rt, 1)
        step(v.reciprocal(k.r5[:, :], k.r5[:, :]))
        for m in range(SK):
            ins = v.scalar_tensor_tensor(k.y5n[:, m].rearrange("p (c s) -> p s c", s=CH),
                                         k.sig[:, m].rearrange("p (s c) -> p s c", s=CH), gn[:, m:m + 1],
                                         k.r5[:, :].rearrange("p (s c) -> p s c", s=CH), ALU.mult, ALU.mult)
        ins.then_inc(k.y5n_ready, 1)
        dve.wait_ge(k.s_xre, 16)
        dve.wait_ge(k.gate_evac, 1)
        dve.wait_ge(k.s_ln1, 32)
        for t in range(TT):
            for half in range(2):
                n = 2 * t + half
                cols = slice(half * 512, (half + 1) * 512)
                dve.wait_ge(k.op_out, n + 1)
                step.tell(tt(k.x1[:, t, cols], ps[:, OB[n]], k.gate[:, cols], ALU.mult), k.op_evac, n + 1)
                step(v.scalar_tensor_tensor(k.x1[:, t, cols], k.x_re[:, t, cols], ALPHA, k.x1[:, t, cols], ALU.mult, ALU.add))
                step(v.bn_stats(k.stats[:, t, half], k.x1[:, t, cols]))
            step.tell(v.bn_aggr(k.mv[:, t], k.stats[:, t].rearrange("p a b -> p (a b)")), k.rt1, t + 1)
            dve.wait_ge(k.ln_sq, t + 1)
            step(v.reciprocal(k.rstd[:, t:t + 1], k.rstd[:, t:t + 1]))
            step(v.tensor_scalar(k.x1[:, t], k.x1[:, t], k.mv[:, t, 0:1], k.rstd[:, t:t + 1], ALU.subtract, ALU.mult))
            tt(k.x1[:, t], k.x1[:, t], k.ln_g[:, :], ALU.mult).then_inc(k.ln_gain, 1)
        for kt in range(DK):
            dve.wait_ge(k.x1t_out, kt + 1)
            v.tensor_scalar(k.h2T[:, kt], ps[:, OB[kt]], k.modc[:, 4 * DK + kt:4 * DK + kt + 1], k.modc[:, 3 * DK + kt:3 * DK + kt + 1],
                            ALU.mult, ALU.add)

    @k.block.tensor
    def _(pe):
        def project_out(n, tiles):
            t, half = n // 2, n % 2
            for kt in tiles:
                y = (k.ymT if kt < SK else k.y5n)[:, kt % SK, t * P:(t + 1) * P]
                w = k.w_out[:, (kt + SK) % DK, half * 512:(half + 1) * 512]
                ins = mm(ps[:, OB[n]], y, w, start=(kt == 0), stop=(kt == DK - 1))
            return ins

        for b in range(4):
            for q in range(4 * b, 4 * b + 4):
                out = ps[:, b, (q % 4) * P:(q % 4 + 1) * P]
                for part, z in enumerate((k.zr, k.zn)):
                    mm(out, z[:, q, 1:].rearrange("p s h -> p (s h)"), k.spad[:, part, q].rearrange("p a c -> p (a c)"),
                       start=(part == 0), stop=False)
                for g2 in range(2):
                    ins = mm(out[:, g2 * NC:(g2 + 1) * NC], k.m1[:, 2 * q + g2], k.ut[:, 2 * q + g2], start=False, stop=(g2 == 1))
            ins.then_inc(k.y_out, 1)
        pe.wait_ge(k.gcol_ready, 1)
        for i in range(DK):
            ins = mm(ps[:, 4 + i // 4, (i % 4) * P:(i % 4 + 1) * P], k.gcol[:, i], k.ident[:, :], start=True, stop=True)
        ins.then_inc(k.gate_out, 1)
        pe.wait_ge(k.ym_ready, 1)
        for m in range(SK):
            if m == 2:
                pe.wait_ge(k.gate_evac, 1)
            for t in range(TT):
                ins = nc.tensor.transpose(ps[:, (6, 7, 4, 5)[m], t * P:(t + 1) * P], k.y_mla[:, t, m * P:(m + 1) * P], k.ident[:, :])
            ins.then_inc(k.ym_out, 1)
        pe.wait_ge(k.ym_evac, 4)
        pe.wait_ge(k.s_wout, 16)
        for n in range(EARLY):
            project_out(n, range(SK))
        pe.wait_ge(k.gelu4_done, 4)
        pe.wait_ge(k.s_wglu, 16)
        pe.wait_ge(k.y_evac, 4)
        for m in range(SK):
            for kt in range(SK):
                ins = mm(ps[:, m], k.w_glu[:, kt, m * P:(m + 1) * P], k.gT[:, kt], start=(kt == 0), stop=(kt == SK - 1))
            ins.then_inc(k.z_out, 1)
        for m in range(SK):
            pe.wait_ge(k.sq5_ready, m + 1)
            ins = mm(ps[:, 4], k.ones[:, :], k.sq5[:, m], start=(m == 0), stop=(m == SK - 1))
        ins.then_inc(k.r5_out, 1)
        for n in range(EARLY, 2 * TT - 1):
            project_out(n, range(SK))
        pe.wait_ge(k.y5n_ready, 1)
        pe.wait_ge(k.s_wout, 32)
        for n in range(2 * TT):
            project_out(n, range(SK if n < 2 * TT - 1 else 0, DK)).then_inc(k.op_out, 1)
        pe.wait_ge(k.x1_ready, TT)
        for kt in range(DK):
            pe.wait_ge(k.op_evac, kt + 1)
            for t in range(TT):
                ins = nc.tensor.transpose(ps[:, OB[kt], t * P:(t + 1) * P], k.x1[:, t, kt * P:(kt + 1) * P], k.ident[:, :])
            ins.then_inc(k.x1t_out, 1)


BIG_NEG = -3.0e38
NBLK = PKEYS
BPT = 12
CHK = 64
GRP = 16
LEAD1 = TT * BPT
LEAD = LEAD1 + T // GRP


def place_peer(k):
    k.iota = k.sb("iota", [P, PKEYS], 3)
    k.iota16 = k.sb("iota16", [P, PTOP], 3.5)
    k.iotai = k.sb("iotai", [P, PKEYS], 4, I32)
    k.h2h = k.sb("h2h", [P, DK, T], 6, F32R)
    k.h2l = k.sb("h2l", [P, DK, T], 22, F32R)
    k.w_q = k.sb("w_q", [P, 4, DK, 2 * PHALF], 98)
    k.w_qh = k.sb("w_qh", [P, 2, DK, 2 * PHALF], 190, F32R)
    k.w_ql = k.sb("w_ql", [P, 2, DK, 2 * PHALF], 78, F32R)
    k.keys = k.sb("keys", [P, 2, PH, PHALF], 182)
    k.keysT = k.sb("keysT", [P, PH, 2, PKEYS], 174)
    k.qT = k.sb("qT", [P, 2 * PH, T], 142)
    k.s_all = k.sb("s_all", [P, TT, PH, 2, PKEYS], 110)
    k.u_raw = k.sb("u_raw", [P, 4, D], 38)
    k.uth = k.sb("uth", [P, 2, DK, P], 54, F32R)
    k.utl = k.sb("utl", [P, 2, DK, P], 62, F32R)
    k.acts = k.sb("acts", [P, 4, T], 70)
    k.cand = k.sb("cand", [P, 2, PTOP, PTOP], 78)
    k.cand2 = k.sb("cand2", [P, 2, PTOP * PTOP], 80)
    k.s2 = k.sb("s2", [P, 2, 2, PKEYS], 82)
    k.vals = k.sb("vals", [P, PH, 2, PTOP], 84)
    k.idx = k.sb("idx", [P, PH, 2, PTOP], 85, U32)
    k.idxf = k.sb("idxf", [P, PH, 2, PTOP], 86)
    k.tops = k.sb("tops", [P, PH, PTOP], 87)
    k.topc = k.sb("topc", [P, PH, PTOP], 87.5, U32)
    k.cab = k.sb("cab", [P, 2, PH * PTOP], 88, U32)
    k.cabf = k.sb("cabf", [P, 2, PH * PTOP], 89)
    k.gsum = k.sb("gsum", [P, PH], 90)
    k.best = k.sb("best", [P, PH], 90.125)
    k.route = k.sb("route", [P, TT, 3, PH * PTOP], 174)
    k.s_tt = k.sb("s_tt", [P, PH, 2, PKEYS], 182)
    k.eq = k.sb("eq", [P, PH * PTOP, PTOP], 190)
    k.routeT = k.sb("routeT", [P, 3, T], 198)
    k.hot2 = k.sb("hot2", [P, GRP, P], 94)
    k.hot1 = k.sb("hot1", [P, GRP, P], 102)
    k.stage = k.sb("stage", [P, 2, PKEYS, CHK], 110)
    k.yacc = k.sb("yacc", [P, TT, D], 78)
    k.g_in = k.sb("g_in", [P, 2, 2, T], 190)
    k.v_raw = k.sb("v_raw", [P, 2, 2, 512], 182)
    k.vh = k.sb("vh", [P, 2, 2, 2, 512], 94, F32R)
    k.vl = k.sb("vl", [P, 2, 2, 2, 512], 110, F32R)
    k.w_f = k.sb("w_f", [P, 2, T], 126)
    k.wh = k.sb("wh", [P, 2, 2, T], 130, F32R)
    k.wl = k.sb("wl", [P, 2, 2, T], 198, F32R)


def place_end(k):
    k.x1b = k.sb("x1b", [P, TT, D], 142)
    k.ln2_g = k.sb("ln2_g", [P, D], 162)
    k.ln2_b = k.sb("ln2_b", [P, D], 166)
    k.gate2 = k.sb("gate2", [P, D], 170)
    k.gcol2 = k.sb("gcol2", [P, DK, P], 174)
    k.stats2 = k.sb("stats2", [P, TT, 2, 6], 178)
    k.mv2 = k.sb("mv2", [P, TT, 2], 178.25)
    k.rstd2 = k.sb("rstd2", [P, TT], 178.5)


def query(nc, io, k, ps, bl):
    k.q_out, k.q_evac, k.h2h_done, k.h2l_done, k.iota_done = k.sems("q_out q_evac h2h_done h2l_done iota_done")
    k.wqh_done, k.wql_done = k.sems("wqh_done wql_done")
    wq = k.s_wq
    mm = nc.tensor.matmul
    KT0, Q0, S0 = 0, 4, 4 + 2 * PH
    S_END = S0 + 4 * TT

    @k.block.sync
    def _(sp):
        for h in range(2, PH):
            if h >= 4:
                sp.wait_ge(k.wql_done, h - 3)
            load_w_q(sp, io, k, h)
        for i in range(4):
            bl.load_u(sp, i, i)

    @k.block.gpsimd
    def _(pool):
        nc.gpsimd.iota(k.iotai[:, :], [[1, PKEYS]], base=0, channel_multiplier=0).then_inc(k.iota_done, 1)
        pool.wait_ge(k.iota_done, 1)
        nc.gpsimd.tensor_copy(k.iota[:, :], k.iotai[:, :])
        nc.gpsimd.tensor_copy(k.iota16[:, :], k.iotai[:, 0:PTOP])

    @k.block.tensor
    def _(pe):
        def bank(n):
            if n >= 8:
                pe.wait_ge(k.q_evac, n - 7)
            return ps[:, n % 8]

        bl.credits_pe(pe)
        pe.wait_ge(k.s_keys, 32)
        for n in range(Q0):
            for i in range(4):
                h, side = 2 * n + i // 2, i % 2
                ins = nc.tensor.transpose(ps[:, n, i * P:(i + 1) * P], k.keys[:, side, h], k.ident[:, :])
            ins.then_inc(k.q_out, 1)
        for j in range(2 * PH):
            h, side = j // 2, j % 2
            if side == 0:
                pe.wait_ge(k.wql_done, h + 1)
            out = bank(Q0 + j)
            for kt in range(DK):
                if j == 0:
                    pe.wait_ge(k.h2l_done, kt + 1)
                hi, lo = (w[:, h % 2, kt, side * PHALF:(side + 1) * PHALF] for w in (k.w_qh, k.w_ql))
                mm(out, hi, k.h2h[:, kt], start=(kt == 0), stop=False)
                mm(out, hi, k.h2l[:, kt], start=False, stop=False)
                ins = mm(out, lo, k.h2h[:, kt], start=False, stop=(kt == DK - 1))
            ins.then_inc(k.q_out, 1)
        for t in range(TT):
            for j in range(4):
                out = bank(S0 + 4 * t + j)
                if t == 0:
                    pe.wait_ge(k.q_evac, Q0 + 4 * (j + 1))
                for i in range(4):
                    h, side = 2 * j + i // 2, i % 2
                    ins = mm(out[:, i * PKEYS:(i + 1) * PKEYS], k.qT[:, 2 * h + side, t * P:(t + 1) * P], k.keysT[:, h, side],
                             start=True, stop=True)
                ins.then_inc(k.q_out, 1)

    @k.block.scalar
    def _(act):
        def split_high(h):
            act.wait_ge(wq[h % 4], 16 * (h // 4 + 1))
            if h >= 2:
                act.wait_ge(k.q_out, Q0 + 2 * h - 2)
            nc.scalar.activation(k.w_qh[:, h % 2].rearrange("p k n -> p (k n)"), k.w_q[:, h % 4].rearrange("p k n -> p (k n)"),
                                 ACT.Copy).then_inc(k.wqh_done, 1)

        split_high(0)
        for kt in range(DK):
            nc.scalar.activation(k.h2h[:, kt], k.h2T[:, kt], ACT.Copy).then_inc(k.h2h_done, 1)
        split_high(1)
        for n in range(S_END):
            if Q0 < n < S0 and (n - Q0) % 2 == 0 and (n - Q0) // 2 + 1 < PH:
                split_high((n - Q0) // 2 + 1)
            act.wait_ge(k.q_out, n + 1)
            if n == 0:
                act.wait_ge(k.s_x1out, 16 * TT)
            if n < Q0:
                dst = k.keysT[:, 2 * n:2 * n + 2].rearrange("p a b c -> p (a b c)")
            elif n < S0:
                dst = k.qT[:, n - Q0]
            else:
                t, j = (n - S0) // 4, (n - S0) % 4
                dst = k.s_all[:, t, 2 * j:2 * j + 2].rearrange("p a b c -> p (a b c)")
            nc.scalar.activation(dst, ps[:, n % 8], ACT.Copy).then_inc(k.q_evac, 1)

    @k.block.vector
    def _(dve):
        def split_low(h):
            f = "p k n -> p (k n)"
            dve.wait_ge(k.wqh_done, h + 1)
            nc.vector.tensor_tensor(k.w_ql[:, h % 2].rearrange(f), k.w_q[:, h % 4].rearrange(f),
                                    k.w_qh[:, h % 2].bitcast(F32).rearrange(f), ALU.subtract).then_inc(k.wql_done, 1)

        split_low(0)
        for kt in range(DK):
            dve.wait_ge(k.h2h_done, kt + 1)
            nc.vector.tensor_tensor(k.h2l[:, kt], k.h2T[:, kt], k.h2h[:, kt].bitcast(F32), ALU.subtract).then_inc(k.h2l_done, 1)
        for h in range(1, PH):
            split_low(h)


class Blocks:
    UT_OUT, UTL, ACT_OUT, GELU, ACT_STORED, W, WL, Y_MM, YACC, VL = 8, 2, 2, 2, 1, 4, 2, 13, 4, 2

    def __init__(self, nc, io, k, ps):
        self.nc, self.k, self.ps = nc, k, ps
        self.u = io["peer_u"][0].rearrange("(e p) d -> p e d", p=P)
        self.v = io["peer_v"][0].rearrange("(e p) d -> p e d", p=P)
        k.ut_out, k.uth_done, k.utl_done, k.act_out, k.gelu_done = k.sems("ut_out uth_done utl_done act_out gelu_done")
        k.w_done, k.wh_done, k.wl_done, k.vh_done, k.vl_done = k.sems("w_done wh_done wl_done vh_done vl_done")
        k.y_mm, k.yacc_done, k.yacc_zero = k.sems("y_mm yacc_done yacc_zero")
        self.u_in = [k.sem(f"s_u_in{i}") for i in range(4)]
        self.act_stored = [k.sem(f"s_act_stored{i}") for i in range(2)]
        self.ga_in = [k.sem(f"s_ga_in{i}") for i in range(2)]
        self.v_in = [k.sem(f"s_v_in{i}") for i in range(2)]

    def credits_sp(self, sp):
        for i in range(2):
            sp.sem_inc(self.act_stored[i], self.ACT_STORED)

    def credits_pe(self, pe):
        pe.sem_inc(self.k.ut_out, self.UT_OUT)
        pe.sem_inc(self.k.act_out, self.ACT_OUT)
        pe.sem_inc(self.k.y_mm, self.Y_MM)

    def credits_act(self, act):
        act.sem_inc(self.k.gelu_done, self.GELU)

    def credits_dve(self, dve):
        dve.sem_inc(self.k.utl_done, self.UTL)
        dve.sem_inc(self.k.w_done, self.W)
        dve.sem_inc(self.k.yacc_done, self.YACC)

    def credits_pool(self, pool):
        pool.sem_inc(self.k.wl_done, self.WL)
        pool.sem_inc(self.k.vl_done, self.VL)

    def load_u(self, sp, b, i):
        k = self.k
        sp.wait_ge(k.ut_out, self.UT_OUT + 2 * b - 6)
        sp.dma_start(k.u_raw[:, i % 4], self.u[:, bass.ds(b, 1), :].rearrange("p a d -> p (a d)")).then_inc(self.u_in[i % 4], 16)

    def transpose_u(self, pe, b, quarter_b, i):
        k = self.k
        pe.wait_ge(self.u_in[i % 4], 16 * quarter_b + 16)
        for hf in range(2):
            pe.wait_ge(k.utl_done, self.UTL + 2 * b - 1 + hf)
            for c in range(4):
                ins = self.nc.tensor.transpose(self.ps[:, hf, c * P:(c + 1) * P],
                                               k.u_raw[:, i % 4, (4 * hf + c) * P:(4 * hf + c + 1) * P], k.ident[:, :])
            ins.then_inc(k.ut_out, 1)

    def split_u_high(self, act, b, i):
        k = self.k
        act.wait_ge(k.act_out, self.ACT_OUT + b - 1)
        for hf in range(2):
            act.wait_ge(k.ut_out, self.UT_OUT + 2 * b + 1 + hf)
            self.nc.scalar.activation(k.uth[:, i % 2, 4 * hf:4 * hf + 4].rearrange("p c n -> p (c n)"), self.ps[:, hf],
                                      ACT.Copy).then_inc(k.uth_done, 1)

    def split_u_low(self, dve, b, i):
        k = self.k
        for hf in range(2):
            dve.wait_ge(k.uth_done, 2 * b + 1 + hf)
            hi = k.uth[:, i % 2, 4 * hf:4 * hf + 4].rearrange("p c n -> p (c n)")
            lo = k.utl[:, i % 2, 4 * hf:4 * hf + 4].rearrange("p c n -> p (c n)")
            self.nc.vector.tensor_tensor(lo, self.ps[:, hf], hi.bitcast(F32), ALU.subtract).then_inc(k.utl_done, 1)

    def activations(self, pe, b, i):
        k = self.k
        pe.wait_ge(k.utl_done, self.UTL + 2 * b + 2)
        pe.wait_ge(k.gelu_done, self.GELU + b - 1)
        out = self.ps[:, 2 + i % 2]
        for kt in range(DK):
            hi, lo = k.uth[:, i % 2, kt], k.utl[:, i % 2, kt]
            self.nc.tensor.matmul(out, hi, k.h2h[:, kt], start=(kt == 0), stop=False)
            self.nc.tensor.matmul(out, hi, k.h2l[:, kt], start=False, stop=False)
            ins = self.nc.tensor.matmul(out, lo, k.h2h[:, kt], start=False, stop=(kt == DK - 1))
        ins.then_inc(k.act_out, 1)

    def gelu(self, act, b, i):
        k = self.k
        act.wait_ge(k.act_out, self.ACT_OUT + b + 1)
        self.nc.scalar.activation(k.acts[:, i % 4], self.ps[:, 2 + i % 2], ACT.Gelu_apprx_tanh).then_inc(k.gelu_done, 1)

    def gelu_to_store(self, act, b, quarter_b, i):
        if i % 2 == 0:
            act.wait_ge(self.act_stored[i // 2 % 2], self.ACT_STORED + 16 * quarter_b)
        self.gelu(act, b, i)

    def store_acts(self, sp, p, i):
        k = self.k
        sp.wait_ge(k.gelu_done, self.GELU + 2 * p + 2)
        sp.dma_start(k.act_scr[bass.ds(2 * p, 2)].rearrange("e p t -> p e t"), k.acts[:, 2 * i:2 * i + 2]).then_inc(self.act_stored[i], 16)

    def gelu_to_weigh(self, act, b, i):
        n = b - LEAD
        act.wait_ge(self.k.w_done, self.W + n - 3)
        self.gelu(act, b, i)

    def load_g(self, sp, p, at, i):
        k = self.k
        sp.wait_ge(k.w_done, self.W + 2 * p - 2)
        sp.dma_start(k.g_in[:, i % 2], k.g_scr[bass.ds(at, 2)].rearrange("e p t -> p e t")).then_inc(self.ga_in[i % 2], 16)

    def load_acts(self, sp, at, i):
        k = self.k
        sp.dma_start(k.acts[:, 2 * i:2 * i + 2], k.act_scr[bass.ds(at, 2)].rearrange("e p t -> p e t")).then_inc(self.ga_in[i % 2], 16)

    def load_v(self, sp, p, at, half):
        k = self.k
        sp.wait_ge(k.vl_done, self.VL + 2 * p + half - 1)
        sp.dma_start(k.v_raw[:, half], self.v[:, bass.ds(at, 2), half * 512:(half + 1) * 512]).then_inc(self.v_in[half], 16)

    def weight(self, dve, n, loaded, i):
        k = self.k
        pr, e = i // 2, i % 2
        if e == 0:
            dve.wait_ge(self.ga_in[pr], loaded)
        dve.wait_ge(k.wl_done, self.WL + n - 1)
        self.nc.vector.tensor_tensor(k.w_f[:, e], k.acts[:, i], k.g_in[:, pr, e], ALU.mult).then_inc(k.w_done, 1)

    def split_w_high(self, act, n, p, i):
        k = self.k
        act.wait_ge(k.w_done, self.W + n + 1)
        act.wait_ge(k.y_mm, self.Y_MM + 8 * p - 8)
        self.nc.scalar.activation(k.wh[:, i // 2, i % 2], k.w_f[:, i % 2], ACT.Copy).then_inc(k.wh_done, 1)

    def split_w_low(self, pool, n, i):
        k = self.k
        pool.wait_ge(k.wh_done, n + 1)
        self.nc.gpsimd.tensor_tensor(k.wl[:, i // 2, i % 2], k.w_f[:, i % 2], k.wh[:, i // 2, i % 2].bitcast(F32),
                                     ALU.subtract).then_inc(k.wl_done, 1)

    def split_v_high(self, act, p, i, half):
        k = self.k
        act.wait_ge(self.v_in[half], 16 * p + 16)
        act.wait_ge(k.y_mm, self.Y_MM + 8 * p - 12 + 4 * half)
        self.nc.scalar.activation(k.vh[:, i % 2, half].rearrange("p e d -> p (e d)"), k.v_raw[:, half].rearrange("p e d -> p (e d)"),
                                  ACT.Copy).then_inc(k.vh_done, 1)

    def split_v_low(self, pool, p, i, half):
        k = self.k
        pool.wait_ge(k.vh_done, 2 * p + half + 1)
        f = "p e d -> p (e d)"
        self.nc.gpsimd.tensor_tensor(k.vl[:, i % 2, half].rearrange(f), k.v_raw[:, half].rearrange(f),
                                     k.vh[:, i % 2, half].bitcast(F32).rearrange(f), ALU.subtract).then_inc(k.vl_done, 1)

    def products(self, pe, p, pr, half):
        k, mm = self.k, self.nc.tensor.matmul
        pe.wait_ge(k.wl_done, self.WL + 2 * p + 2)
        pe.wait_ge(k.vl_done, self.VL + 2 * p + half + 1)
        for t in range(TT):
            pe.wait_ge(k.yacc_done, self.YACC + 8 * p + 4 * half - 3 + t)
            out = self.ps[:, 4 + t]
            for e in range(2):
                hi, lo = k.wh[:, pr, e, t * P:(t + 1) * P], k.wl[:, pr, e, t * P:(t + 1) * P]
                mm(out, hi, k.vh[:, pr, half, e], start=(e == 0), stop=False)
                mm(out, hi, k.vl[:, pr, half, e], start=False, stop=False)
                ins = mm(out, lo, k.vh[:, pr, half, e], start=False, stop=(e == 1))
            ins.then_inc(k.y_mm, 1)

    def add_products(self, dve, p, half, tiles=range(TT)):
        k = self.k
        for t in tiles:
            dve.wait_ge(k.y_mm, self.Y_MM + 8 * p + 4 * half + t + 1)
            y = k.yacc[:, t, half * 512:(half + 1) * 512]
            self.nc.vector.tensor_tensor(y, y, self.ps[:, 4 + t], ALU.add).then_inc(k.yacc_done, 1)


def experts(nc, io, k, ps, bl, out):
    k.s_ready, k.s_used, k.steps6, k.route_ready = k.sems("s_ready s_used steps6 route_ready")
    k.rt_out, k.rt_evac, k.exp6_in, k.exp6_done = k.sems("rt_out rt_evac exp6_in exp6_done")
    k.hot_ready, k.g_out, k.g_evac = k.sems("hot_ready g_out g_evac")
    s_g_hi = [k.sem(f"s_g_hi{i}") for i in range(2)]
    s_g_lo = [k.sem(f"s_g_lo{i}") for i in range(2)]
    mm = nc.tensor.matmul
    NCH = T // CHK
    RPC = CHK // GRP
    CREDIT = 4
    REST = (NBLK - LEAD) // 4
    FOURS = NBLK // 4
    k.s_x1b, k.s_ln2, k.s_out = k.sems("s_x1b s_ln2 s_out")

    @k.block.sync
    def _(sp):
        bl.credits_sp(sp)
        for i in range(2):
            sp.sem_inc(s_g_hi[i], 1)
            sp.sem_inc(s_g_lo[i], 1)

        def quad(Q):
            for i in range(2):
                bl.load_u(sp, 4 * Q + 4 + 2 * i, 2 * i)
                bl.load_u(sp, 4 * Q + 5 + 2 * i, 2 * i + 1)
                bl.store_acts(sp, 2 * Q + i, i)

        with sp.Fori(0, LEAD1 // 4) as Q:
            quad(Q)

        def store_g(ch, c, lo, hi, stored):
            sp.dma_start(k.g_scr.rearrange("e p t -> p e t")[:, lo:hi, bass.ds(ch * CHK, CHK)],
                         k.stage[:, c, lo:hi]).then_inc(stored[c], 16)

        def piece(ch, c, all_of_it=True):
            quad(LEAD1 // 4 + ch)
            sp.wait_ge(k.g_evac, CREDIT + 4 * RPC * (ch + 1))
            store_g(ch, c, LEAD, NBLK, s_g_hi)
            if all_of_it:
                store_g(ch, c, 0, LEAD, s_g_lo)

        with sp.Fori(0, NCH // 2 - 1) as ch2:
            for c in range(2):
                piece(2 * ch2 + c, c)
        piece(NCH - 2, 0)
        piece(NCH - 1, 1, False)

        def second(Q, at, i, stored):
            p = 2 * Q + i
            if stored:
                bl.load_g(sp, p, at + 2 * i, i)
                bl.load_acts(sp, at + 2 * i, i)
            for half in range(2):
                bl.load_v(sp, p, at + 2 * i, half)
            if not stored:
                bl.load_g(sp, p, at + 2 * i, i)

        def both(Q, first=False):
            for i in range(2):
                for j in range(2):
                    bl.load_u(sp, LEAD + 4 + 4 * Q + 2 * i + j, 2 * i + j)
                if first and i == 0:
                    for c in range(2):
                        sp.wait_ge(s_g_hi[c], 1 + 16 * (NCH // 2))
                    sp.wait_ge(s_g_lo[0], 1 + 16 * (NCH // 2))
                second(Q, LEAD + 4 * Q, i, False)

        both(0, True)
        store_g(NCH - 1, 1, 0, LEAD, s_g_lo)
        with sp.Fori(1, REST - 1) as Q:
            both(Q)
        for i in range(2):
            second(REST - 1, NBLK - 4, i, False)
        sp.wait_ge(s_g_lo[1], 1 + 16 * (NCH // 2))
        for name, dst in (("ln2_g", k.ln2_g), ("ln2_b", k.ln2_b)):
            a = io[name]
            sp.dma_start(dst[:, :], bass.AP(a.tensor, a.offset, [[0, P], [1, D]])).then_inc(k.s_ln2, 16)
        sp.wait_ge(k.s_x1out, 16 * TT)
        sp.dma_start(k.x1b[:, :, :], k.x1_scr.rearrange("(t p) d -> p t d", p=P)).then_inc(k.s_x1b, 16)
        for i in range(2):
            sp.wait_ge(bl.act_stored[i], bl.ACT_STORED + 16 * (LEAD // 4))
        with sp.Fori(REST, FOURS) as Q:
            for i in range(2):
                second(Q, 4 * Q - 4 * REST, i, True)

        for t in range(TT):
            sp.wait_ge(k.x1_ready, TT + t + 1)
            sp.dma_start(out[0, t * P:(t + 1) * P, :], k.yacc[:, t, :]).then_inc(k.s_out, 16)
        sp.wait_ge(k.s_out, 16 * TT)

    @k.block.gpsimd
    def _(pool):
        bl.credits_pool(pool)

        def quad(Q):
            for i in range(4):
                bl.split_w_low(pool, 4 * Q + i, i)
                bl.split_v_low(pool, 2 * Q + i // 2, i // 2, i % 2)

        with pool.Fori(0, REST) as Q:
            quad(Q)
        nc.gpsimd.tensor_copy(k.gcol2[:, :, :], k.modc[:, 5 * DK:6 * DK].unsqueeze(2).broadcast_to([P, DK, P])).then_inc(k.gcol_ready, 1)
        with pool.Fori(REST, FOURS) as Q:
            quad(Q)

        pool.wait_ge(k.s_ln2, 32)
        for t in range(TT):
            pool.wait_ge(k.ln_gain, TT + t + 1)
            nc.gpsimd.tensor_tensor(k.yacc[:, t], k.yacc[:, t], k.ln2_b[:, :], ALU.add).then_inc(k.x1_ready, 1)

    @k.block.scalar
    def _(act):
        bl.credits_act(act)
        act.sem_inc(k.g_evac, CREDIT)

        def scores(it, j):
            act.wait_ge(k.s_used, CREDIT + 4 * it + j - 3)
            nc.scalar.activation(k.s_tt[:, 2 * j:2 * j + 2].rearrange("p a b c -> p (a b c)"),
                                 k.s_all[:, bass.ds(it, 1), 2 * j:2 * j + 2].rearrange("p t a b c -> p (t a b c)"),
                                 ACT.Copy).then_inc(k.s_ready, 1)

        def tile(it, last):
            for i in range(BPT):
                b = it * BPT + i
                bl.split_u_high(act, b + 1, i + 1)
                if i == PH:
                    act.wait_ge(k.exp6_in, it + 1)
                    nc.scalar.activation(k.tops[:, :, :], k.tops[:, :, :], ACT.Exp).then_inc(k.exp6_done, 1)
                bl.gelu_to_store(act, b, it * (BPT // 4) + i // 4, i)
                if not last and i % 3 == 2:
                    scores(it + 1, i // 3)

        for j in range(4):
            scores(0, j)
        bl.split_u_high(act, 0, 0)
        with act.Fori(0, TT - 1) as it:
            tile(it, False)
        tile(TT - 1, True)
        for t in range(TT):
            act.wait_ge(k.rt_out, t + 1)
            nc.scalar.activation(k.routeT[:, :, t * P:(t + 1) * P], ps[:, 4 + t, 0:3 * P].rearrange("p (a t) -> p a t", a=3),
                                 ACT.Copy).then_inc(k.rt_evac, 1)
        with act.Fori(0, NCH // 2) as ch2:
            for c in range(2):
                act.wait_ge(s_g_hi[c], 1 + 16 * ch2)
                act.wait_ge(s_g_lo[c], 1 + 16 * ch2)
                for r in range(RPC):
                    rnd = (2 * ch2 + c) * RPC + r
                    for j in range(4):
                        at = r * GRP + 4 * j
                        act.wait_ge(k.g_out, CREDIT + 4 * rnd + j + 1)
                        nc.scalar.activation(k.stage[:, c, :, at:at + 4].rearrange("p e t -> p t e"),
                                             ps[:, 4 + j].rearrange("p (t e) -> p t e", t=4), ACT.Copy).then_inc(k.g_evac, 1)
                    b = LEAD1 + rnd
                    bl.split_u_high(act, b + 1, r + 1)
                    bl.gelu_to_store(act, b, LEAD1 // 4 + 2 * ch2 + c, r)

        def quad(Q, first, next_first=True):
            for i in range(4):
                b = LEAD + 4 * Q + i
                if first and (next_first or i < 3):
                    bl.split_u_high(act, b + 1, i + 1)
                if first:
                    bl.gelu_to_weigh(act, b, i)
                bl.split_w_high(act, 4 * Q + i, 2 * Q + i // 2, i)
                bl.split_v_high(act, 2 * Q + i // 2, i // 2, i % 2)

        for i in range(2):
            act.wait_ge(bl.act_stored[i], bl.ACT_STORED + 16 * (LEAD // 4))
        with act.Fori(0, REST - 1) as Q:
            quad(Q, True)
        quad(REST - 1, True, False)
        act.wait_ge(k.gate_out, 2)
        for half in range(2):
            ins = nc.scalar.activation(k.gate2[:, half * 512:(half + 1) * 512], ps[:, half], ACT.Copy)
        ins.then_inc(k.gate_evac, 1)
        with act.Fori(REST, FOURS) as Q:
            quad(Q, False)

        for t in range(TT):
            act.wait_ge(k.rt1, TT + t + 1)
            nc.scalar.activation(k.rstd2[:, t:t + 1], k.mv2[:, t, 1:2], ACT.Sqrt, bias=k.eps[:, 0:1]).then_inc(k.ln_sq, 1)

    @k.block.tensor
    def _(pe):
        pe.sem_inc(k.g_out, CREDIT)
        bl.transpose_u(pe, 0, 0, 0)
        with pe.Fori(0, TT) as it:
            for i in range(BPT):
                b = it * BPT + i
                bl.transpose_u(pe, b + 1, it * (BPT // 4) + (i + 1) // 4, i + 1)
                bl.activations(pe, b, i)
        for t in range(TT):
            pe.wait_ge(k.route_ready, 2 * t + 2)
            for a in range(3):
                ins = nc.tensor.transpose(ps[:, 4 + t, a * P:(a + 1) * P], k.route[:, t, a], k.ident[:, :])
            ins.then_inc(k.rt_out, 1)
        pe.wait_ge(k.rt_evac, TT)
        with pe.Fori(0, NCH // 2) as ch2:
            for c in range(2):
                for r in range(RPC):
                    rnd = (2 * ch2 + c) * RPC + r
                    b = LEAD1 + rnd
                    for j in range(GRP):
                        if j % 4 == 0:
                            pe.wait_ge(k.hot_ready, 4 * rnd + j // 4 + 1)
                            pe.wait_ge(k.g_evac, CREDIT + 4 * rnd + j // 4 - 3)
                        ins = mm(ps[:, 4 + j // 4, (j % 4) * P:(j % 4 + 1) * P], k.hot2[:, j], k.hot1[:, j], start=True, stop=True)
                        if j % 4 == 3:
                            ins.then_inc(k.g_out, 1)
                    bl.transpose_u(pe, b + 1, LEAD1 // 4 + 2 * ch2 + c + (r + 1) // 4, r + 1)
                    bl.activations(pe, b, r)

        def quad(Q, first, next_first=True, before=True):
            for i in range(4):
                b = LEAD + 4 * Q + i
                if first and (next_first or i < 3):
                    bl.transpose_u(pe, b + 1, LEAD // 4 + Q + (i + 1) // 4, i + 1)
                if first:
                    bl.activations(pe, b, i)
                if i >= 2 or before:
                    bl.products(pe, 2 * Q + i // 2 - 1, (i // 2 + 1) % 2, i % 2)

        quad(0, True, before=False)
        with pe.Fori(1, REST - 1) as Q:
            quad(Q, True)
        quad(REST - 1, True, False)
        pe.wait_ge(k.utl_done, bl.UTL + 2 * NBLK)
        pe.wait_ge(k.gcol_ready, 2)
        for i in range(DK):
            ins = mm(ps[:, i // 4, (i % 4) * P:(i % 4 + 1) * P], k.gcol2[:, i], k.ident[:, :], start=True, stop=True)
        ins.then_inc(k.gate_out, 1)
        with pe.Fori(REST, FOURS) as Q:
            quad(Q, False)
        for half in range(2):
            bl.products(pe, NBLK // 2 - 1, 1, half)

    @k.block.vector
    def _(dve):
        v = nc.vector
        tt = v.tensor_tensor
        bl.credits_dve(dve)
        dve.sem_inc(k.s_used, CREDIT)
        with dve.Fori(0, TT) as it:
            dve.sem_clear(k.steps6)
            dve.wait_ge(k.s_ready, 4 * it + 1)
            v.memset(k.gsum[:, :], 0.0)
            step = Steps(k.steps6).on(dve)
            for j in range(PH // 2):
                two = (0, 1)
                lists = [(h, side) for h in two for side in (0, 1)]
                s = {(h, d): k.s_tt[:, 2 * j + h, d] for h, d in lists}
                vals = {(h, d): k.vals[:, 2 * j + h, d] for h, d in lists}
                idx = {(h, d): k.idx[:, 2 * j + h, d] for h, d in lists}
                for x in lists:
                    ins = v.max(vals[x][:, 0:8], s[x])
                step(ins)
                for x in lists:
                    v.max_index(idx[x][:, 0:8], vals[x][:, 0:8], s[x])
                for h, d in lists:
                    ins = v.match_replace(k.s2[:, h, d], vals[h, d][:, 0:8], s[h, d], BIG_NEG)
                step(ins)
                for h, d in lists:
                    ins = v.max(vals[h, d][:, 8:16], k.s2[:, h, d])
                step(ins)
                for h, d in lists:
                    v.max_index(idx[h, d][:, 8:16], vals[h, d][:, 8:16], k.s2[:, h, d])
                bl.split_u_low(dve, it * BPT + 2 * j, 2 * j)
                sums = [tt(k.cand[:, h], vals[h, 0].unsqueeze(2).broadcast_to([P, PTOP, PTOP]),
                           vals[h, 1].unsqueeze(1).broadcast_to([P, PTOP, PTOP]), ALU.add) for h in two]
                sums[0].then_inc(k.s_used, 1)
                step(sums[1])
                cands = [k.cand[:, h].rearrange("p a b -> p (a b)") for h in two]
                tops = [k.tops[:, 2 * j + h] for h in two]
                topc = [k.topc[:, 2 * j + h] for h in two]
                if j < PH // 2 - 1:
                    dve.wait_ge(k.s_ready, 4 * it + j + 2)
                bl.split_u_low(dve, it * BPT + 2 * j + 1, 2 * j + 1)
                for h in two:
                    ins = v.max(tops[h][:, 0:8], cands[h])
                step(ins)
                for h in two:
                    v.max_index(topc[h][:, 0:8], tops[h][:, 0:8], cands[h])
                for h in two:
                    ins = v.match_replace(k.cand2[:, h], tops[h][:, 0:8], cands[h], BIG_NEG)
                step(ins)
                for h in two:
                    ins = v.max(tops[h][:, 8:16], k.cand2[:, h])
                step(ins)
                for h in two:
                    ins = v.max_index(topc[h][:, 8:16], tops[h][:, 8:16], k.cand2[:, h])
            tops = k.tops[:, :, :]
            step(ins)
            step(v.tensor_copy(k.best[:, :], k.tops[:, :, 0]))
            tt(tops, tops, k.best[:, :].unsqueeze(2).broadcast_to([P, PH, PTOP]), ALU.subtract).then_inc(k.exp6_in, 1)
            bl.split_u_low(dve, it * BPT + PH, PH)
            c = k.topc[:, :, :].rearrange("p h c -> p (h c)")
            v.tensor_scalar(k.cab[:, 0], c, 4, None, ALU.logical_shift_right)
            v.tensor_scalar(k.cab[:, 1], c, PTOP - 1, None, ALU.bitwise_and)
            step(v.tensor_copy(k.idxf[:, :, :, :], k.idx[:, :, :, :]))
            step(v.tensor_copy(k.cabf[:, :, :], k.cab[:, :, :]))
            for side in range(2):
                e3 = k.eq[:, :, :]
                e4 = e3.rearrange("p (h c) a -> p h c a", h=PH)
                step(tt(e3, k.cabf[:, side].unsqueeze(2).broadcast_to([P, PH * PTOP, PTOP]),
                        k.iota16[:, :].unsqueeze(1).broadcast_to([P, PH * PTOP, PTOP]), ALU.is_equal))
                bl.split_u_low(dve, it * BPT + PH + side + 1, PH + side + 1)
                step(tt(e4, e4, k.idxf[:, :, side, :].unsqueeze(2).broadcast_to([P, PH, PTOP, PTOP]), ALU.mult))
                ins = v.tensor_reduce(k.route[:, bass.ds(it, 1), side].rearrange("p a c -> p (a c)"), e3, AXX, ALU.add)
                if side == 0:
                    step(ins)
                else:
                    ins.then_inc(k.route_ready, 1)
            bl.split_u_low(dve, it * BPT + BPT - 1, BPT - 1)
            dve.wait_ge(k.exp6_done, it + 1)
            step(v.tensor_reduce(k.gsum[:, :], tops, AXX, ALU.add))
            step(v.reciprocal(k.gsum[:, :], k.gsum[:, :]))
            tt(k.route[:, bass.ds(it, 1), 2].rearrange("p a (h c) -> p (a h) c", h=PH), tops,
               k.gsum[:, :].unsqueeze(2).broadcast_to([P, PH, PTOP]), ALU.mult).then_inc(k.route_ready, 1)
            dve.wait_ge(k.route_ready, 2 * it + 2)
        dve.wait_ge(k.rt_evac, TT)
        with dve.Fori(0, NCH // 2) as ch2:
            for c in range(2):
                for r in range(RPC):
                    rnd = (2 * ch2 + c) * RPC + r
                    for j in range(GRP):
                        if j == GRP // 2:
                            bl.split_u_low(dve, LEAD1 + rnd, r)
                        if j % 4 == 0:
                            dve.wait_ge(k.g_out, CREDIT + 4 * rnd + j // 4 - 3)
                        e1, e2, w = (k.routeT[:, a, bass.ds(rnd * GRP + j, 1)] for a in range(3))
                        v.tensor_scalar(k.hot2[:, j], k.iota[:, :], e2, None, ALU.is_equal)
                        ins = v.tensor_scalar(k.hot1[:, j], k.iota[:, :], e1, w, ALU.is_equal, ALU.mult)
                        if j % 4 == 3:
                            ins.then_inc(k.hot_ready, 1)
        bl.split_u_low(dve, LEAD, 0)

        nc.vector.memset(k.yacc[:, :, :], 0.0).then_inc(k.yacc_zero, 1)
        dve.wait_ge(k.yacc_zero, 1)

        def quad(Q, first, next_first=True, before=True):
            for i in range(4):
                n = 4 * Q + i
                if first:
                    if next_first or i < 3:
                        bl.split_u_low(dve, LEAD + n + 1, i + 1)
                    dve.wait_ge(k.gelu_done, bl.GELU + LEAD + n + 1)
                    bl.weight(dve, n, 16 * Q + 16, i)
                else:
                    bl.weight(dve, n, 16 * REST + 32 * (Q - REST) + 32, i)
                if i >= 2 or before:
                    bl.add_products(dve, 2 * Q + i // 2 - 1, i % 2)

        quad(0, True, before=False)
        with dve.Fori(1, REST - 1) as Q:
            quad(Q, True)
        quad(REST - 1, True, False)
        with dve.Fori(REST, FOURS) as Q:
            quad(Q, False)
        bl.add_products(dve, NBLK // 2 - 1, 0)

        step = k.dve_steps.on(dve)
        dve.wait_ge(k.gate_evac, 2)
        dve.wait_ge(k.s_x1b, 16)
        dve.wait_ge(k.s_ln2, 32)

        def stats(t):
            y = k.yacc[:, t]
            step(tt(y, y, k.gate2[:, :], ALU.mult))
            step(v.scalar_tensor_tensor(y, k.x1b[:, t], ALPHA, y, ALU.mult, ALU.add))
            for half in range(2):
                ins = v.bn_stats(k.stats2[:, t, half], k.yacc[:, t, half * 512:(half + 1) * 512])
            step(ins)
            step.tell(v.bn_aggr(k.mv2[:, t], k.stats2[:, t].rearrange("p a b -> p (a b)")), k.rt1, TT + t + 1)

        def normalise(t):
            y = k.yacc[:, t]
            dve.wait_ge(k.ln_sq, TT + t + 1)
            step(v.reciprocal(k.rstd2[:, t:t + 1], k.rstd2[:, t:t + 1]))
            step(v.tensor_scalar(y, y, k.mv2[:, t, 0:1], k.rstd2[:, t:t + 1], ALU.subtract, ALU.mult))
            tt(y, y, k.ln2_g[:, :], ALU.mult).then_inc(k.ln_gain, 1)

        for t in range(TT):
            bl.add_products(dve, NBLK // 2 - 1, 1, [t])
            dve.wait_ge(k.yacc_done, bl.YACC + 8 * (NBLK // 2 - 1) + 4 + t + 1)
            stats(t)
            if t:
                normalise(t - 1)
        normalise(TT - 1)


def build(nc, io, out):
    k = Plan(nc)
    for f in (place, place_attention, place_mix, place_peer, place_end):
        f(k)
    ps = nc.alloc_psum_tensor("ps", [P, 8, 512], F32)
    bl = Blocks(nc, io, k, ps)
    parts = [lambda: condition(nc, io, k, ps), lambda: project(nc, io, k, ps), lambda: attend(nc, io, k, ps),
             lambda: mix(nc, io, k, ps), lambda: query(nc, io, k, ps, bl), lambda: experts(nc, io, k, ps, bl, out)]
    for part in parts:
        with nc.Block() as block:
            k.block = block
            part()



_INS = ["x", "c", "positions", "w_ada", "b_ada", "w_in",
        "s5_lambda_re", "s5_lambda_im", "s5_log_dt", "s5_b_re", "s5_b_im", "s5_c_re", "s5_c_im",
        "s5_d", "s5_w_glu", "s5_b_glu", "mla_q_norm", "mla_w_uq", "mla_kv_norm", "mla_w_ukv",
        "gn_s5", "gn_mla", "w_out", "ln1_g", "ln1_b",
        "peer_w_query", "peer_keys1", "peer_keys2", "peer_u", "peer_v", "ln2_g", "ln2_b"]


def rope_rows():
    inv = np.float32(10000.0) ** (-np.arange(0, ROPE, 2, dtype=np.float32) / np.float32(ROPE))
    sign = np.repeat(np.array([-1.0, 1.0], np.float32), ROPE // 2)
    return np.stack([np.tile(inv, 8), np.tile(sign, 4)], 1).astype(np.float32)


def kernel(**inputs):
    import concourse.bacc as bacc
    from concourse.bass_utils import run_bass_kernel_spmd as run

    nc = bacc.Bacc("TRN2", target_bir_lowering=False, num_devices=1)
    arrays, io = {}, {}
    for name in _INS + ["rope_rows"]:
        a = rope_rows() if name == "rope_rows" else np.ascontiguousarray(inputs[name])
        arrays["in_" + name] = a
        io[name] = nc.dram_tensor("in_" + name, a.shape, mybir.dt.from_np(a.dtype), kind="ExternalInput").ap()
    out = nc.dram_tensor("out", (1, T, D), F32, kind="ExternalOutput").ap()
    build(nc, io, out)
    return run(nc, [arrays], core_ids=[0]).results[0]["out"]
```
